# Optimizing a Trainium2 kernel written in Bass

```python
import jax
import jax.numpy as jnp
from jax import lax
import numpy as np
import math

D_MODEL = 1024
BATCH = 1
SEQ = 256
DEPTH = 2

GRID_W = 64
CTX_LEN = 256
NORM_EPS = 1e-6
ROPE_BASE = 10000.0
NEG_INF = -1e30

A_HEADS = 8
A_KV_HEADS = 2
A_HEAD_DIM = 64
WINDOW = 128
A_BLOCK = 128
B_WIDTH = 512
B_GROUPS = 4
B_CHUNK = 128
C_HEADS = 8
C_Q_LORA = 384
C_KV_LORA = 256
C_NOPE = 64
C_ROPE = 32
C_V = 64
C_BLOCK = 128
D_WIDTH = 512
D_CONV = 3
N_EXPERTS = 16
EXPERT_FF = 1024
EC_FACTOR = 2

A_Q_W = A_HEADS * A_HEAD_DIM
A_KV_W = A_KV_HEADS * A_HEAD_DIM
EVEN_CTX_COLS = 2 * A_KV_W
EVEN_IN = EVEN_CTX_COLS + A_Q_W + 2 * B_WIDTH
EVEN_OUT = A_Q_W + B_WIDTH
ODD_CTX_COLS = C_KV_LORA + C_ROPE
ODD_IN = ODD_CTX_COLS + C_Q_LORA + 3 * D_WIDTH
ODD_OUT = C_HEADS * C_V + D_WIDTH
N_EVEN = (DEPTH + 1) // 2
N_ODD = DEPTH // 2


def rms_norm(x, g):
    xf = x.astype(jnp.float32)
    y = xf * lax.rsqrt(jnp.mean(xf * xf, axis=-1, keepdims=True) + NORM_EPS)
    return (y * g.astype(jnp.float32)).astype(x.dtype)

def layer_norm(x, g):
    xf = x.astype(jnp.float32)
    mu = jnp.mean(xf, axis=-1, keepdims=True)
    var = jnp.mean(jnp.square(xf - mu), axis=-1, keepdims=True)
    return ((xf - mu) * lax.rsqrt(var + NORM_EPS) * g.astype(jnp.float32)).astype(x.dtype)

def axial_rope_tables(rows, rot_dim):
    row = jnp.repeat(jnp.arange(rows, dtype=jnp.float32), GRID_W)
    col = jnp.tile(jnp.arange(GRID_W, dtype=jnp.float32), rows)
    n_freq = rot_dim // 4
    inv_freq = ROPE_BASE ** (-jnp.arange(n_freq, dtype=jnp.float32) / n_freq)
    ang = jnp.concatenate([row[:, None] * inv_freq[None, :], col[:, None] * inv_freq[None, :]], axis=-1)
    return jnp.cos(ang), jnp.sin(ang)

def apply_rope(x, cos, sin):
    x1, x2 = jnp.split(x, 2, axis=-1)
    cs = cos[None, :, None, :].astype(x.dtype)
    sn = sin[None, :, None, :].astype(x.dtype)
    return jnp.concatenate([x1 * cs - x2 * sn, x2 * cs + x1 * sn], axis=-1)

def gqa_attend(q, k, v, mask, sink, scale):
    s = jnp.einsum('bqhgd,bkhd->bhgqk', q, k).astype(jnp.float32) * scale
    if mask is not None:
        s = jnp.where(mask, s, NEG_INF)
    if sink is not None:
        sk = jnp.broadcast_to(sink.astype(jnp.float32)[None, :, :, None, None], s.shape[:-1] + (1,))
        s = jnp.concatenate([s, sk], axis=-1)
    p = jax.nn.softmax(s, axis=-1)
    if sink is not None:
        p = p[..., :-1]
    return jnp.einsum('bhgqk,bkhd->bqhgd', p.astype(v.dtype), v)

def window_attention(q, k, v, k_ctx, v_ctx, sink_g, scale):
    bsz, n = q.shape[0], q.shape[1]
    g = A_HEADS // A_KV_HEADS
    nb = n // A_BLOCK
    span = A_BLOCK + 2 * WINDOW
    pad = ((0, 0), (WINDOW, WINDOW), (0, 0), (0, 0))
    kp = jnp.pad(k, pad)
    vp = jnp.pad(v, pad)
    qi = jnp.arange(A_BLOCK)
    kj = jnp.arange(span)
    band = jnp.abs(kj[None, :] - WINDOW - qi[:, None]) <= WINDOW
    ctx_ok = jnp.ones((A_BLOCK, k_ctx.shape[1]), dtype=jnp.bool_)

    def block(nidx):
        start = nidx * A_BLOCK
        qb = lax.dynamic_slice_in_dim(q, start, A_BLOCK, axis=1).reshape(bsz, A_BLOCK, A_KV_HEADS, g, A_HEAD_DIM)
        kb = lax.dynamic_slice_in_dim(kp, start, span, axis=1)
        vb = lax.dynamic_slice_in_dim(vp, start, span, axis=1)
        kpos = start - WINDOW + kj
        mask = band & ((kpos >= 0) & (kpos < n))[None, :]
        mask = jnp.concatenate([mask, ctx_ok], axis=1)
        o = gqa_attend(qb, jnp.concatenate([kb, k_ctx], axis=1), jnp.concatenate([vb, v_ctx], axis=1), mask, sink_g, scale)
        return o.reshape(bsz, A_BLOCK, A_Q_W)

    out = lax.map(block, jnp.arange(nb))
    return jnp.moveaxis(out, 0, 1).reshape(bsz, n, A_Q_W)

def dense_block_attention(q, k_all, v_all, scale):
    bsz, n, h, _ = q.shape
    dv = v_all.shape[-1]
    nb = n // C_BLOCK

    def block(nidx):
        qb = lax.dynamic_slice_in_dim(q, nidx * C_BLOCK, C_BLOCK, axis=1)
        return gqa_attend(qb[:, :, :, None], k_all, v_all, None, None, scale)[:, :, :, 0]

    out = lax.map(block, jnp.arange(nb))
    return jnp.moveaxis(out, 0, 1).reshape(bsz, n, h * dv)

def spatial_gating(z, norm_g, w_s, b_s):
    bsz, n, _ = z.shape
    u, v = jnp.split(jax.nn.gelu(z), 2, axis=-1)
    v = layer_norm(v, norm_g)
    vc = v.reshape(bsz, n // B_CHUNK, B_CHUNK, B_GROUPS, B_WIDTH // B_GROUPS)
    mixed = jnp.einsum('gpq,bcqgd->bcpgd', w_s, vc) + b_s.T[None, None, :, :, None]
    return u * mixed.reshape(bsz, n, B_WIDTH)

def gated_short_conv(z, conv_w):
    gb, gc, hh = jnp.split(z, 3, axis=-1)
    u = gc * hh
    n = u.shape[1]
    half = D_CONV // 2
    up = jnp.pad(u, ((0, 0), (half, half), (0, 0)))
    conv = sum(up[:, j:j + n] * conv_w[j] for j in range(D_CONV))
    return gb * conv

def mla_q(cq, q_norm_g, w_uq, cos, sin):
    bsz, n, _ = cq.shape
    q = (rms_norm(cq, q_norm_g) @ w_uq).reshape(bsz, n, C_HEADS, C_NOPE + C_ROPE)
    q_nope, q_rope = q[..., :C_NOPE], q[..., C_NOPE:]
    if cos is not None:
        q_rope = apply_rope(q_rope, cos, sin)
    return jnp.concatenate([q_nope, q_rope], axis=-1)

def mla_kv(ckv, kr, kv_norm_g, w_ukv, cos, sin):
    bsz, n, _ = ckv.shape
    kv = (rms_norm(ckv, kv_norm_g) @ w_ukv).reshape(bsz, n, C_HEADS, C_NOPE + C_V)
    k_nope, v = kv[..., :C_NOPE], kv[..., C_NOPE:]
    kr = kr[:, :, None, :]
    if cos is not None:
        kr = apply_rope(kr, cos, sin)
    k = jnp.concatenate([k_nope, jnp.broadcast_to(kr, (bsz, n, C_HEADS, C_ROPE))], axis=-1)
    return k, v

def even_mixer(h_lat, h_ctx, w_in, sink, sgu_norm_g, sgu_w, sgu_b, w_out, cos, sin, need_ctx):
    bsz, n_lat, _ = h_lat.shape
    n_ctx = h_ctx.shape[1]
    g = A_HEADS // A_KV_HEADS
    scale = A_HEAD_DIM ** -0.5
    sink_g = sink.reshape(A_KV_HEADS, g)
    z_lat = h_lat @ w_in
    z_ctx = h_ctx @ (w_in if need_ctx else w_in[:, :EVEN_CTX_COLS])
    k_ctx = z_ctx[..., :A_KV_W].reshape(bsz, n_ctx, A_KV_HEADS, A_HEAD_DIM)
    v_ctx = z_ctx[..., A_KV_W:EVEN_CTX_COLS].reshape(bsz, n_ctx, A_KV_HEADS, A_HEAD_DIM)
    k_lat = apply_rope(z_lat[..., :A_KV_W].reshape(bsz, n_lat, A_KV_HEADS, A_HEAD_DIM), cos, sin)
    v_lat = z_lat[..., A_KV_W:EVEN_CTX_COLS].reshape(bsz, n_lat, A_KV_HEADS, A_HEAD_DIM)
    q_lat = apply_rope(z_lat[..., EVEN_CTX_COLS:EVEN_CTX_COLS + A_Q_W].reshape(bsz, n_lat, A_HEADS, A_HEAD_DIM), cos, sin)
    o_lat = window_attention(q_lat, k_lat, v_lat, k_ctx, v_ctx, sink_g, scale)
    s_lat = spatial_gating(z_lat[..., EVEN_CTX_COLS + A_Q_W:], sgu_norm_g, sgu_w, sgu_b)
    y_lat = jnp.concatenate([o_lat, s_lat], axis=-1) @ w_out
    if not need_ctx:
        return y_lat, None
    q_ctx = z_ctx[..., EVEN_CTX_COLS:EVEN_CTX_COLS + A_Q_W].reshape(bsz, n_ctx, A_KV_HEADS, g, A_HEAD_DIM)
    o_ctx = gqa_attend(q_ctx, k_ctx, v_ctx, None, sink_g, scale).reshape(bsz, n_ctx, A_Q_W)
    s_ctx = spatial_gating(z_ctx[..., EVEN_CTX_COLS + A_Q_W:], sgu_norm_g, sgu_w, sgu_b)
    y_ctx = jnp.concatenate([o_ctx, s_ctx], axis=-1) @ w_out
    return y_lat, y_ctx

def odd_mixer(h_lat, h_ctx, w_in, q_norm_g, w_uq, kv_norm_g, w_ukv, conv_w, w_out, cos, sin, need_ctx):
    bsz, n_ctx = h_ctx.shape[0], h_ctx.shape[1]
    scale = (C_NOPE + C_ROPE) ** -0.5
    z_lat = h_lat @ w_in
    z_ctx = h_ctx @ (w_in if need_ctx else w_in[:, :ODD_CTX_COLS])
    k_ctx, v_ctx = mla_kv(z_ctx[..., :C_KV_LORA], z_ctx[..., C_KV_LORA:ODD_CTX_COLS], kv_norm_g, w_ukv, None, None)
    k_lat, v_lat = mla_kv(z_lat[..., :C_KV_LORA], z_lat[..., C_KV_LORA:ODD_CTX_COLS], kv_norm_g, w_ukv, cos, sin)
    q_lat = mla_q(z_lat[..., ODD_CTX_COLS:ODD_CTX_COLS + C_Q_LORA], q_norm_g, w_uq, cos, sin)
    k_all = jnp.concatenate([k_lat, k_ctx], axis=1)
    v_all = jnp.concatenate([v_lat, v_ctx], axis=1)
    o_lat = dense_block_attention(q_lat, k_all, v_all, scale)
    c_lat = gated_short_conv(z_lat[..., ODD_CTX_COLS + C_Q_LORA:], conv_w)
    y_lat = jnp.concatenate([o_lat, c_lat], axis=-1) @ w_out
    if not need_ctx:
        return y_lat, None
    q_ctx = mla_q(z_ctx[..., ODD_CTX_COLS:ODD_CTX_COLS + C_Q_LORA], q_norm_g, w_uq, None, None)
    o_ctx = gqa_attend(q_ctx[:, :, :, None], k_ctx, v_ctx, None, None, scale)[:, :, :, 0].reshape(bsz, n_ctx, C_HEADS * C_V)
    c_ctx_out = gated_short_conv(z_ctx[..., ODD_CTX_COLS + C_Q_LORA:], conv_w)
    y_ctx = jnp.concatenate([o_ctx, c_ctx_out], axis=-1) @ w_out
    return y_lat, y_ctx

def expert_choice_ffn(h, w_router, w1, w3, w2):
    n_tok, d = h.shape[1], h.shape[2]
    cap = EC_FACTOR * n_tok // N_EXPERTS
    aff = jax.nn.softmax(jnp.einsum('bnd,de->bne', h, w_router).astype(jnp.float32), axis=-1)
    gate, idx = lax.top_k(jnp.swapaxes(aff, 1, 2), cap)
    xs = jax.vmap(lambda hb, ib: hb[ib])(h, idx)
    a = jnp.einsum('becd,edf->becf', xs, w1)
    b = jnp.einsum('becd,edf->becf', xs, w3)
    y = jnp.einsum('becf,efd->becd', jax.nn.silu(a) * b, w2) * gate[..., None].astype(h.dtype)

    def combine(yb, ib):
        return jnp.zeros((n_tok, d), h.dtype).at[ib.reshape(-1)].add(yb.reshape(-1, d))

    return jax.vmap(combine)(y, idx)

def first_inputs(seed: int = 0) -> dict:
    key = jax.random.key(seed)
    ks = iter(jax.random.split(key, 32))
    D = D_MODEL

    def nrm(shape, scale):
        return jax.random.normal(next(ks), shape, jnp.float32) * scale

    return {
        'x': nrm((BATCH, SEQ, D), 1.0),
        'c': nrm((BATCH, D), 1.0),
        'ctx': nrm((BATCH, CTX_LEN, D), 1.0),
        'c_ctx': nrm((D,), 1.0),
        'mod_w': nrm((DEPTH, D, 6 * D), 0.5 * D ** -0.5),
        'mod_b': nrm((DEPTH, 6 * D), 0.01),
        'norm1_g': 1.0 + nrm((DEPTH, D), 0.05),
        'norm2_g': 1.0 + nrm((DEPTH, D), 0.05),
        'ev_w_in': nrm((N_EVEN, D, EVEN_IN), D ** -0.5),
        'ev_sink': nrm((N_EVEN, A_HEADS), 0.5),
        'ev_sgu_norm_g': 1.0 + nrm((N_EVEN, B_WIDTH), 0.05),
        'ev_sgu_w': nrm((N_EVEN, B_GROUPS, B_CHUNK, B_CHUNK), B_CHUNK ** -0.5),
        'ev_sgu_b': nrm((N_EVEN, B_GROUPS, B_CHUNK), 0.1),
        'ev_w_out': nrm((N_EVEN, EVEN_OUT, D), EVEN_OUT ** -0.5),
        'od_w_in': nrm((N_ODD, D, ODD_IN), D ** -0.5),
        'od_q_norm_g': 1.0 + nrm((N_ODD, C_Q_LORA), 0.05),
        'od_w_uq': nrm((N_ODD, C_Q_LORA, C_HEADS * (C_NOPE + C_ROPE)), C_Q_LORA ** -0.5),
        'od_kv_norm_g': 1.0 + nrm((N_ODD, C_KV_LORA), 0.05),
        'od_w_ukv': nrm((N_ODD, C_KV_LORA, C_HEADS * (C_NOPE + C_V)), C_KV_LORA ** -0.5),
        'od_conv_w': nrm((N_ODD, D_CONV, D_WIDTH), D_CONV ** -0.5),
        'od_w_out': nrm((N_ODD, ODD_OUT, D), ODD_OUT ** -0.5),
        'router_w': nrm((DEPTH, D, N_EXPERTS), D ** -0.5),
        'exp_w1': nrm((DEPTH, N_EXPERTS, D, EXPERT_FF), D ** -0.5),
        'exp_w3': nrm((DEPTH, N_EXPERTS, D, EXPERT_FF), D ** -0.5),
        'exp_w2': nrm((DEPTH, N_EXPERTS, EXPERT_FF, D), EXPERT_FF ** -0.5),
        'final_g': 1.0 + nrm((D,), 0.05),
    }

def first_block(x, c, ctx, c_ctx, mod_w, mod_b, norm1_g, norm2_g, ev_w_in, ev_sink, ev_sgu_norm_g, ev_sgu_w, ev_sgu_b, ev_w_out, od_w_in, od_q_norm_g, od_w_uq, od_kv_norm_g, od_w_ukv, od_conv_w, od_w_out, router_w, exp_w1, exp_w3, exp_w2, final_g):
    rows = x.shape[1] // GRID_W
    cos_a, sin_a = axial_rope_tables(rows, A_HEAD_DIM)
    cos_c, sin_c = axial_rope_tables(rows, C_ROPE)
    silu_c = jax.nn.silu(c)
    silu_cc = jax.nn.silu(c_ctx)[None, :]
    x_lat, x_ctx = x, ctx
    for layer in range(DEPTH):
        need_ctx = layer < DEPTH - 1
        m_lat = jnp.split((silu_c @ mod_w[layer] + mod_b[layer])[:, None, :], 6, axis=-1)
        m_ctx = jnp.split((silu_cc @ mod_w[layer] + mod_b[layer])[:, None, :], 6, axis=-1)
        h_lat = rms_norm(x_lat, norm1_g[layer]) * (1 + m_lat[1]) + m_lat[0]
        h_ctx = rms_norm(x_ctx, norm1_g[layer]) * (1 + m_ctx[1]) + m_ctx[0]
        i = layer // 2
        if layer % 2 == 0:
            y_lat, y_ctx = even_mixer(h_lat, h_ctx, ev_w_in[i], ev_sink[i], ev_sgu_norm_g[i], ev_sgu_w[i], ev_sgu_b[i], ev_w_out[i], cos_a, sin_a, need_ctx)
        else:
            y_lat, y_ctx = odd_mixer(h_lat, h_ctx, od_w_in[i], od_q_norm_g[i], od_w_uq[i], od_kv_norm_g[i], od_w_ukv[i], od_conv_w[i], od_w_out[i], cos_c, sin_c, need_ctx)
        x_lat = x_lat + m_lat[2] * y_lat
        h_lat = rms_norm(x_lat, norm2_g[layer]) * (1 + m_lat[4]) + m_lat[3]
        x_lat = x_lat + m_lat[5] * expert_choice_ffn(h_lat, router_w[layer], exp_w1[layer], exp_w3[layer], exp_w2[layer])
        if need_ctx:
            x_ctx = x_ctx + m_ctx[2] * y_ctx
            h_ctx = rms_norm(x_ctx, norm2_g[layer]) * (1 + m_ctx[4]) + m_ctx[3]
            x_ctx = x_ctx + m_ctx[5] * expert_choice_ffn(h_ctx, router_w[layer], exp_w1[layer], exp_w3[layer], exp_w2[layer])
    return rms_norm(x_lat, final_g)


HEAD_DIM = 64
DIL_GROUPS = ((128, 1), (512, 4), (2048, 16))
HEADS_PER_DIL_GROUP = 4
N_HEADS_A = HEADS_PER_DIL_GROUP * len(DIL_GROUPS)
N_HEADS_B = 6
N_HEADS_C = 6
N_HEADS = N_HEADS_A + N_HEADS_B + N_HEADS_C
MIX_WIDTH = N_HEADS * HEAD_DIM
WIDTH_A = HEADS_PER_DIL_GROUP * HEAD_DIM
WIDTH_B = N_HEADS_B * HEAD_DIM
WIDTH_C = N_HEADS_C * HEAD_DIM
ROPE_DIM = HEAD_DIM // 4
ROPE_THETA = 500000.0
MOBA_BLOCK = 256
MOBA_TOPK = 3
MOBA_QCHUNK = 32
SB_QBLOCK = 128
D_FF = 4 * D_MODEL
N_BRANCHES = 3
IN_COLS = 3 * MIX_WIDTH + N_BRANCHES * D_MODEL


def rmsnorm(x, g):
    xf = x.astype(jnp.float32)
    y = xf * lax.rsqrt(jnp.mean(xf * xf, axis=-1, keepdims=True) + NORM_EPS)
    return (y * g.astype(jnp.float32)).astype(x.dtype)

def partial_rope(t, pos):
    inv_freq = jnp.exp(-math.log(ROPE_THETA) * jnp.arange(0, ROPE_DIM, 2, dtype=jnp.float32) / ROPE_DIM)
    ang = pos[:, None] * inv_freq[None, :]
    cos, sin = jnp.cos(ang), jnp.sin(ang)
    half = ROPE_DIM // 2
    x1, x2, rest = t[..., :half], t[..., half:ROPE_DIM], t[..., ROPE_DIM:]
    return jnp.concatenate([x1 * cos - x2 * sin, x2 * cos + x1 * sin, rest], axis=-1)

def dilated_window_attention(q, k, v, window, dilation):
    B, H, S, Dh = q.shape
    span = window // dilation
    blk = span
    unit = dilation * blk
    L = -(-S // unit) * unit
    nb = L // unit
    pad = ((0, 0), (0, 0), (0, L - S), (0, 0))

    def split(t):
        t = jnp.pad(t, pad).reshape(B, H, L // dilation, dilation, Dh)
        return jnp.swapaxes(t, 2, 3).reshape(B, H, dilation, nb, blk, Dh)

    def with_prev(t):
        prev = jnp.concatenate([jnp.zeros_like(t[:, :, :, :1]), t[:, :, :, :-1]], axis=3)
        return jnp.concatenate([prev, t], axis=4)

    qb = split(q)
    kc, vc = with_prev(split(k)), with_prev(split(v))
    s = jnp.einsum('bhrnqd,bhrnkd->bhrnqk', qb, kc) * (Dh ** -0.5)
    qi = jnp.arange(blk)[:, None]
    kj = jnp.arange(2 * blk)[None, :]
    dist = qi + blk - kj
    band = (dist >= 0) & (dist <= span)
    first = (jnp.arange(nb) == 0)[:, None, None]
    mask = band[None] & ~(first & (kj < blk)[None])
    s = jnp.where(mask, s, -jnp.inf)
    m = jnp.max(s, axis=-1, keepdims=True)
    p = jnp.exp(s - m)
    l = jnp.sum(p, axis=-1, keepdims=True)
    o = jnp.einsum('bhrnqk,bhrnkd->bhrnqd', p, vc) / l
    lse = (m + jnp.log(l))[..., 0]

    def merge(t):
        tail = t.shape[5:]
        t = t.reshape((B, H, dilation, L // dilation) + tail)
        return jnp.swapaxes(t, 2, 3).reshape((B, H, L) + tail)[:, :, :S]

    return merge(o), merge(lse)

def dilated_mixture(q, k, v):
    outs, lses = [], []
    for g, (w, d) in enumerate(DIL_GROUPS):
        sl = slice(g * HEADS_PER_DIL_GROUP, (g + 1) * HEADS_PER_DIL_GROUP)
        o, lse = dilated_window_attention(q[:, sl], k[:, sl], v[:, sl], w, d)
        outs.append(o)
        lses.append(lse)
    o = jnp.stack(outs, axis=0)
    wgt = jax.nn.softmax(jnp.stack(lses, axis=0), axis=0)
    return jnp.sum(wgt[..., None] * o, axis=0)

def moba_attention(q, k, v):
    B, H, S, Dh = q.shape
    L = -(-S // MOBA_BLOCK) * MOBA_BLOCK
    nblk = L // MOBA_BLOCK
    topk = min(MOBA_TOPK, nblk)
    pad = ((0, 0), (0, 0), (0, L - S), (0, 0))
    qp, kp, vp = jnp.pad(q, pad), jnp.pad(k, pad), jnp.pad(v, pad)
    kblocks = kp.reshape(B, H, nblk, MOBA_BLOCK, Dh)
    vblocks = vp.reshape(B, H, nblk, MOBA_BLOCK, Dh)
    kmean = jnp.mean(kblocks, axis=3)
    scale = Dh ** -0.5
    gather = jax.vmap(jax.vmap(lambda blocks, idx: blocks[idx]))

    def chunk(c):
        start = c * MOBA_QCHUNK
        qc = lax.dynamic_slice_in_dim(qp, start, MOBA_QCHUNK, axis=2)
        qpos = start + jnp.arange(MOBA_QCHUNK)
        own = start // MOBA_BLOCK
        gate = jnp.einsum('bhqd,bhnd->bhqn', qc, kmean)
        gate = jnp.where((jnp.arange(nblk) < own)[None, None, None, :], gate, -jnp.inf)
        _, idx = lax.top_k(gate, topk)
        valid = idx < own
        ksel = gather(kblocks, idx)
        vsel = gather(vblocks, idx)
        s_sel = jnp.einsum('bhqd,bhqjkd->bhqjk', qc, ksel) * scale
        s_sel = jnp.where(valid[..., None], s_sel, -jnp.inf).reshape(B, H, MOBA_QCHUNK, topk * MOBA_BLOCK)
        kown = lax.dynamic_index_in_dim(kblocks, own, axis=2, keepdims=False)
        vown = lax.dynamic_index_in_dim(vblocks, own, axis=2, keepdims=False)
        s_own = jnp.einsum('bhqd,bhkd->bhqk', qc, kown) * scale
        kpos = own * MOBA_BLOCK + jnp.arange(MOBA_BLOCK)
        s_own = jnp.where(kpos[None, :] <= qpos[:, None], s_own, -jnp.inf)
        p = jax.nn.softmax(jnp.concatenate([s_own, s_sel], axis=-1), axis=-1)
        p_own = p[..., :MOBA_BLOCK]
        p_sel = p[..., MOBA_BLOCK:].reshape(B, H, MOBA_QCHUNK, topk, MOBA_BLOCK)
        return (jnp.einsum('bhqk,bhkd->bhqd', p_own, vown)
                + jnp.einsum('bhqjk,bhqjkd->bhqd', p_sel, vsel))

    o = lax.map(chunk, jnp.arange(L // MOBA_QCHUNK))
    return jnp.moveaxis(o, 0, 2).reshape(B, H, L, Dh)[:, :, :S]

def stick_breaking_attention(q, k, v):
    B, H, S, Dh = q.shape
    scale = Dh ** -0.5
    outs = []
    for start in range(0, S, SB_QBLOCK):
        end = min(start + SB_QBLOCK, S)
        z = jnp.einsum('bhqd,bhkd->bhqk', q[:, :, start:end], k[:, :, :end]) * scale
        causal = jnp.arange(end)[None, :] < jnp.arange(start, end)[:, None]
        log_1m = jnp.where(causal, jax.nn.log_sigmoid(-z), 0.0)
        suffix = lax.cumsum(log_1m, axis=3, reverse=True) - log_1m
        a = jnp.where(causal, jnp.exp(jax.nn.log_sigmoid(z) + suffix), 0.0)
        outs.append(jnp.einsum('bhqk,bhkd->bhqd', a, v[:, :, :end]))
    return jnp.concatenate(outs, axis=2)

def hybrid_layer(x, norm_mix, w_in, w_out_a, w_out_b, w_out_c, w_o, norm_mlp, w_up, w_down, pos):
    B, S, D = x.shape
    h = rmsnorm(x, norm_mix)
    proj = h @ w_in

    def heads(t):
        return t.reshape(B, S, N_HEADS, HEAD_DIM).transpose(0, 2, 1, 3).astype(jnp.float32)

    q = heads(proj[..., :MIX_WIDTH])
    k = heads(proj[..., MIX_WIDTH:2 * MIX_WIDTH])
    v = heads(proj[..., 2 * MIX_WIDTH:3 * MIX_WIDTH])
    gates = jax.nn.sigmoid(proj[..., 3 * MIX_WIDTH:]).reshape(B, S, N_BRANCHES, D)

    n_rot = N_HEADS_A + N_HEADS_B
    q = jnp.concatenate([partial_rope(q[:, :n_rot], pos), q[:, n_rot:]], axis=1)
    k = jnp.concatenate([partial_rope(k[:, :n_rot], pos), k[:, n_rot:]], axis=1)

    a_sl = slice(0, N_HEADS_A)
    b_sl = slice(N_HEADS_A, N_HEADS_A + N_HEADS_B)
    c_sl = slice(N_HEADS_A + N_HEADS_B, N_HEADS)
    o_a = dilated_mixture(q[:, a_sl], k[:, a_sl], v[:, a_sl])
    o_b = moba_attention(q[:, b_sl], k[:, b_sl], v[:, b_sl])
    o_c = stick_breaking_attention(q[:, c_sl], k[:, c_sl], v[:, c_sl])

    def flat(o):
        return o.transpose(0, 2, 1, 3).reshape(B, S, -1).astype(x.dtype)

    y_a = flat(o_a) @ w_out_a
    y_b = flat(o_b) @ w_out_b
    y_c = flat(o_c) @ w_out_c
    merged = gates[:, :, 0] * y_a + gates[:, :, 1] * y_b + gates[:, :, 2] * y_c
    x = x + merged @ w_o

    h = rmsnorm(x, norm_mlp)
    return x + jnp.square(jax.nn.relu(h @ w_up)) @ w_down

def second_inputs(seed: int = 0) -> dict:
    key = jax.random.key(seed)
    ks = jax.random.split(key, 12)
    f32 = jnp.float32

    def nrm(k, shape, fan_in):
        return jax.random.normal(k, shape, f32) * (fan_in ** -0.5)

    x = jax.random.normal(ks[0], (BATCH, SEQ, D_MODEL), f32)
    norm_mix = 1.0 + 0.05 * jax.random.normal(ks[1], (DEPTH, D_MODEL), f32)
    w_in = nrm(ks[2], (DEPTH, D_MODEL, IN_COLS), D_MODEL)
    w_out_a = nrm(ks[3], (DEPTH, WIDTH_A, D_MODEL), WIDTH_A)
    w_out_b = nrm(ks[4], (DEPTH, WIDTH_B, D_MODEL), WIDTH_B)
    w_out_c = nrm(ks[5], (DEPTH, WIDTH_C, D_MODEL), WIDTH_C)
    w_o = nrm(ks[6], (DEPTH, D_MODEL, D_MODEL), D_MODEL)
    norm_mlp = 1.0 + 0.05 * jax.random.normal(ks[7], (DEPTH, D_MODEL), f32)
    w_up = nrm(ks[8], (DEPTH, D_MODEL, D_FF), D_MODEL)
    w_down = nrm(ks[9], (DEPTH, D_FF, D_MODEL), D_FF)
    norm_final = 1.0 + 0.05 * jax.random.normal(ks[10], (D_MODEL,), f32)
    return {"x": x, "norm_mix": norm_mix, "w_in": w_in, "w_out_a": w_out_a,
            "w_out_b": w_out_b, "w_out_c": w_out_c, "w_o": w_o, "norm_mlp": norm_mlp,
            "w_up": w_up, "w_down": w_down, "norm_final": norm_final}

def second_block(x, norm_mix, w_in, w_out_a, w_out_b, w_out_c, w_o, norm_mlp, w_up, w_down, norm_final):
    pos = jnp.arange(x.shape[1], dtype=jnp.float32)
    for layer in range(DEPTH):
        x = hybrid_layer(x, norm_mix[layer], w_in[layer], w_out_a[layer], w_out_b[layer],
                         w_out_c[layer], w_o[layer], norm_mlp[layer], w_up[layer],
                         w_down[layer], pos)
    return rmsnorm(x, norm_final)


def setup_inputs(seed=0):
    out = dict(first_inputs(seed))
    for name, value in second_inputs(seed + 1).items():
        if name != "x":
            out[name + "_2"] = value
    return out


def reference(
    x, c, ctx, c_ctx, mod_w, mod_b, norm1_g, norm2_g, ev_w_in, ev_sink, ev_sgu_norm_g, ev_sgu_w,
    ev_sgu_b, ev_w_out, od_w_in, od_q_norm_g, od_w_uq, od_kv_norm_g, od_w_ukv, od_conv_w,
    od_w_out, router_w, exp_w1, exp_w3, exp_w2, final_g, norm_mix_2, w_in_2, w_out_a_2,
    w_out_b_2, w_out_c_2, w_o_2, norm_mlp_2, w_up_2, w_down_2, norm_final_2,
):
    x = first_block(
        x, c, ctx, c_ctx, mod_w, mod_b, norm1_g, norm2_g, ev_w_in, ev_sink, ev_sgu_norm_g,
        ev_sgu_w, ev_sgu_b, ev_w_out, od_w_in, od_q_norm_g, od_w_uq, od_kv_norm_g, od_w_ukv,
        od_conv_w, od_w_out, router_w, exp_w1, exp_w3, exp_w2, final_g,
    )
    return second_block(
        x, norm_mix_2, w_in_2, w_out_a_2, w_out_b_2, w_out_c_2, w_o_2, norm_mlp_2, w_up_2,
        w_down_2, norm_final_2,
    )


_drawn_inputs = setup_inputs


def setup_inputs(seed=0):
    import zlib

    import numpy as np

    out = dict(_drawn_inputs(seed))
    spreads = {}
    factors = {'mod_b': 3.142,
     'norm2_g': 2.799,
     'ev_sink': 8.0,
     'ev_sgu_norm_g': 4.486,
     'od_q_norm_g': 8.0,
     'od_kv_norm_g': 8.0}
    for name, (base, spread) in spreads.items():
        noise = np.random.default_rng([zlib.crc32(name.encode()), seed]).standard_normal(out[name].shape)
        drawn = base * np.exp(spread * noise) if base else spread * noise
        out[name] = jnp.asarray(drawn.astype(out[name].dtype))
    for name, factor in factors.items():
        out[name] = (out[name] * factor).astype(out[name].dtype)
    return out
```

```python
from contextlib import ExitStack, contextmanager

import numpy as np

import concourse.bass as bass
from concourse import mybir

F32 = mybir.dt.float32
ALU = mybir.AluOpType
ACT = mybir.ActivationFunctionType
AX = mybir.AxisListType

P = 128
D = 1024
SEQ = 256
TT = SEQ // P
KD = D // P
EPS = 1e-6
NEG = -1e30
CHUNK = 4096
SLOTS = 6
BANKS = 8
NCOL = CHUNK // KD
GRID_W = 64

N_EXP = 16
CAP = 2 * SEQ // N_EXP
PER_GROUP = P // CAP
GROUPS = N_EXP // PER_GROUP

EV_PAIRS = 4
EV_SCALE = 64 ** -0.5
WINDOW = 128
OD_HEADS = 8
OD_DIM = 96
OD_SCALE = OD_DIM ** -0.5
Q_LORA, KV_LORA, KR = 384, 256, 32
ZA_W = KV_LORA + KR + Q_LORA
ZB_W = 3 * 512
OD_TAIL = ZA_W + ZB_W - 4 * NCOL
UQ_W = OD_HEADS * OD_DIM

B2_HEADS = 24
B2_ROT = 18
B2_PAIRS = B2_HEADS // 2
B2_W = B2_HEADS * 64
B2_SCALE = 64 ** -0.5
B2_LAYERS = 2
WO_PIECES = (384, 384, 256)
N_FF = 8
MOE_STEPS, B2_STEPS = 7, 50


def pipeline(n, stages):
    last = max(lag for _, lag in stages)
    return [(name, step - lag) for step in range(n + last) for name, lag in stages if 0 <= step - lag < n]

ATT_LAGS = [("s", 0), ("t", 2), ("o", 3)]
EV_UNITS = [(h, t) for t in range(2 * TT) for h in range(2 * EV_PAIRS)]
OD_UNITS = [(h, t) for t in range(TT) for h in range(OD_HEADS)]
AB_UNITS = [("A", h, t) for h in range(4) for t in range(TT)] + [("B", h, t) for h in range(6) for t in range(TT)]
C_UNITS = list(range(6))

def ab_keys(kind, h, t):
    heads = [4 * g + h for g in range(3)] if kind == "A" else [12 + h]
    return [(hd, kt) for hd in heads for kt in range(t + 1)]

def ab_keys_per_bank(kind, h, t):
    keys = ab_keys(kind, h, t)
    return [keys[i:i + 4] for i in range(0, len(keys), 4)]

AB_SCHED = []
for _name, _u in pipeline(len(AB_UNITS), ATT_LAGS):
    _n = 1 if _name == "o" else len(ab_keys_per_bank(*AB_UNITS[_u]))
    AB_SCHED += [(_name, _u, _b) for _b in range(_n)]
C_SCHED = []
for _name, _u in pipeline(len(C_UNITS), [("s", 0), ("c", 2), ("o", 3)]):
    C_SCHED += [(_name, _u, _t) for _t in range(TT if _name == "o" else 1)]

FF_ORDER = pipeline(N_FF, [("up", 0), ("down", 1)])

TICKET = {}
LAP = {}

def _tickets():
    n = 0

    def stage(name, keys):
        nonlocal n
        for k in (range(keys) if isinstance(keys, int) else keys):
            TICKET[name, k] = n
            n += 1

    def repeated(name, first, times):
        nonlocal n
        per = n - first
        assert per % BANKS == 0, (name, per)
        LAP[name] = per // BANKS
        n = first + per * times

    def norm(name):
        stage(name, KD)

    for layer in range(2):
        streams = 2 if layer == 0 else 1
        L = str(layer)
        stage("mod" + L, 12)
        stage("modcol" + L, 1)
        stage("modrow" + L, 4 * streams)
        norm("n1_" + L)
        if layer == 0:
            stage("evz", [(c, t) for c in range(4) for t in range(4)])
            stage("sgu", 4)
            stage("evqk", 1 + EV_PAIRS)
            stage("evatt", pipeline(len(EV_UNITS), ATT_LAGS))
        else:
            stage("odz", [(c, t) for c in range(5) for t in range(4 if c == 0 else 2)])
            stage("conv", [(t, d) for t in range(TT) for d in range(2)])
            stage("ckvT", 2)
            stage("cqT", 3)
            stage("uq", [(p, t) for p in range(2) for t in range(TT)])
            stage("ukv", [(p, t) for p in range(2) for t in range(4)])
            stage("odkT", OD_HEADS)
            stage("odqT", OD_HEADS // 2)
            stage("odatt", pipeline(len(OD_UNITS), ATT_LAGS))
        stage("cat" + L, KD)
        stage("mix" + L, [(c, t) for c in range(2) for t in range(2 * streams)])
        norm("n2_" + L)
        stage("logit" + L, 1)
        stage("affT" + L, 1)
        stage("selT" + L, 1)
        stage("rank" + L, 1)
        stage("gateT" + L, GROUPS)
        first = n
        for e in range(PER_GROUP):
            stage("moe" + L, [(e, k) for k in ("x", "a0", "b0", "a1", "t0", "b1", "y", "t1")])
        stage("comb" + L, 8)
        repeated("moe" + L, first, GROUPS)
    first = n
    norm("nmix")
    stage("qkv", [(c, t) for c in range(9) for t in range(TT)])
    stage("qkT", [(w, j) for w in range(2) for j in range(B2_PAIRS // 2)])
    stage("ab", AB_SCHED)
    stage("c", C_SCHED)
    stage("ocat", 4)
    stage("merge", [(c, t, k) for c in range(2) for t in range(TT) for k in range(6)])
    stage("mergeT", 4)
    stage("wo", [(c, t) for c in range(3) for t in range(TT)])
    norm("nmlp")
    for which, j in FF_ORDER:
        stage(which, [(j, 0), (j, 1)] if which == "up" else [(j, t, h) for t in range(TT) for h in range(2)])
    repeated("b2", first, B2_LAYERS)

_tickets()

CHUNK_AT = {}
CHUNK_LAP = {}

def _chunks():
    n = 0

    def put(name, count):
        nonlocal n
        for k in range(count):
            CHUNK_AT[name, k] = n
            n += 1

    def repeated(name, first, times):
        nonlocal n
        per = n - first
        assert per % SLOTS == 0, (name, per)
        CHUNK_LAP[name] = per // SLOTS
        n = first + per * times

    put("mod0", 12)
    put("evz", 4)
    put("mix0", 2)
    first = n
    put("moe0", 6 * PER_GROUP)
    repeated("moe0", first, GROUPS)
    put("mod1", 12)
    put("odz", 5)
    put("ukv", 1)
    put("mix1", 2)
    first = n
    put("moe1", 6 * PER_GROUP)
    repeated("moe1", first, GROUPS)
    first = n
    put("qkv", 9)
    put("merge", 8)
    put("wo", 3)
    for which, j in FF_ORDER:
        CHUNK_AT[which, j] = n
        n += 1
    repeated("b2", first, B2_LAYERS)
    return n

N_CHUNKS = _chunks()


def _rope(n_freq_total, pos_pairs):
    c = np.cos(pos_pairs).astype(np.float32).reshape(TT, P, -1).transpose(1, 0, 2)
    s = np.sin(pos_pairs).astype(np.float32).reshape(TT, P, -1).transpose(1, 0, 2)
    return np.concatenate([c.reshape(P, -1), s.reshape(P, -1)], 1)

def _axial(rot):
    rows = SEQ // GRID_W
    row = np.repeat(np.arange(rows, dtype=np.float32), GRID_W)
    col = np.tile(np.arange(GRID_W, dtype=np.float32), rows)
    n = rot // 4
    inv = np.power(np.float32(10000.0), -np.arange(n, dtype=np.float32) / np.float32(n)).astype(np.float32)
    return _rope(2 * n, np.concatenate([row[:, None] * inv, col[:, None] * inv], 1).astype(np.float32))

def _partial():
    inv = np.exp(np.float32(-np.log(500000.0)) * np.arange(0, 16, 2, dtype=np.float32) / np.float32(16))
    return _rope(8, (np.arange(SEQ, dtype=np.float32)[:, None] * inv.astype(np.float32)[None, :]).astype(np.float32))

def shape_constants():
    p = np.arange(P)[:, None]
    q = np.arange(P)[None, :]
    f = np.float32
    sel = np.zeros((P, 2 * P), f)
    sel[0, :P] = 1
    sel[1, P:] = 1
    base = np.concatenate([(p == q).astype(f), (p <= q).astype(f), (p >= q).astype(f), np.ones((P, P), f),
                           np.broadcast_to(np.arange(1, CAP + 1, dtype=f), (P, CAP)), sel], 1)
    keys = np.arange(SEQ)[None, :]
    win = []
    for t in range(TT):
        qp = t * P + p
        win += [np.where(np.abs(keys - qp) <= WINDOW, 0, NEG).astype(f), np.zeros((P, SEQ), f)]
    shift = np.concatenate([(p == q - 1), (p == P - 1) & (q == 0), (p == q + 1), (p == 0) & (q == P - 1)], 1).astype(f)
    amask = []
    for t in range(TT):
        kk = np.arange((t + 1) * P)[None, :]
        d = t * P + p - kk
        for span, dil in ((128, 1), (512, 4), (2048, 16)):
            amask.append(np.where((d >= 0) & (d <= span) & (d % dil == 0), 0, NEG).astype(f))
    bmask = np.where(keys <= P + p, 0, NEG).astype(f)
    cmask = np.concatenate([np.where(p < keys, 0, NEG), np.where(p < q, 0, NEG)], 1).astype(f)
    return {"base": base, "win": np.concatenate(win, 1), "ev_rope": _axial(64), "od_rope": _axial(32),
            "shift": shift, "b2_masks": np.concatenate(amask + [bmask, cmask], 1), "b2_rope": _partial()}

IDENT, TRI_LE, TRI_GE, ONES, IOTA, SEL = 0, 128, 256, 384, 512, 544
BASE_W = 800
G_N1, G_N2, G_MIX, G_MLP, G_Q, G_KV = 0, 16, 32, 48, 64, 67
SMALL_W = 69 + 2 * KD * N_EXP
ARENA = 22668

MROW, MODB = 0, 15360
HT, XN, BC = 0, 4096, 11264
EV_CAT, EV_Z, EV_CATT = 0, 4096, 4096
EV_QT, EV_KT, EV_S, EV_PT, EV_PACK = 15360, 17408, 17920, 19456, 20480
EV_WIN, EV_SGUW, EV_SGUG, EV_SGUB, EV_SINK, EV_ROPE = 20480, 21504, 22016, 22528, 22532, 22540
EV_PACK_W = 2188
MOE_XN, MOE_HT, MOE_YST, MOE_OH, MOE_AFF = 0, 4096, 4096, 8192, 10240
MOE_GT, MOE_GW, MOE_XST, MOE_XTMP, MOE_G, MOE_GTR, MOE_GTST = 15360, 17408, 17408, 18432, 19456, 20480, 21504
MOE_W = 22016
MOE_TMP, MIX_TMP = 6144, 19456
OD_HT, OD_KT, OD_ZA, OD_ZC, OD_CQT, OD_CKVT, OD_ZB, OD_KF, OD_ROPE = 0, 0, 4096, 5440, 6016, 6784, 7808, 7808, 10880
OD_QT, OD_S, OD_PT, OD_SHIFT, OD_CONVW, OD_Q, OD_CAT = 15360, 17408, 18944, 19968, 20480, 20480, 13312
OD_CATT = 4096
B2_Q, B2_K, B2_V, B2_QT, B2_KT, B2_MASK = 0, 3072, 6144, 9216, 12288, 15360
B2_S, B2_PT, B2_ROPE, FINAL_G = 17152, 19456, 20992, 21024
B2_XN1, B2_XN2, B2_OCAT, B2_OCATT, B2_MERGED, B2_MERGT, B2_SIG, B2_HID = 0, 6144, 0, 3072, 9216, 11264, 17152, 17152

def program(nc, stream, base_c, small_c, ccols, x_in, modb, ev_pack, od_rope, od_pack, b2_masks, b2_rope, gains, out):
    with ExitStack() as ctx:
        def sb(name, shape):
            return ctx.enter_context(nc.sbuf_tensor(name, shape, F32))

        sems = {}

        def sem(name):
            if name not in sems:
                sems[name] = ctx.enter_context(nc.semaphore(name))
            return sems[name]

        ring = sb("ring", [P, SLOTS, CHUNK])
        X = sb("x", [P, 2 * TT, D])
        base = sb("base", [P, BASE_W])
        small = sb("small", [P, SMALL_W])
        sc = sb("silu_c", [P, KD, 2])
        modc = sb("mod_columns", [P, 4, KD, 2])
        A1, B1, A2, B2 = (modc[:, n] for n in range(4))
        stat = sb("statistics", [P, 653])
        arena = sb("arena", [P, ARENA])
        psum = [ctx.enter_context(nc.psum_tensor(f"bank{b}", [P, 512], F32)) for b in range(BANKS)]

        slot_loaded = [sem(f"slot_loaded{s}") for s in range(SLOTS)]
        slot_free = [sem(f"slot_free{s}") for s in range(SLOTS)]
        filled_sem = [sem(f"filled{b}") for b in range(BANKS)]
        drained_sem = [sem(f"drained{b}") for b in range(BANKS)]

        def region(off, *shape):
            n = int(np.prod(shape))
            v = arena[:, off:off + n]
            if len(shape) == 2:
                return v.rearrange("p (a b) -> p a b", a=shape[0])
            if len(shape) == 3:
                return v.rearrange("p (a b c) -> p a b c", a=shape[0], b=shape[1])
            return v

        ident = base[:, IDENT:IDENT + P]
        tri_le = base[:, TRI_LE:TRI_LE + P]
        tri_ge = base[:, TRI_GE:TRI_GE + P]
        ones = base[:, ONES:ONES + P]
        iota = base[:, IOTA:IOTA + CAP]
        router = small[:, 69:].rearrange("p (l k e) -> p l k e", l=2, k=KD)

        def gain(off, n=KD):
            return small[:, off:off + n]

        def bank(name, key):
            return psum[TICKET[name, key] % BANKS]

        def chunk(name, k):
            return ring[:, CHUNK_AT[name, k] % SLOTS, :]

        class Banks:

            def __init__(self, eng):
                self.eng, self.lap = eng, 0

            def filled(self, name, key):
                n = TICKET[name, key]
                self.eng.wait_ge(filled_sem[n % BANKS], self.lap + (n // BANKS + 1))

            def drained(self, name, key, back=0):
                n = TICKET[name, key]
                self.eng.wait_ge(drained_sem[n % BANKS], self.lap + (n // BANKS + 1 - back))

            def vacant(self, name, key):
                n = TICKET[name, key]
                if n >= BANKS:
                    self.eng.wait_ge(drained_sem[n % BANKS], self.lap + n // BANKS)

        def frees(name, key):
            return drained_sem[TICKET[name, key] % BANKS]

        def fills(name, key):
            return filled_sem[TICKET[name, key] % BANKS]

        class Steps:

            def __init__(self, eng, semaphore):
                self.eng, self.sem, self.base, self.n = eng, semaphore, 0, 0

            def add(self, ins):
                ins.then_inc(self.sem, 1)
                self.n += 1

            def sync(self):
                self.eng.wait_ge(self.sem, self.base + self.n)

            def do(self, ins):
                self.add(ins)
                self.sync()

            @contextmanager
            def loop(self, times, per):
                before = self.base + self.n
                with self.eng.Fori(0, times) as i:
                    self.base, self.n = i * per + before, 0
                    yield i
                    assert self.n == per, (self.n, per)
                self.base, self.n = before + times * per, 0

        mrow = arena[0:2, MROW:MROW + 6 * D]
        modb_sb = arena[0:2, MODB:MODB + 6 * D]
        bc = region(BC, 4, D)
        xn4 = region(XN, 4, D)
        ht4 = region(HT, KD, 512)
        ev_z = region(EV_Z, 4, 1792)
        ev_qt = region(EV_QT, EV_PAIRS, 512)
        ev_kt = region(EV_KT, 512)
        ev_s = region(EV_S, 3, 512)
        ev_pt = region(EV_PT, 2, 4, P)
        ev_win = region(EV_WIN, TT, 512)
        ev_sguw = region(EV_SGUW, 4, P)
        ev_sgug = region(EV_SGUG, 512)
        ev_sgub = region(EV_SGUB, 4)
        ev_sink = region(EV_SINK, 8)

        ev_cos = region(EV_ROPE, TT, 32)
        ev_sin = region(EV_ROPE + TT * 32, TT, 32)
        ev_cat = region(EV_CAT, 4, D)
        ev_catt = region(EV_CATT, KD, 512)
        od_za = region(OD_ZA, TT, ZA_W)
        od_zb = region(OD_ZB, TT, ZB_W)
        od_zc = region(OD_ZC, TT, KV_LORA + KR)
        od_cqt = region(OD_CQT, 3, SEQ)
        od_ckvt = region(OD_CKVT, 2, 512)
        od_kf = region(OD_KF, 4, OD_HEADS * OD_DIM)
        od_v = X[:, TT:2 * TT, :].rearrange("p a b -> p (a b)").rearrange("p (t c) -> p t c", t=4)
        od_q = region(OD_Q, TT, UQ_W)
        od_kt = region(OD_KT, OD_HEADS, 512)
        od_qt = region(OD_QT, OD_HEADS, SEQ)
        od_s = region(OD_S, 3, 512)
        od_pt = region(OD_PT, 2, 4, P)
        od_shift = region(OD_SHIFT, 4, P)
        od_convw = region(OD_CONVW, 3, 512)
        od_cos = region(OD_ROPE, TT, 16)
        od_sin = region(OD_ROPE + TT * 16, TT, 16)
        od_cat = region(OD_CAT, TT, D)
        od_catt = region(OD_CATT, KD, SEQ)
        moe_ht = region(MOE_HT, KD, 512)
        moe_xn = region(MOE_XN, 4, D)
        moe_aff = region(MOE_AFF, 64)
        moe_work = region(MOE_W, 256)
        moe_chosen = region(MOE_W + 256, 256)
        moe_oh = region(MOE_OH, 4, N_EXP * CAP)
        moe_gw = region(MOE_GW, 4, N_EXP * CAP)
        moe_gt = region(MOE_GT, GROUPS, 512)
        moe_gtst = region(MOE_GTST, 512)
        moe_xst = region(MOE_XST, 2, 512)
        moe_xtmp = region(MOE_XTMP, 512)
        moe_sil = region(MOE_G, 2, 256)
        moe_g = region(MOE_G + 512, 2, 256)
        moe_gtr = region(MOE_GTR, 2, 2, 256)
        moe_yst = region(MOE_YST, 2, D)
        moe_tmp = region(MOE_TMP, 2, 512)
        mix_tmp = region(MIX_TMP, 2, 512)
        b2_q = region(B2_Q, TT, B2_W)
        b2_k = region(B2_K, TT, B2_W)
        b2_v = region(B2_V, TT, B2_W)
        b2_qt = region(B2_QT, B2_PAIRS, SEQ)
        b2_kt = region(B2_KT, B2_PAIRS, SEQ)
        b2_ht = X[:, TT:2 * TT, :].rearrange("p a b -> p (a b)").rearrange("p (k c) -> p k c", k=KD)
        b2_s = region(B2_S, 3, 768)
        b2_pt = region(B2_PT, 2, 6, P)
        b2_cos = region(B2_ROPE, TT, 8)
        b2_sin = region(B2_ROPE + TT * 8, TT, 8)
        b2_ocat = region(B2_OCAT, TT, D)
        b2_ocatt = region(B2_OCATT, KD, SEQ)
        b2_merged = region(B2_MERGED, TT, D)
        b2_mergt = region(B2_MERGT, KD, SEQ)
        b2_sig = region(B2_SIG, 3, 512)
        b2_prod = region(B2_SIG + 1536, 2, 512)
        b2_hid = region(B2_HID, 2, 4, SEQ)
        b2_amask = [region(B2_MASK, 384), region(B2_MASK + 384, 768)]
        b2_bmask = [region(B2_MASK, P), region(B2_MASK + 1152, 256)]
        b2_cmask = region(B2_MASK + 1408, 384)
        final_g = region(FINAL_G, D)

        mx, nm, ls, l, rl = (stat[:, 48 * n:48 * n + 48] for n in range(5))
        ss, rstd = stat[:, 240:248], stat[:, 248:256]
        bn, mv = stat[:, 256:280], stat[:, 280:288]
        lg, lge, lgs = stat[:, 288:352], stat[:, 352:416], stat[:, 416:424]
        pos = stat[:, 424:488]
        mkT = stat[:, 488:552]
        mx2 = stat[:, 552:592]
        ev_nsink = mx2[:, 0:8]
        layer_gain = stat[:, 592:608]
        ss2, rstd2 = stat[:, 608:614], stat[:, 614:620]

        root4, eps, idle = stat[:, 620:624], stat[:, 624:625], stat[:, 625:653]

        block = ctx.enter_context(nc.Block())

        @block.sync
        def _(sp):
            for s in range(SLOTS):
                sp.dma_start(ring[:, s, :], stream[s]).then_inc(slot_loaded[s], 16)
            rounds = N_CHUNKS // SLOTS
            with sp.Fori(1, rounds) as r:
                for s in range(SLOTS):
                    sp.wait_ge(slot_free[s], r)
                    sp.dma_start(ring[:, s, :], stream[bass.ds(r * SLOTS + s, 1)].rearrange("a p n -> (a p) n"))\
                        .then_inc(slot_loaded[s], 16)
            for s in range(N_CHUNKS - rounds * SLOTS):
                sp.wait_ge(slot_free[s], rounds)
                sp.dma_start(ring[:, s, :], stream[rounds * SLOTS + s]).then_inc(slot_loaded[s], 16)
            sp.wait_ge(sem("result"), TT)
            sp.dma_start(out.rearrange("a (t p) d -> p (a t) d", p=P), xn4[:, 0:TT, :]).then_inc(sem("stored"), 16)
            sp.wait_ge(sem("stored"), 16)

        @block.gpsimd
        def _(pool):
            def load(dst, src, name):
                pool.dma_start(dst, src).then_inc(sem(name), 16)

            load(sc[:, :, :], ccols, "c_in")
            load(modb_sb, modb[0], "modb_in")
            load(base[:, :], base_c, "base_in")
            load(X[:, :, :], x_in, "x_in")
            load(small[:, :], small_c, "small_in")
            pool.wait_ge(sem("mod_done"), 1)
            load(region(EV_PACK, EV_PACK_W), ev_pack, "ev_in")
            pool.wait_ge(sem("x_moe"), GROUPS)
            load(modb_sb, modb[1], "modb_in")
            pool.wait_ge(sem("mod_done"), 2)
            load(region(OD_SHIFT, 4 * P + 3 * 512), od_pack, "od_in")
            load(region(OD_ROPE, 4 * 16), od_rope, "od_in2")
            pool.wait_ge(sem("x_moe"), 2 * GROUPS)
            load(region(B2_MASK, 1792), b2_masks, "b2_in")
            load(region(B2_ROPE, 4 * 8), b2_rope, "b2_in2")
            load(final_g, gains[0], "fg_in")
            pool.wait_ge(sem("x_final"), TT)
            load(final_g, gains[1], "fg_in")

        @block.tensor
        def _(pe):
            b = Banks(pe)
            state = {"chunk_lap": 0}
            owed = []

            def mm(o, lhsT, rhs, start, stop, sig=None):
                ins = pe.matmul(o, lhsT, rhs, start=start, stop=stop)
                if sig is not None:
                    ins.then_inc(sig, 1)
                elif owed:
                    ins.then_inc(slot_free[owed.pop(0)], 1)

            def turn(o, in_, n=P, sig=None):
                ins = pe.transpose(o, in_, base[0:n, IDENT:IDENT + n])
                if sig is not None:
                    ins.then_inc(sig, 1)
                elif owed:
                    ins.then_inc(slot_free[owed.pop(0)], 1)

            def arrived(name, k):
                n = CHUNK_AT[name, k]
                pe.wait_ge(slot_loaded[n % SLOTS], state["chunk_lap"] * 16 + 16 * (n // SLOTS + 1))

            def used(name, k):
                owed.append(CHUNK_AT[name, k] % SLOTS)

            def settle():
                while owed:
                    pe.drain().then_inc(slot_free[owed.pop(0)], 1)

            def norm(name, xn, tiles, ready, count):
                pe.wait_ge(ready, count)
                for k in range(KD):
                    b.vacant(name, k)
                    for t in range(tiles):
                        turn(bank(name, k)[:, t * P:(t + 1) * P], xn[:, t, k * P:(k + 1) * P],
                             sig=fills(name, k) if t == tiles - 1 else None)

            def product(name, key, lhs, rhs, kts, width, sig=True, col=0):
                o = bank(name, key)[:, col:col + width]
                for n in range(kts):
                    mm(o, lhs(n), rhs(n), n == 0, n == kts - 1, fills(name, key) if sig and n == kts - 1 else None)

            def mod(layer):
                L = str(layer)
                pe.wait_ge(sem("silu_c"), 1)
                for c in range(12):
                    arrived("mod" + L, c)
                    b.vacant("mod" + L, c)
                    w = chunk("mod" + L, c).rearrange("p (k n) -> p k n", k=KD)
                    o = bank("mod" + L, c)[0:2, :]
                    for k in range(KD):
                        mm(o, sc[:, k, :], w[:, k, :], k == 0, k == KD - 1, fills("mod" + L, c) if k == KD - 1 else None)
                    used("mod" + L, c)
                if layer == 0:
                    pe.wait_ge(sem("base_in"), 16)
                b.drained("mod" + L, 11)
                b.vacant("modcol" + L, 0)
                cols = bank("modcol" + L, 0)
                for n, v in enumerate((1, 0, 4, 3)):
                    for k in range(KD):
                        at = (n * KD + k) * 2
                        turn(cols[:, at:at + 2], mrow[:, v * D + k * P:v * D + (k + 1) * P], 2,
                             fills("modcol" + L, 0) if n == 3 and k == KD - 1 else None)
                streams = 2 - layer
                for n in range(4 * streams):
                    v, s, h = n // (2 * streams), n // 2 % streams, n % 2
                    b.vacant("modrow" + L, n)
                    mm(bank("modrow" + L, n)[:, :], base[0:2, SEL + s * P:SEL + (s + 1) * P],
                       mrow[:, (2 + 3 * v) * D + h * 512:(2 + 3 * v) * D + (h + 1) * 512], True, True, fills("modrow" + L, n))

            def attention(name, units, score, nk, value, p, pt, ready):
                for kind, u in pipeline(len(units), ATT_LAGS):
                    b.vacant(name, (kind, u))
                    o = bank(name, (kind, u))
                    if kind == "s":
                        score(u, o)
                    elif kind == "t":
                        ready(u)
                        for n in range(nk(u)):
                            turn(o[:, n * P:(n + 1) * P], p[:, u % 3, n * P:(n + 1) * P],
                                 sig=fills(name, (kind, u)) if n == nk(u) - 1 else None)
                    else:
                        b.drained(name, ("t", u))
                        for n in range(nk(u)):
                            mm(o[:, 0:64], pt[:, u % 2, n, :], value(u, n), n == 0, n == nk(u) - 1,
                               fills(name, (kind, u)) if n == nk(u) - 1 else None)

            def cat_turns(name, src, tiles):
                for k in range(KD):
                    b.vacant(name, k)
                    for t in range(tiles):
                        turn(bank(name, k)[:, t * P:(t + 1) * P], src[:, t, k * P:(k + 1) * P],
                             sig=fills(name, k) if t == tiles - 1 else None)

            def mix(layer, catt, tiles):
                L = str(layer)
                for k in (6, 7):
                    b.drained("cat" + L, k)
                for c in range(2):
                    arrived("mix" + L, c)
                    w = chunk("mix" + L, c).rearrange("p (k n) -> p k n", k=KD)
                    for t in range(tiles):
                        b.vacant("mix" + L, (c, t))
                        product("mix" + L, (c, t), lambda k: catt[:, k, t * P:(t + 1) * P], lambda k: w[:, k, :], KD, 512)
                    used("mix" + L, c)

            def experts(layer):
                L = str(layer)
                streams = 2 - layer
                tiles = TT * streams
                rows = streams * CAP
                parts = P // rows
                moe = "moe" + L
                for k in (6, 7):
                    b.drained("n2_" + L, k)
                b.vacant("logit" + L, 0)
                o = bank("logit" + L, 0)
                for t in range(tiles):
                    at = ((t % TT) * streams + t // TT) * N_EXP
                    for k in range(KD):
                        mm(o[:, at:at + N_EXP], moe_ht[:, k, t * P:(t + 1) * P],
                           router[:, layer, k, :], k == 0, k == KD - 1,
                           fills("logit" + L, 0) if t == tiles - 1 and k == KD - 1 else None)
                ne = streams * N_EXP
                pe.wait_ge(sem("aff"), layer + 1)
                b.vacant("affT" + L, 0)
                for t in range(TT):
                    turn(bank("affT" + L, 0)[0:ne, t * P:(t + 1) * P], moe_aff[:, t * ne:(t + 1) * ne],
                         sig=fills("affT" + L, 0) if t == TT - 1 else None)
                pe.wait_ge(sem("chosen"), layer + 1)
                b.vacant("selT" + L, 0)
                for t in range(TT):
                    turn(bank("selT" + L, 0)[:, t * ne:(t + 1) * ne], moe_chosen[0:ne, t * P:(t + 1) * P], ne,
                         fills("selT" + L, 0) if t == TT - 1 else None)
                b.drained("selT" + L, 0)
                b.vacant("rank" + L, 0)
                o = bank("rank" + L, 0)
                mm(o[:, 0:ne], tri_le, mkT[:, 0:ne], True, True)
                mm(o[:, ne:2 * ne], ones, mkT[:, 0:ne], True, False)
                mm(o[:, ne:2 * ne], tri_le, mkT[:, ne:2 * ne], False, True, fills("rank" + L, 0))
                pe.wait_ge(sem("gated"), tiles * 1 if layer == 0 else 4 + tiles)
                for g in range(GROUPS):
                    b.vacant("gateT" + L, g)
                    for t in range(tiles):
                        turn(bank("gateT" + L, g)[:, t * P:(t + 1) * P], moe_gw[:, t, g * P:(g + 1) * P],
                             sig=fills("gateT" + L, g) if t == tiles - 1 else None)
                settle()
                b.drained("gateT" + L, GROUPS - 1)
                with pe.Fori(0, GROUPS) as i:
                    b.lap = i * LAP[moe]
                    state["chunk_lap"] = i * CHUNK_LAP[moe]
                    for e in range(PER_GROUP):
                        b.vacant(moe, (e, "x"))
                        o = bank(moe, (e, "x"))
                        for k in range(KD):
                            for s in range(streams):
                                at = (k * streams + s) * CAP
                                for t in range(TT):
                                    tok = s * TT + t
                                    mm(o[:, at:at + CAP], moe_xn[:, tok, k * P:(k + 1) * P],
                                       moe_oh[:, tok, bass.ds(i * P + e * CAP, CAP)], t == 0, t == TT - 1,
                                       fills(moe, (e, "x")) if (k, s, t) == (KD - 1, streams - 1, TT - 1) else None)
                        xs = moe_xst[:, e % 2, 0:KD * rows].rearrange("p (k n) -> p k n", k=KD)
                        width = NCOL // parts

                        def hidden(key, c):
                            arrived(moe, e * 6 + c)
                            b.vacant(moe, (e, key))
                            w = chunk(moe, e * 6 + c).rearrange("p (k n) -> p k n", k=KD)
                            o = bank(moe, (e, key))
                            for k in range(KD):
                                for q in range(parts):
                                    last = k == KD - 1 and q == parts - 1
                                    mm(o[q * rows:(q + 1) * rows, 0:width], xs[:, k, :], w[:, k, q * width:(q + 1) * width],
                                       k == 0, k == KD - 1, fills(moe, (e, key)) if last else None)
                            used(moe, e * 6 + c)

                        def turn_hidden(c):
                            b.drained(moe, (e, f"b{c}"))
                            b.vacant(moe, (e, f"t{c}"))
                            for j in range(width // P):
                                turn(bank(moe, (e, f"t{c}"))[:, j * P:(j + 1) * P], moe_g[:, c, j * P:(j + 1) * P],
                                     sig=fills(moe, (e, f"t{c}")) if j == width // P - 1 else None)

                        def down(c, kts):
                            w = chunk(moe, e * 6 + 4 + c).rearrange("p (k n) -> p k n", k=4)
                            o = bank(moe, (e, "y"))
                            yw = D // parts
                            for kt in kts:
                                q, j = kt // (width // P), kt % (width // P)
                                lhs = moe_gtr[:, e % 2, c, j * P + q * rows:j * P + (q + 1) * rows]
                                for n in range(parts):
                                    last = c == 1 and kt == 3 and n == parts - 1
                                    mm(o[n * rows:(n + 1) * rows, 0:yw], lhs, w[:, kt, n * yw:(n + 1) * yw],
                                       c == 0 and kt == 0, c == 1 and kt == 3, fills(moe, (e, "y")) if last else None)

                        b.drained(moe, (e, "x"))
                        pe.wait_ge(sem("xst" + L), i * PER_GROUP + e + 1)
                        hidden("a0", 0)
                        hidden("b0", 1)
                        hidden("a1", 2)
                        turn_hidden(0)
                        hidden("b1", 3)
                        arrived(moe, e * 6 + 4)
                        b.vacant(moe, (e, "y"))
                        b.drained(moe, (e, "t0"))
                        down(0, (0, 1))
                        turn_hidden(1)
                        down(0, (2, 3))
                        used(moe, e * 6 + 4)
                        arrived(moe, e * 6 + 5)
                        b.drained(moe, (e, "t1"))
                        down(1, (0, 1, 2, 3))
                        used(moe, e * 6 + 5)
                    settle()
                    pe.wait_ge(sem("gates_staged" + L), i + 1)
                    b.drained(moe, (PER_GROUP - 1, "y"))
                    pieces = 8 // tiles
                    w = D // pieces
                    for n in range(8):
                        t, c = n // pieces, n % pieces
                        b.vacant("comb" + L, n)
                        mm(bank("comb" + L, n)[:, 0:w], moe_gtst[:, t * P:(t + 1) * P],
                           moe_yst[:, t // TT, c * w:(c + 1) * w], True, True, fills("comb" + L, n))
                b.lap = 0
                state["chunk_lap"] = 0

            mod(0)
            norm("n1_0", xn4, 4, sem("xn"), 4)
            for k in (6, 7):
                b.drained("n1_0", k)
            for c in range(4):
                arrived("evz", c)
                width = 512 if c < 3 else 256
                w = chunk("evz", c)[:, 0:KD * width].rearrange("p (k n) -> p k n", k=KD)
                for t in range(4):
                    b.vacant("evz", (c, t))
                    product("evz", (c, t), lambda k: ht4[:, k, t * P:(t + 1) * P], lambda k: w[:, k, :], KD, width)
                used("evz", c)
            pe.wait_ge(sem("ev_in"), 16)
            for t in range(4):
                pe.wait_ge(sem("sgu_v"), t + 1)
                b.vacant("sgu", t)
                for g in range(4):
                    mm(bank("sgu", t)[:, g * P:(g + 1) * P], ev_sguw[:, g, :], ev_z[:, t, 512 + g * P:512 + (g + 1) * P],
                       True, True, fills("sgu", t) if g == 3 else None)
            b.drained("evz", (3, 3))
            pe.wait_ge(sem("ev_rope"), TT)
            for j in range(1 + EV_PAIRS):
                b.vacant("evqk", j)
                for t in range(4):
                    turn(bank("evqk", j)[:, t * P:(t + 1) * P], ev_z[:, t, 1152 + j * P:1152 + (j + 1) * P],
                         sig=fills("evqk", j) if t == 3 else None)

            def ev_score(u, o):
                h, t = EV_UNITS[u]
                r = 64 * (h % 2)
                if u == 0:
                    b.drained("evqk", EV_PAIRS)
                first = 0 if t < TT else SEQ
                mm(o[:, 0:512 - first], ev_qt[r:r + 64, h // 2, t * P:(t + 1) * P], ev_kt[r:r + 64, first:512],
                   True, True, fills("evatt", ("s", u)))

            def ev_keys(u):
                return 4 if EV_UNITS[u][1] < TT else 2

            def ev_value(u, n):
                h, t = EV_UNITS[u]
                return ev_z[:, n + (0 if t < TT else TT), 1024 + 64 * (h % 2):1088 + 64 * (h % 2)]

            attention("evatt", EV_UNITS, ev_score, ev_keys, ev_value, ev_s, ev_pt,
                      lambda u: pe.wait_ge(sem("ev_p"), u + 1))
            b.drained("evatt", ("o", len(EV_UNITS) - 1))
            b.drained("sgu", 3)
            cat_turns("cat0", ev_cat, 4)
            mix(0, ev_catt, 4)
            norm("n2_0", moe_xn, 4, sem("xn"), 8)
            experts(0)

            mod(1)
            norm("n1_1", xn4, 4, sem("xn"), 12)
            for k in (6, 7):
                b.drained("n1_1", k)
            for c in range(5):
                arrived("odz", c)
                width = 512 if c < 4 else OD_TAIL
                w = chunk("odz", c)[:, 0:KD * width].rearrange("p (k n) -> p k n", k=KD)
                for t in range(4 if c == 0 else 2):
                    n = width if t < TT else KV_LORA + KR
                    b.vacant("odz", (c, t))
                    product("odz", (c, t), lambda k: ht4[:, k, t * P:(t + 1) * P], lambda k: w[:, k, 0:n], KD, n)
                if c < 4:
                    used("odz", c)
            pe.wait_ge(sem("od_in"), 16)
            pe.wait_ge(sem("conv_u"), TT)
            for t in range(TT):
                for d in range(2):
                    b.vacant("conv", (t, d))
                    o = bank("conv", (t, d))[:, :]
                    seam = t == 1 - d
                    mm(o, od_shift[:, 2 * d, :], od_zb[:, t, 512:1024], True, not seam, None if seam else fills("conv", (t, d)))
                    if seam:
                        mm(o, od_shift[:, 2 * d + 1, :], od_zb[:, 1 - t, 512:1024], False, True, fills("conv", (t, d)))
            pe.wait_ge(sem("lora_n"), 6)
            for j in range(2):
                b.vacant("ckvT", j)
                for t in range(4):
                    src = od_za[:, t, :] if t < TT else od_zc[:, t - TT, :]
                    turn(bank("ckvT", j)[:, t * P:(t + 1) * P], src[:, j * P:(j + 1) * P],
                         sig=fills("ckvT", j) if t == 3 else None)
            for j in range(3):
                b.vacant("cqT", j)
                for t in range(TT):
                    at = KV_LORA + KR + j * P
                    turn(bank("cqT", j)[:, t * P:(t + 1) * P], od_za[:, t, at:at + P],
                         sig=fills("cqT", j) if t == TT - 1 else None)
            uq = chunk("odz", 4)[:, KD * OD_TAIL:KD * OD_TAIL + 3 * UQ_W].rearrange("p (k n) -> p k n", k=3)
            b.drained("cqT", 2)
            for p in range(2):
                for t in range(TT):
                    b.vacant("uq", (p, t))
                    product("uq", (p, t), lambda k: od_cqt[:, k, t * P:(t + 1) * P],
                            lambda k: uq[:, k, p * 384:(p + 1) * 384], 3, 384)
            used("odz", 4)
            arrived("ukv", 0)
            ukv = chunk("ukv", 0)[:, 0:2 * D].rearrange("p (k n) -> p k n", k=2)
            for p in range(2):
                for t in range(4):
                    b.vacant("ukv", (p, t))
                    product("ukv", (p, t), lambda k: od_ckvt[:, k, t * P:(t + 1) * P],
                            lambda k: ukv[:, k, p * 512:(p + 1) * 512], 2, 512)
            used("ukv", 0)
            b.drained("ukv", (1, 3))
            pe.wait_ge(sem("od_kr"), 4)
            for h in range(OD_HEADS):
                b.vacant("odkT", h)
                for t in range(4):
                    turn(bank("odkT", h)[0:OD_DIM, t * P:(t + 1) * P], od_kf[:, t, h * OD_DIM:(h + 1) * OD_DIM],
                         sig=fills("odkT", h) if t == 3 else None)
            pe.wait_ge(sem("od_rope"), TT)
            for j in range(OD_HEADS // 2):
                b.vacant("odqT", j)
                for n in range(2):
                    for t in range(TT):
                        h = 2 * j + n
                        turn(bank("odqT", j)[0:OD_DIM, (n * TT + t) * P:(n * TT + t + 1) * P],
                             od_q[:, t, h * OD_DIM:(h + 1) * OD_DIM],
                             sig=fills("odqT", j) if n == 1 and t == TT - 1 else None)

            def od_score(u, o):
                h, t = OD_UNITS[u]
                if u == 0:
                    b.drained("odqT", OD_HEADS // 2 - 1)
                    b.drained("odkT", OD_HEADS - 1)
                mm(o[:, :], od_qt[0:OD_DIM, h, t * P:(t + 1) * P], od_kt[0:OD_DIM, h, :], True, True, fills("odatt", ("s", u)))

            attention("odatt", OD_UNITS, od_score, lambda u: 4,
                      lambda u, n: od_v[:, n, OD_UNITS[u][0] * 64:OD_UNITS[u][0] * 64 + 64], od_s, od_pt,
                      lambda u: b.drained("odatt", ("s", u)))
            b.drained("odatt", ("o", len(OD_UNITS) - 1))
            pe.wait_ge(sem("conv_done"), TT)
            cat_turns("cat1", od_cat, TT)
            mix(1, od_catt, TT)
            norm("n2_1", moe_xn, TT, sem("xn"), 14)
            experts(1)

            with pe.Fori(0, B2_LAYERS) as i:
                b.lap = i * LAP["b2"]
                state["chunk_lap"] = i * CHUNK_LAP["b2"]
                norm("nmix", region(B2_XN1, TT, D), TT, sem("b2_xn"), i * 4 + 2)
                for k in (6, 7):
                    b.drained("nmix", k)
                for c in range(9):
                    arrived("qkv", c)
                    w = chunk("qkv", c).rearrange("p (k n) -> p k n", k=KD)
                    for t in range(TT):
                        b.vacant("qkv", (c, t))
                        product("qkv", (c, t), lambda k: b2_ht[:, k, t * P:(t + 1) * P], lambda k: w[:, k, :], KD, 512)
                    used("qkv", c)
                for wh in range(2):
                    src = (b2_q, b2_k)[wh]
                    pe.wait_ge(sem("b2_rope"), i * 4 + 2 + 2 * wh)
                    b.drained("qkv", (2 + 3 * wh, 1))
                    for j in range(B2_PAIRS // 2):
                        b.vacant("qkT", (wh, j))
                        for n in range(2):
                            for t in range(TT):
                                turn(bank("qkT", (wh, j))[:, (n * TT + t) * P:(n * TT + t + 1) * P],
                                     src[:, t, (2 * j + n) * P:(2 * j + n + 1) * P],
                                     sig=fills("qkT", (wh, j)) if n == 1 and t == TT - 1 else None)
                for j in (B2_PAIRS // 2 - 2, B2_PAIRS // 2 - 1):
                    b.drained("qkT", (1, j))
                b.drained("qkv", (8, 1))
                for kind, u, n in AB_SCHED:
                    key = (kind, u, n)
                    unit = AB_UNITS[u]
                    t = unit[2]
                    per_bank = ab_keys_per_bank(*unit)
                    b.vacant("ab", key)
                    o = bank("ab", key)
                    if kind == "s":
                        blocks = per_bank[n]
                        heads = list(dict.fromkeys(hd for hd, _ in blocks))
                        for q, hd in enumerate(heads):
                            at = [m for m, x in enumerate(blocks) if x[0] == hd]
                            kts = [blocks[m][1] for m in at]
                            r = 64 * (hd % 2)
                            mm(o[:, at[0] * P:(at[-1] + 1) * P], b2_qt[r:r + 64, hd // 2, t * P:(t + 1) * P],
                               b2_kt[r:r + 64, hd // 2, kts[0] * P:(kts[-1] + 1) * P], True, True,
                               fills("ab", key) if q == len(heads) - 1 else None)
                    elif kind == "t":
                        if n == 0:
                            pe.wait_ge(sem("b2_p"), i * len(AB_UNITS) + u + 1)
                        for m in range(len(per_bank[n])):
                            turn(o[:, m * P:(m + 1) * P], b2_s[:, u % 3, (4 * n + m) * P:(4 * n + m + 1) * P],
                                 sig=fills("ab", key) if m == len(per_bank[n]) - 1 else None)
                    else:
                        for m in range(len(per_bank)):
                            b.drained("ab", ("t", u, m))
                        keys = ab_keys(*unit)
                        for m, (hd, kt) in enumerate(keys):
                            mm(o[:, 0:64], b2_pt[:, u % 2, m, :], b2_v[:, kt, hd * 64:(hd + 1) * 64], m == 0, m == len(keys) - 1,
                               fills("ab", key) if m == len(keys) - 1 else None)
                for kind, u, n in C_SCHED:
                    key = (kind, u, n)
                    hd = 18 + u
                    r = 64 * (hd % 2)
                    b.vacant("c", key)
                    o = bank("c", key)
                    buf = b2_s[:, u % 3, :]
                    if kind == "s":
                        mm(o[:, 0:SEQ], b2_kt[r:r + 64, hd // 2, 0:P], b2_qt[r:r + 64, hd // 2, :], True, True)
                        mm(o[:, SEQ:SEQ + P], b2_kt[r:r + 64, hd // 2, P:SEQ], b2_qt[r:r + 64, hd // 2, P:SEQ], True, True, fills("c", key))
                    elif kind == "c":
                        pe.wait_ge(sem("c_softplus"), i * len(C_UNITS) + u + 1)
                        mm(o[:, 0:SEQ], tri_ge, buf[:, 384:384 + SEQ], True, False)
                        mm(o[:, P:SEQ], ones, buf[:, 384 + SEQ:768], False, True)
                        mm(o[:, SEQ:SEQ + P], tri_ge, buf[:, 384 + SEQ:768], True, True, fills("c", key))
                    else:
                        if n == 0:
                            pe.wait_ge(sem("c_weights"), i * len(C_UNITS) + u + 1)
                        for kt in range(n + 1):
                            at = 384 + (n * P if kt == 0 else SEQ)
                            mm(o[:, 0:64], buf[:, at:at + P], b2_v[:, kt, hd * 64:(hd + 1) * 64], kt == 0, kt == n,
                               fills("c", key) if kt == n else None)
                b.drained("c", ("o", 5, 1))
                b.drained("ab", ("o", len(AB_UNITS) - 1, 0))
                for j in range(4):
                    b.vacant("ocat", j)
                    for n in range(2):
                        for t in range(TT):
                            k = 2 * j + n
                            turn(bank("ocat", j)[:, (n * TT + t) * P:(n * TT + t + 1) * P], b2_ocat[:, t, k * P:(k + 1) * P],
                                 sig=fills("ocat", j) if n == 1 and t == TT - 1 else None)
                for j in (2, 3):
                    b.drained("ocat", j)
                for c in range(2):
                    for n in range(4):
                        arrived("merge", 4 * c + n)
                    for t in range(TT):
                        for k in range(6):
                            b.vacant("merge", (c, t, k))
                            w = chunk("merge", 4 * c + (k + 1 if k < 3 else 0)).rearrange("p (k n) -> p k n", k=KD)
                            k0, k1 = (0, KD) if k < 3 else ((0, 2), (2, 5), (5, 8))[k - 3]
                            src = b2_ht if k < 3 else b2_ocatt
                            product("merge", (c, t, k), lambda m: src[:, k0 + m, t * P:(t + 1) * P],
                                    lambda m: w[:, k0 + m, :], k1 - k0, 512)
                    for n in range(4):
                        used("merge", 4 * c + n)
                    settle()
                pe.wait_ge(sem("b2_merged"), i * 4 + 4)
                for j in range(4):
                    b.vacant("mergeT", j)
                    for n in range(2):
                        for t in range(TT):
                            k = 2 * j + n
                            turn(bank("mergeT", j)[:, (n * TT + t) * P:(n * TT + t + 1) * P], b2_merged[:, t, k * P:(k + 1) * P],
                                 sig=fills("mergeT", j) if n == 1 and t == TT - 1 else None)
                for j in (2, 3):
                    b.drained("mergeT", j)
                for c in range(3):
                    arrived("wo", c)
                    width = WO_PIECES[c]
                    w = chunk("wo", c)[:, 0:KD * width].rearrange("p (k n) -> p k n", k=KD)
                    for t in range(TT):
                        b.vacant("wo", (c, t))
                        product("wo", (c, t), lambda k: b2_mergt[:, k, t * P:(t + 1) * P], lambda k: w[:, k, :], KD, width)
                    used("wo", c)
                norm("nmlp", region(B2_XN2, TT, D), TT, sem("b2_xn"), i * 4 + 4)
                for k in (6, 7):
                    b.drained("nmlp", k)

                def up(j):
                    arrived("up", j)
                    w = chunk("up", j).rearrange("p (k n) -> p k n", k=KD)
                    for n in range(2):
                        b.vacant("up", (j, n))
                        for m in range(2):
                            f = 2 * n + m
                            product("up", (j, n), lambda k: w[:, k, f * P:(f + 1) * P], lambda k: b2_ht[:, k, :], KD, SEQ,
                                    sig=m == 1, col=m * SEQ)
                    used("up", j)

                def down_ff(j):
                    pe.wait_ge(sem("b2_hidden"), i * (2 * N_FF) + 2 * j + 2)
                    arrived("down", j)
                    w = chunk("down", j).rearrange("p (k n) -> p k n", k=4)
                    for t in range(TT):
                        for h in range(2):
                            b.vacant("down", (j, t, h))
                            product("down", (j, t, h), lambda k: b2_hid[:, j % 2, k, t * P:(t + 1) * P],
                                    lambda k: w[:, k, h * 512:(h + 1) * 512], 4, 512)
                    used("down", j)

                for which, j in FF_ORDER:
                    (up if which == "up" else down_ff)(j)
                settle()

        @block.scalar
        def _(act):
            b = Banks(act)
            squares = [0]

            def copy(o, i, sig=None):
                ins = act.activation(o, i, ACT.Copy)
                if sig is not None:
                    ins.then_inc(sig, 1)

            def root(v, width, sig):
                act.activation(v, v, ACT.Sqrt, bias=eps, scale=1.0 / width).then_inc(sig, 1)

            def square_sums(x, junk, tiles):
                for t in range(tiles):
                    act.activation(junk[:, t, :], x[:, t, :], ACT.Square, accum_out=ss[:, t:t + 1]).then_inc(sem("sq"), 1)
                squares[0] += tiles
                act.wait_ge(sem("sq"), squares[0])
                root(ss[:, 0:tiles], D, sem("root"))

            def norm_out(name, dst, tiles, scale, shift):
                for k in range(0, KD, 2):
                    b.filled(name, k)
                    for s in range(tiles // TT):
                        cols = slice(s * SEQ, (s + 1) * SEQ)
                        ins = act.activation(dst[:, k, cols], bank(name, k)[:, cols], ACT.Identity,
                                             bias=shift[:, k, s:s + 1], scale=scale[:, k, s:s + 1])
                    ins.then_inc(frees(name, k), 1)

            def mod(layer):
                L = str(layer)
                streams = 2 - layer
                for n in range(4 * streams):
                    b.filled("modrow" + L, n)
                    copy(bc[:, n // 2, (n % 2) * 512:(n % 2 + 1) * 512], bank("modrow" + L, n)[:, :], frees("modrow" + L, n))
                b.drained("modcol" + L, 0)

            def cat_out(name, dst, width):
                for k in range(0, KD, 2):
                    b.filled(name, k)
                    copy(dst[:, k, :], bank(name, k)[:, 0:width], frees(name, k))

            def probs_out(name, u, pt, nk):
                b.filled(name, ("t", u))
                if u >= 2:
                    b.filled(name, ("o", u - 2))
                copy(pt[:, u % 2, 0:nk, :], bank(name, ("t", u))[:, 0:nk * P].rearrange("p (n q) -> p n q", n=nk),
                     frees(name, ("t", u)))

            def experts(layer):
                L = str(layer)
                moe = "moe" + L
                streams = 2 - layer
                tiles = TT * streams
                rows = streams * CAP
                parts = P // rows
                width, yw = NCOL // parts, D // parts
                b.drained("logit" + L, 0)
                act.activation(lge[:, 0:tiles * N_EXP], lg[:, 0:tiles * N_EXP], ACT.Exp).then_inc(sem("lgt_exp"), 1)
                for g in range(GROUPS):
                    b.filled("gateT" + L, g)
                    copy(moe_gt[:, g, 0:tiles * P], bank("gateT" + L, g)[:, 0:tiles * P], frees("gateT" + L, g))
                with act.Fori(0, GROUPS) as i:
                    b.lap = i * LAP[moe]
                    for e in range(PER_GROUP):
                        for c in range(2):
                            b.filled(moe, (e, f"a{c}"))
                            act.activation(moe_sil[:, c, 0:width], bank(moe, (e, f"a{c}"))[:, 0:width], ACT.Silu)\
                                .then_inc(frees(moe, (e, f"a{c}")), 1)
                        for c in range(2):
                            b.filled(moe, (e, f"t{c}"))
                            copy(moe_gtr[:, e % 2, c, 0:width], bank(moe, (e, f"t{c}"))[:, 0:width], frees(moe, (e, f"t{c}")))
                        b.filled(moe, (e, "y"))
                        for n in range(parts):
                            for s in range(streams):
                                last = n == parts - 1 and s == streams - 1
                                at = n * rows + s * CAP
                                copy(moe_yst[e * CAP:(e + 1) * CAP, s, n * yw:(n + 1) * yw],
                                     bank(moe, (e, "y"))[at:at + CAP, 0:yw], frees(moe, (e, "y")) if last else None)
                b.lap = 0

            act.wait_ge(sem("eps"), 1)
            act.wait_ge(sem("c_in"), 16)
            act.activation(sc[:, :, :], sc[:, :, :], ACT.Silu).then_inc(sem("silu_c"), 1)

            mod(0)
            act.wait_ge(sem("x_in"), 16)
            square_sums(X, xn4, 4)
            norm_out("n1_0", ht4, 4, A1, B1)
            for c in range(4):
                for t in range(4):
                    b.filled("evz", (c, t))
                    w = 512 if c < 3 else 256
                    act.activation(ev_z[:, t, c * 512:c * 512 + w], bank("evz", (c, t))[:, 0:w],
                                   ACT.Gelu_apprx_tanh if c < 2 else ACT.Copy).then_inc(frees("evz", (c, t)), 1)
                if c == 2:
                    act.wait_ge(sem("sgu_var"), 4)
                    root(root4, 1, sem("sgu_root"))
            for j in range(1 + EV_PAIRS):
                b.filled("evqk", j)
                copy(ev_kt[:, :] if j == 0 else ev_qt[:, j - 1, :], bank("evqk", j)[:, :], frees("evqk", j))
            for kind, u in pipeline(len(EV_UNITS), ATT_LAGS):
                h, t = EV_UNITS[u]
                n = 512 if t < TT else SEQ
                if kind == "s":
                    act.wait_ge(sem("ev_nm"), u + 1)
                    act.activation(ev_s[:, u % 3, 0:n], ev_s[:, u % 3, 0:n], ACT.Exp, bias=nm[:, u:u + 1], scale=EV_SCALE,
                                   accum_out=l[:, u:u + 1]).then_inc(sem("ev_p"), 1)
                    act.activation(ls[:, u:u + 1], ev_sink[:, h:h + 1], ACT.Exp, bias=nm[:, u:u + 1]).then_inc(sem("ev_ls"), 1)
                elif kind == "t":
                    probs_out("evatt", u, ev_pt, n // P)
            cat_out("cat0", ev_catt, 512)
            act.wait_ge(sem("x_mix"), 8)
            square_sums(X, moe_xn, 4)
            norm_out("n2_0", moe_ht, 4, A2, B2)
            experts(0)

            mod(1)
            act.wait_ge(sem("x_moe"), GROUPS)
            square_sums(X, xn4, 4)
            norm_out("n1_1", ht4, 4, A1, B1)
            for c in range(5):
                for t in range(4 if c == 0 else 2):
                    b.filled("odz", (c, t))
                    o = bank("odz", (c, t))
                    done = frees("odz", (c, t))
                    if c == 0 and t >= TT:
                        copy(od_zc[:, t - TT, :], o[:, 0:KV_LORA + KR], done)
                    elif c == 0:
                        copy(od_za[:, t, 0:512], o[:, :], done)
                    elif c == 1:
                        copy(od_za[:, t, 512:ZA_W], o[:, 0:ZA_W - 512])
                        copy(od_zb[:, t, 0:1024 - ZA_W], o[:, ZA_W - 512:512], done)
                    else:
                        at = c * 512 - ZA_W
                        w = 512 if c < 4 else OD_TAIL
                        copy(od_zb[:, t, at:at + w], o[:, 0:w], done)
            for t in range(4):
                src = od_za[:, t, 0:KV_LORA] if t < TT else od_zc[:, t - TT, 0:KV_LORA]
                act.activation(od_s[:, 2, 0:KV_LORA], src, ACT.Square, accum_out=ss2[:, t:t + 1]).then_inc(sem("lora_sq"), 1)
                act.wait_ge(sem("lora_sq"), t + 1)
            for t in range(TT):
                act.activation(od_s[:, 2, 0:Q_LORA], od_za[:, t, KV_LORA + KR:], ACT.Square,
                               accum_out=ss2[:, 4 + t:5 + t]).then_inc(sem("lora_sq"), 1)
                act.wait_ge(sem("lora_sq"), 5 + t)
            root(ss2[:, 0:4], KV_LORA, sem("lora_root"))
            root(ss2[:, 4:6], Q_LORA, sem("lora_root"))
            act.wait_ge(sem("conv_done"), TT)
            for p in range(2):
                for t in range(TT):
                    b.filled("uq", (p, t))
                    copy(od_q[:, t, p * 384:(p + 1) * 384], bank("uq", (p, t))[:, 0:384], frees("uq", (p, t)))
            for p in range(2):
                for t in range(4):
                    b.filled("ukv", (p, t))
                    o = bank("ukv", (p, t))[:, :].rearrange("p (h d) -> p h d", h=4)
                    kf = od_kf[:, t, :].rearrange("p (h d) -> p h d", h=OD_HEADS)
                    copy(kf[:, 4 * p:4 * p + 4, 0:64], o[:, :, 0:64])
                    copy(od_v[:, t, p * 256:(p + 1) * 256].rearrange("p (h d) -> p h d", h=4), o[:, :, 64:128], frees("ukv", (p, t)))
            for h in range(OD_HEADS):
                b.filled("odkT", h)
                copy(od_kt[0:OD_DIM, h, :], bank("odkT", h)[0:OD_DIM, :], frees("odkT", h))
            for kind, u in pipeline(len(OD_UNITS), ATT_LAGS):
                if kind == "s":
                    act.wait_ge(sem("od_nm"), u + 1)
                    if u >= 3:
                        b.filled("odatt", ("t", u - 3))
                    act.activation(od_s[:, u % 3, :], bank("odatt", ("s", u))[:, :], ACT.Exp, bias=nm[:, u:u + 1], scale=OD_SCALE,
                                   accum_out=l[:, u:u + 1]).then_inc(frees("odatt", ("s", u)), 1)
                elif kind == "t":
                    probs_out("odatt", u, od_pt, 4)
            cat_out("cat1", od_catt, SEQ)
            act.wait_ge(sem("x_mix"), 8 + 4)
            square_sums(X, moe_xn, TT)
            norm_out("n2_1", moe_ht, TT, A2, B2)
            experts(1)

            act.wait_ge(sem("x_moe"), 2 * GROUPS)
            square_sums(X, xn4, TT)
            act.wait_ge(sem("x_final"), TT)

            with act.Fori(0, B2_LAYERS) as i:
                b.lap = i * LAP["b2"]

                def squares2(junk, at):
                    for t in range(TT):
                        act.activation(junk[:, t, :], X[:, t, :], ACT.Square, accum_out=ss[:, t:t + 1]).then_inc(sem("b2_sq"), 1)
                    act.wait_ge(sem("b2_sq"), i * 4 + at + 2)
                    root(ss[:, 0:TT], D, sem("b2_root"))

                def gain_out(name, off):
                    for k in range(0, KD, 2):
                        b.filled(name, k)
                        act.activation(b2_ht[:, k, :], bank(name, k)[:, 0:SEQ], ACT.Identity,
                                       scale=layer_gain[:, off + k:off + k + 1]).then_inc(frees(name, k), 1)

                b.drained("down", (N_FF - 1, 1, 1), LAP["b2"])
                squares2(region(B2_XN1, TT, D), 0)
                act.wait_ge(sem("b2_gain"), i * 2 + 2)
                gain_out("nmix", 0)
                for c in range(9):
                    for t in range(TT):
                        b.filled("qkv", (c, t))
                        dst = (b2_q, b2_k, b2_v)[c // 3]
                        copy(dst[:, t, c % 3 * 512:(c % 3 + 1) * 512], bank("qkv", (c, t))[:, :], frees("qkv", (c, t)))
                for wh in range(2):
                    for j in range(B2_PAIRS // 2):
                        b.filled("qkT", (wh, j))
                        copy((b2_qt, b2_kt)[wh][:, 2 * j:2 * j + 2, :],
                             bank("qkT", (wh, j))[:, :].rearrange("p (n q) -> p n q", n=2), frees("qkT", (wh, j)))
                for kind, u, n in AB_SCHED:
                    per_bank = ab_keys_per_bank(*AB_UNITS[u])
                    width = P * len(ab_keys(*AB_UNITS[u]))
                    if kind == "s" and n == len(per_bank) - 1:
                        act.wait_ge(sem("b2_nm"), i * len(AB_UNITS) + u + 1)
                        act.activation(b2_s[:, u % 3, 0:width], b2_s[:, u % 3, 0:width], ACT.Exp, bias=nm[:, u:u + 1],
                                       scale=B2_SCALE, accum_out=l[:, u:u + 1]).then_inc(sem("b2_p"), 1)
                    elif kind == "t":
                        b.filled("ab", (kind, u, n))
                        if u >= 2:
                            b.filled("ab", ("o", u - 2, 0))
                        m = len(per_bank[n])
                        copy(b2_pt[:, u % 2, 4 * n:4 * n + m, :],
                             bank("ab", (kind, u, n))[:, 0:m * P].rearrange("p (n q) -> p n q", n=m), frees("ab", (kind, u, n)))
                for kind, u, n in C_SCHED:
                    buf = b2_s[:, u % 3, :]
                    k = i * len(C_UNITS) + u + 1
                    if kind == "s":
                        act.wait_ge(sem("c_abs"), k)
                        act.activation(buf[:, 384:768], buf[:, 384:768], ACT.Exp).then_inc(sem("c_exp"), 1)
                        act.wait_ge(sem("c_exp"), k)
                        act.activation(buf[:, 384:768], buf[:, 384:768], ACT.Ln, bias=1.0).then_inc(sem("c_ln"), 1)
                    elif kind == "c":
                        b.drained("c", (kind, u, 0))
                        act.activation(buf[:, 384:768], buf[:, 0:384], ACT.Exp).then_inc(sem("c_weights"), 1)
                    else:
                        b.filled("c", (kind, u, n))
                        copy(b2_ocat[:, n, 640 + u * 64:640 + (u + 1) * 64], bank("c", (kind, u, n))[:, 0:64], frees("c", (kind, u, n)))
                for j in (0, 2):
                    b.filled("ocat", j)
                    copy(b2_ocatt[:, 2 * j:2 * j + 2, :], bank("ocat", j)[:, :].rearrange("p (n q) -> p n q", n=2), frees("ocat", j))
                before = None
                for c in range(2):
                    for t in range(TT):
                        for k in range(3):
                            if before is not None:
                                b.drained("merge", (*before, 3 + k))
                            b.filled("merge", (c, t, k))
                            act.activation(b2_sig[:, k, :], bank("merge", (c, t, k))[:, :], ACT.Sigmoid).then_inc(frees("merge", (c, t, k)), 1)
                        before = (c, t)
                for j in (0, 2):
                    b.filled("mergeT", j)
                    copy(b2_mergt[:, 2 * j:2 * j + 2, :], bank("mergeT", j)[:, :].rearrange("p (n q) -> p n q", n=2), frees("mergeT", j))
                b.drained("wo", (2, 1))
                squares2(region(B2_XN2, TT, D), 2)
                gain_out("nmlp", KD)
                for which, j in FF_ORDER:
                    if which == "up":
                        for n in range(2):
                            b.filled("up", (j, n))
                            if j >= 2:
                                b.filled("down", (j - 2, 1, 1))
                            act.activation(b2_hid[:, j % 2, 2 * n:2 * n + 2, :],
                                           bank("up", (j, n))[:, :].rearrange("p (m q) -> p m q", m=2), ACT.Relu)\
                                .then_inc(frees("up", (j, n)), 1)
            b.lap = LAP["b2"] * (B2_LAYERS - 1)
            b.drained("down", (N_FF - 1, 1, 1))
            square_sums(X, xn4, TT)

        @block.vector
        def _(dve):
            b = Banks(dve)
            steps = Steps(dve, sem("dve_step"))
            dve.memset(eps, EPS).then_inc(sem("eps"), 1)

            def norm(name, x, xn, tiles, n_root, dst, scale, shift):
                dve.wait_ge(sem("root"), n_root)
                steps.do(dve.reciprocal(rstd[:, 0:tiles], ss[:, 0:tiles]))
                for t in range(tiles):
                    dve.tensor_scalar(xn[:, t, :], x[:, t, :], rstd[:, t:t + 1], None, ALU.mult).then_inc(sem("xn"), 1)
                for k in range(1, KD, 2):
                    b.filled(name, k)
                    for s in range(tiles // TT):
                        cols = slice(s * SEQ, (s + 1) * SEQ)
                        ins = dve.tensor_scalar(dst[:, k, cols], bank(name, k)[:, cols], scale[:, k, s:s + 1],
                                                shift[:, k, s:s + 1], ALU.mult, ALU.add)
                    ins.then_inc(frees(name, k), 1)

            def mod(layer):
                L = str(layer)
                dve.wait_ge(sem("modb_in"), 16 * (layer + 1))
                for c in range(12):
                    b.filled("mod" + L, c)
                    cols = slice(c * 512, (c + 1) * 512)
                    dve.tensor_tensor(mrow[:, cols], bank("mod" + L, c)[0:2, :], modb_sb[:, cols], ALU.add)\
                        .then_inc(frees("mod" + L, c), 1)
                if layer == 0:
                    dve.wait_ge(sem("small_in"), 16)
                b.filled("modcol" + L, 0)
                cols = bank("modcol" + L, 0)[:, 0:64].rearrange("p (v k s) -> p v k s", v=4, k=KD)
                for n, (a, sh, off) in enumerate(((A1, B1, G_N1), (A2, B2, G_N2))):
                    g = gain(off + layer * KD).unsqueeze(2).to_broadcast([P, KD, 2])
                    ins = dve.scalar_tensor_tensor(out=a, in0=cols[:, 2 * n], scalar=1.0, in1=g, op0=ALU.add, op1=ALU.mult)
                    if n == 0:
                        ins.then_inc(sem("mod_done"), 1)
                    ins = dve.tensor_copy(sh, cols[:, 2 * n + 1])
                ins.then_inc(frees("modcol" + L, 0), 1)
                b.drained("modcol" + L, 0)

            def rope(x1, x2, cos, sin, tmp, sig):
                steps.add(dve.tensor_tensor(tmp[0], x1, cos, ALU.mult))
                steps.add(dve.tensor_tensor(tmp[1], x2, sin, ALU.mult))
                steps.add(dve.tensor_tensor(tmp[2], x2, cos, ALU.mult))
                steps.do(dve.tensor_tensor(tmp[3], x1, sin, ALU.mult))
                steps.add(dve.tensor_tensor(x1, tmp[0], tmp[1], ALU.subtract))
                dve.tensor_tensor(x2, tmp[2], tmp[3], ALU.add).then_inc(sig, 1)

            def heads_tmp(off, n, w):
                return [region(off + m * n * w, n, w) for m in range(4)]

            def over_heads(c, n, w):
                return c.unsqueeze(1).to_broadcast([P, n, w])

            def cat_out(name, dst, width):
                for k in range(1, KD, 2):
                    b.filled(name, k)
                    dve.tensor_copy(dst[:, k, :], bank(name, k)[:, 0:width]).then_inc(frees(name, k), 1)

            def add_gated(name, key, gate, x, tmp, width, sig=None):
                b.filled(name, key)
                dve.tensor_tensor(tmp[:, 0:width], bank(name, key)[:, 0:width], gate, ALU.mult).then_inc(frees(name, key), 1)
                b.drained(name, key)
                ins = dve.tensor_tensor(x, x, tmp[:, 0:width], ALU.add)
                if sig is None:
                    steps.do(ins)
                else:
                    ins.then_inc(sig, 1)

            def mix(layer):
                L = str(layer)
                streams = 2 - layer
                for c in range(2):
                    for t in range(TT * streams):
                        cols = slice(c * 512, (c + 1) * 512)
                        n = c * TT * streams + t
                        add_gated("mix" + L, (c, t), bc[:, t // TT, cols], X[:, t, cols], mix_tmp[:, n % 2], 512, sem("x_mix"))

            def experts(layer):
                L = str(layer)
                moe = "moe" + L
                streams = 2 - layer
                tiles = TT * streams
                rows = streams * CAP
                parts = P // rows
                width = NCOL // parts
                ne = streams * N_EXP
                b.filled("logit" + L, 0)
                groups = lambda v: v[:, 0:tiles * N_EXP].rearrange("p (g e) -> p g e", g=tiles)
                each = lambda v: v[:, 0:tiles].unsqueeze(2).to_broadcast([P, tiles, N_EXP])
                logits = groups(bank("logit" + L, 0))
                steps.do(dve.tensor_reduce(lgs[:, 0:tiles], logits, AX.X, ALU.max))
                dve.tensor_tensor(groups(lg), logits, each(lgs), ALU.subtract).then_inc(frees("logit" + L, 0), 1)
                dve.wait_ge(sem("lgt_exp"), layer + 1)
                steps.do(dve.tensor_reduce(lgs[:, 0:tiles], groups(lge), AX.X, ALU.add))
                steps.do(dve.reciprocal(lgs[:, 0:tiles], lgs[:, 0:tiles]))
                dve.tensor_tensor(groups(moe_aff), groups(lge), each(lgs), ALU.mult).then_inc(sem("aff"), 1)
                b.filled("affT" + L, 0)
                work = moe_work[0:ne, :]
                top = mx2[0:ne, 0:8]
                dve.tensor_copy(work, bank("affT" + L, 0)[0:ne, 0:SEQ]).then_inc(frees("affT" + L, 0), 1)
                b.drained("affT" + L, 0)
                for _ in range(CAP // 8):
                    steps.do(dve.max(top, work))
                    steps.do(dve.match_replace(work, top, work, -1.0))
                dve.tensor_scalar(moe_chosen[0:ne, :], work, 0.0, None, ALU.is_lt).then_inc(sem("chosen"), 1)
                b.filled("selT" + L, 0)
                dve.tensor_copy(mkT[:, 0:2 * ne], bank("selT" + L, 0)[:, 0:2 * ne]).then_inc(frees("selT" + L, 0), 1)
                b.filled("rank" + L, 0)
                b.drained("selT" + L, 0)
                dve.tensor_tensor(pos[:, 0:2 * ne], bank("rank" + L, 0)[:, 0:2 * ne], mkT[:, 0:2 * ne], ALU.mult)\
                    .then_inc(frees("rank" + L, 0), 1)
                b.drained("rank" + L, 0)
                dve.wait_ge(sem("aff"), layer + 1)
                slots = iota.unsqueeze(1).to_broadcast([P, N_EXP, CAP])
                for tok in range(tiles):
                    s, t = tok // TT, tok % TT
                    at = t * ne + s * N_EXP
                    spread = lambda v: v[:, at:at + N_EXP].unsqueeze(2).to_broadcast([P, N_EXP, CAP])
                    hot = moe_oh[:, tok, :].rearrange("p (e c) -> p e c", e=N_EXP)
                    gated = moe_gw[:, tok, :].rearrange("p (e c) -> p e c", e=N_EXP)
                    steps.do(dve.tensor_tensor(hot, spread(pos), slots, ALU.is_equal))
                    dve.tensor_tensor(gated, hot, spread(moe_aff), ALU.mult).then_inc(sem("gated"), 1)
                b.drained("gateT" + L, GROUPS - 1)
                scale = (modc[:, 2].rearrange("p k s -> p (k s)") if streams == 2 else modc[:, 2, :, 0])
                shift = (modc[:, 3].rearrange("p k s -> p (k s)") if streams == 2 else modc[:, 3, :, 0])
                nks = KD * streams
                with steps.loop(GROUPS, MOE_STEPS) as i:
                    b.lap = i * LAP[moe]
                    dve.tensor_copy(moe_gtst[:, 0:tiles * P], moe_gt[:, bass.ds(i, 1), 0:tiles * P].rearrange("p a n -> p (a n)"))\
                        .then_inc(sem("gates_staged" + L), 1)
                    for e in range(PER_GROUP):
                        b.filled(moe, (e, "x"))
                        view = lambda v: v[:, 0:nks * CAP].rearrange("p (k c) -> p k c", k=nks)
                        wide = lambda v: v.unsqueeze(2).to_broadcast([P, nks, CAP])
                        dve.tensor_tensor(view(moe_xtmp), view(bank(moe, (e, "x"))), wide(scale), ALU.mult)\
                            .then_inc(frees(moe, (e, "x")), 1)
                        b.drained(moe, (e, "x"))
                        dve.tensor_tensor(view(moe_xst[:, e % 2, :]), view(moe_xtmp), wide(shift), ALU.add)\
                            .then_inc(sem("xst" + L), 1)
                        for c in range(2):
                            b.filled(moe, (e, f"b{c}"))
                            b.drained(moe, (e, f"a{c}"))
                            dve.tensor_tensor(moe_g[:, c, 0:width], moe_sil[:, c, 0:width], bank(moe, (e, f"b{c}"))[:, 0:width], ALU.mult)\
                                .then_inc(frees(moe, (e, f"b{c}")), 1)
                    pieces = 8 // tiles
                    w = D // pieces
                    for n in range(8):
                        t, c = n // pieces, n % pieces
                        cols = slice(c * w, (c + 1) * w)
                        add_gated("comb" + L, n, bc[:, streams + t // TT, cols], X[:, t, cols], moe_tmp[:, n % 2], w,
                                  sem("x_moe") if n == 7 else None)
                b.lap = 0
                dve.wait_ge(sem("x_moe"), GROUPS * (layer + 1))

            def weights_out(name, u, dst):
                b.filled(name, u)
                steps.do(dve.reciprocal(rl[:, u[1]:u[1] + 1], l[:, u[1]:u[1] + 1]))
                dve.tensor_scalar(dst, bank(name, u)[:, 0:64], rl[:, u[1]:u[1] + 1], None, ALU.mult).then_inc(frees(name, u), 1)

            mod(0)
            norm("n1_0", X, xn4, 4, 1, ht4, A1, B1)
            dve.wait_ge(sem("ev_in"), 16)
            steps.add(dve.tensor_scalar(ev_nsink, ev_sink[:, :], -1.0, None, ALU.mult))
            for t in range(4):
                b.filled("evz", (1, t))
                b.drained("evz", (1, t))
                v = ev_z[:, t, 512:1024]
                var = mv[:, 2 * t + 1:2 * t + 2]
                steps.do(dve.bn_stats(bn[:, 6 * t:6 * t + 6], v))
                steps.do(dve.bn_aggr(mv[:, 2 * t:2 * t + 2], bn[:, 6 * t:6 * t + 6]))
                dve.tensor_copy(root4[:, t:t + 1], var).then_inc(sem("sgu_var"), 1)
            dve.wait_ge(sem("sgu_root"), 1)
            steps.do(dve.reciprocal(root4, root4))
            for t in range(4):
                v = ev_z[:, t, 512:1024]
                steps.do(dve.tensor_scalar(v, v, mv[:, 2 * t:2 * t + 1], root4[:, t:t + 1], ALU.subtract, ALU.mult))
                dve.tensor_tensor(v, v, ev_sgug[:, :], ALU.mult).then_inc(sem("sgu_v"), 1)
            b.drained("evz", (3, 1))
            for t in range(TT):
                x = ev_z[:, t, 1152:1792].rearrange("p (h d) -> p h d", d=64)
                rope(x[:, :, 0:32], x[:, :, 32:64], over_heads(ev_cos[:, t, :], 10, 32), over_heads(ev_sin[:, t, :], 10, 32),
                     heads_tmp(EV_S, 10, 32), sem("ev_rope"))
                dve.wait_ge(sem("ev_rope"), t + 1)
            for t in range(4):
                b.filled("sgu", t)
                for g in range(4):
                    cols = slice(g * P, (g + 1) * P)
                    ins = dve.scalar_tensor_tensor(out=ev_cat[:, t, 512 + g * P:512 + (g + 1) * P], in0=bank("sgu", t)[:, cols],
                                                   scalar=ev_sgub[:, g:g + 1], in1=ev_z[:, t, cols], op0=ALU.add, op1=ALU.mult)
                ins.then_inc(frees("sgu", t), 1)
            for kind, u in pipeline(len(EV_UNITS), ATT_LAGS):
                h, t = EV_UNITS[u]
                first = 0 if t < TT else SEQ
                n = 512 - first
                if kind == "s":
                    b.filled("evatt", ("s", u))
                    if u >= 3:
                        b.filled("evatt", ("t", u - 3))
                    dve.tensor_tensor_reduce(ev_s[:, u % 3, 0:n], bank("evatt", ("s", u))[:, 0:n], ev_win[:, t % TT, first:512], 1.0, -3e38,
                                             ALU.add, ALU.max, mx[:, u:u + 1]).then_inc(frees("evatt", ("s", u)), 1)
                    b.drained("evatt", ("s", u))
                    dve.tensor_scalar(nm[:, u:u + 1], mx[:, u:u + 1], -EV_SCALE, ev_nsink[:, h:h + 1], ALU.mult, ALU.min)\
                        .then_inc(sem("ev_nm"), 1)
                elif kind == "o":
                    dve.wait_ge(sem("ev_ls"), u + 1)
                    steps.do(dve.tensor_tensor(l[:, u:u + 1], l[:, u:u + 1], ls[:, u:u + 1], ALU.add))
                    weights_out("evatt", ("o", u), ev_cat[:, t, h * 64:(h + 1) * 64])
            cat_out("cat0", ev_catt, 512)
            mix(0)
            norm("n2_0", X, moe_xn, 4, 2, moe_ht, A2, B2)
            experts(0)

            mod(1)
            norm("n1_1", X, xn4, 4, 3, ht4, A1, B1)
            b.drained("odz", (4, 1))
            for t in range(TT):
                gb, gc, hh = (od_zb[:, t, n * 512:(n + 1) * 512] for n in range(3))
                dve.tensor_tensor(gc, gc, hh, ALU.mult).then_inc(sem("conv_u"), 1)
            dve.wait_ge(sem("lora_root"), 2)
            steps.do(dve.reciprocal(rstd2[:, :], ss2[:, :]))
            for n in range(6):
                part = od_za[:, n, 0:KV_LORA] if n < TT else od_zc[:, n - TT, 0:KV_LORA] if n < 4 else od_za[:, n - 4, KV_LORA + KR:]
                dve.tensor_scalar(part, part, rstd2[:, n:n + 1], None, ALU.mult).then_inc(sem("lora_n"), 1)
            dve.wait_ge(sem("od_in2"), 16)
            for t in range(TT):
                x = od_za[:, t, KV_LORA:KV_LORA + KR].unsqueeze(1)
                rope(x[:, :, 0:16], x[:, :, 16:32], over_heads(od_cos[:, t, :], 1, 16), over_heads(od_sin[:, t, :], 1, 16),
                     heads_tmp(OD_S + 1024, 1, 16), sem("od_krope"))
                dve.wait_ge(sem("od_krope"), t + 1)
            dve.wait_ge(sem("od_in"), 16)
            for t in range(TT):
                gb, u = od_zb[:, t, 0:512], od_zb[:, t, 512:1024]
                acc, tmp = od_s[:, 0, :], od_s[:, 1, :]
                b.filled("conv", (t, 0))
                dve.tensor_tensor(acc, bank("conv", (t, 0))[:, :], od_convw[:, 0, :], ALU.mult).then_inc(frees("conv", (t, 0)), 1)
                steps.do(dve.tensor_tensor(tmp, u, od_convw[:, 1, :], ALU.mult))
                b.drained("conv", (t, 0))
                steps.do(dve.tensor_tensor(acc, acc, tmp, ALU.add))
                b.filled("conv", (t, 1))
                dve.tensor_tensor(tmp, bank("conv", (t, 1))[:, :], od_convw[:, 2, :], ALU.mult).then_inc(frees("conv", (t, 1)), 1)
                b.drained("conv", (t, 1))
                steps.do(dve.tensor_tensor(acc, acc, tmp, ALU.add))
                dve.tensor_tensor(od_cat[:, t, 512:1024], acc, gb, ALU.mult).then_inc(sem("conv_done"), 1)
                dve.wait_ge(sem("conv_done"), t + 1)
            for j in range(2):
                b.filled("ckvT", j)
                dve.tensor_scalar(od_ckvt[:, j, :], bank("ckvT", j)[:, :], gain(G_KV + j, 1), None, ALU.mult).then_inc(frees("ckvT", j), 1)
            for j in range(3):
                b.filled("cqT", j)
                dve.tensor_scalar(od_cqt[:, j, :], bank("cqT", j)[:, 0:SEQ], gain(G_Q + j, 1), None, ALU.mult).then_inc(frees("cqT", j), 1)
            for t in range(4):
                src = od_za[:, t, KV_LORA:KV_LORA + KR] if t < TT else od_zc[:, t - TT, KV_LORA:]
                kf = od_kf[:, t, :].rearrange("p (h d) -> p h d", h=OD_HEADS)
                dve.tensor_copy(kf[:, :, 64:96], over_heads(src, OD_HEADS, KR)).then_inc(sem("od_kr"), 1)
            b.drained("uq", (1, 1))
            for t in range(TT):
                x = od_q[:, t, :].rearrange("p (h d) -> p h d", h=OD_HEADS)
                rope(x[:, :, 64:80], x[:, :, 80:96], over_heads(od_cos[:, t, :], 8, 16), over_heads(od_sin[:, t, :], 8, 16),
                     heads_tmp(OD_S, 8, 16), sem("od_rope"))
                dve.wait_ge(sem("od_rope"), t + 1)
            for j in range(OD_HEADS // 2):
                b.filled("odqT", j)
                dve.tensor_copy(od_qt[0:OD_DIM, 2 * j:2 * j + 2, :],
                                bank("odqT", j)[0:OD_DIM, :].rearrange("p (n q) -> p n q", n=2)).then_inc(frees("odqT", j), 1)
            for kind, u in pipeline(len(OD_UNITS), ATT_LAGS):
                h, t = OD_UNITS[u]
                if kind == "s":
                    b.filled("odatt", ("s", u))
                    steps.do(dve.tensor_reduce(mx[:, u:u + 1], bank("odatt", ("s", u))[:, :], AX.X, ALU.max))
                    dve.tensor_scalar(nm[:, u:u + 1], mx[:, u:u + 1], -OD_SCALE, None, ALU.mult).then_inc(sem("od_nm"), 1)
                elif kind == "o":
                    weights_out("odatt", ("o", u), od_cat[:, t, h * 64:(h + 1) * 64])
            cat_out("cat1", od_catt, SEQ)
            mix(1)
            norm("n2_1", X, moe_xn, TT, 4, moe_ht, A2, B2)
            experts(1)

            def last_norm(n_root, n_gain, dst, sig):
                dve.wait_ge(sem("fg_in"), n_gain)
                dve.wait_ge(sem("root"), n_root)
                steps.do(dve.reciprocal(rstd[:, 0:TT], ss[:, 0:TT]))
                for t in range(TT):
                    dve.scalar_tensor_tensor(out=dst[:, t, :], in0=X[:, t, :], scalar=rstd[:, t:t + 1], in1=final_g[:, :],
                                             op0=ALU.mult, op1=ALU.mult).then_inc(sig, 1)

            last_norm(5, 16, X, sem("x_final"))
            dve.wait_ge(sem("x_final"), TT)
            dve.wait_ge(sem("b2_in"), 16)
            dve.wait_ge(sem("b2_in2"), 16)

            with steps.loop(B2_LAYERS, B2_STEPS) as i:
                b.lap = i * LAP["b2"]
                for n, off in enumerate((G_MIX, G_MLP)):
                    dve.tensor_copy(layer_gain[:, n * KD:(n + 1) * KD], small[:, bass.ds(i * KD + off, KD)]).then_inc(sem("b2_gain"), 1)

                def norm2(name, xn, at, off):
                    dve.wait_ge(sem("b2_root"), i * 2 + at // 2 + 1)
                    steps.do(dve.reciprocal(rstd[:, 0:TT], ss[:, 0:TT]))
                    for t in range(TT):
                        dve.tensor_scalar(xn[:, t, :], X[:, t, :], rstd[:, t:t + 1], None, ALU.mult).then_inc(sem("b2_xn"), 1)
                    dve.wait_ge(sem("b2_gain"), i * 2 + 2)
                    for k in range(1, KD, 2):
                        b.filled(name, k)
                        dve.tensor_scalar(b2_ht[:, k, :], bank(name, k)[:, 0:SEQ], layer_gain[:, off + k:off + k + 1], None, ALU.mult)\
                            .then_inc(frees(name, k), 1)

                norm2("nmix", region(B2_XN1, TT, D), 0, 0)
                for wh in range(2):
                    b.drained("qkv", (2 + 3 * wh, 1))
                    for t in range(TT):
                        x = (b2_q, b2_k)[wh][:, t, :].rearrange("p (h d) -> p h d", d=64)[:, 0:B2_ROT, :]
                        rope(x[:, :, 0:8], x[:, :, 8:16], over_heads(b2_cos[:, t, :], B2_ROT, 8),
                             over_heads(b2_sin[:, t, :], B2_ROT, 8), heads_tmp(B2_S, B2_ROT, 8), sem("b2_rope"))
                        dve.wait_ge(sem("b2_rope"), i * 4 + wh * 2 + t + 1)
                for kind, u, n in AB_SCHED:
                    unit = AB_UNITS[u]
                    which, h, t = unit
                    per_bank = ab_keys_per_bank(*unit)
                    if kind == "s":
                        mask = (b2_amask if which == "A" else b2_bmask)[t]
                        w = P * len(per_bank[n])
                        b.filled("ab", (kind, u, n))
                        if u >= 3 and n == 0:
                            b.filled("ab", ("t", u - 3, len(ab_keys_per_bank(*AB_UNITS[u - 3])) - 1))
                        dve.memset(idle[:, u + 20 * n:u + 20 * n + 1], 0.0)
                        top = mx[:, u:u + 1] if len(per_bank) == 1 else mx2[:, 2 * u + n:2 * u + n + 1]
                        dve.tensor_tensor_reduce(b2_s[:, u % 3, n * 512:n * 512 + w], bank("ab", (kind, u, n))[:, 0:w],
                                                 mask[:, n * 512:n * 512 + w], 1.0, -3e38, ALU.add, ALU.max, top)\
                            .then_inc(frees("ab", (kind, u, n)), 1)
                        if n == len(per_bank) - 1:
                            b.drained("ab", (kind, u, n))
                            if n:
                                steps.do(dve.tensor_reduce(mx[:, u:u + 1], mx2[:, 2 * u:2 * u + 2], AX.X, ALU.max))
                            dve.tensor_scalar(nm[:, u:u + 1], mx[:, u:u + 1], -B2_SCALE, None, ALU.mult).then_inc(sem("b2_nm"), 1)
                    elif kind == "o":
                        at = h * 64 + (0 if which == "A" else 256)
                        weights_out("ab", (kind, u, n), b2_ocat[:, t, at:at + 64])
                for kind, u, n in C_SCHED:
                    buf = b2_s[:, u % 3, :]
                    zm, sp = buf[:, 0:384], buf[:, 384:768]
                    if kind == "s":
                        b.filled("c", (kind, u, n))
                        if u >= 3:
                            b.filled("c", ("o", u - 3, 1))
                        dve.scalar_tensor_tensor(out=zm, in0=bank("c", (kind, u, n))[:, 0:384], scalar=B2_SCALE, in1=b2_cmask[:, :],
                                                 op0=ALU.mult, op1=ALU.add).then_inc(frees("c", (kind, u, n)), 1)
                        b.drained("c", (kind, u, n))
                        dve.scalar_tensor_tensor(out=sp, in0=zm, scalar=-1.0, in1=zm, op0=ALU.mult, op1=ALU.min).then_inc(sem("c_abs"), 1)
                        dve.wait_ge(sem("c_ln"), i * len(C_UNITS) + u + 1)
                        dve.scalar_tensor_tensor(out=sp, in0=zm, scalar=0.0, in1=sp, op0=ALU.max, op1=ALU.add)\
                            .then_inc(sem("c_softplus"), 1)
                    elif kind == "c":
                        b.filled("c", (kind, u, n))
                        dve.tensor_tensor(zm, zm, bank("c", (kind, u, n))[:, 0:384], ALU.subtract).then_inc(frees("c", (kind, u, n)), 1)
                for j in (1, 3):
                    b.filled("ocat", j)
                    dve.tensor_copy(b2_ocatt[:, 2 * j:2 * j + 2, :], bank("ocat", j)[:, :].rearrange("p (n q) -> p n q", n=2))\
                        .then_inc(frees("ocat", j), 1)
                for c in range(2):
                    for t in range(TT):
                        m = b2_merged[:, t, c * 512:(c + 1) * 512]
                        for k in range(3):
                            b.filled("merge", (c, t, 3 + k))
                            b.drained("merge", (c, t, k))
                            dst = m if k == 0 else b2_prod[:, k - 1, :]
                            dve.tensor_tensor(dst, bank("merge", (c, t, 3 + k))[:, :], b2_sig[:, k, :], ALU.mult)\
                                .then_inc(frees("merge", (c, t, 3 + k)), 1)
                            b.drained("merge", (c, t, 3 + k))
                            if k == 1:
                                steps.do(dve.tensor_tensor(m, m, b2_prod[:, 0, :], ALU.add))
                            elif k == 2:
                                dve.tensor_tensor(m, m, b2_prod[:, 1, :], ALU.add).then_inc(sem("b2_merged"), 1)
                for j in (1, 3):
                    b.filled("mergeT", j)
                    dve.tensor_copy(b2_mergt[:, 2 * j:2 * j + 2, :], bank("mergeT", j)[:, :].rearrange("p (n q) -> p n q", n=2))\
                        .then_inc(frees("mergeT", j), 1)
                for c in range(3):
                    at, w = sum(WO_PIECES[:c]), WO_PIECES[c]
                    for t in range(TT):
                        b.filled("wo", (c, t))
                        x = X[:, t, at:at + w]
                        dve.tensor_tensor(x, x, bank("wo", (c, t))[:, 0:w], ALU.add).then_inc(frees("wo", (c, t)), 1)
                norm2("nmlp", region(B2_XN2, TT, D), 2, KD)
                for which, j in FF_ORDER:
                    if which == "up":
                        for n in range(2):
                            b.drained("up", (j, n))
                            hid = b2_hid[:, j % 2, 2 * n:2 * n + 2, :]
                            dve.tensor_tensor(hid, hid, hid, ALU.mult).then_inc(sem("b2_hidden"), 1)
                    else:
                        for t in range(TT):
                            for h in range(2):
                                b.filled("down", (j, t, h))
                                if j:
                                    b.drained("down", (j - 1, t, h))
                                x = X[:, t, h * 512:(h + 1) * 512]
                                dve.tensor_tensor(x, x, bank("down", (j, t, h))[:, :], ALU.add).then_inc(frees("down", (j, t, h)), 1)
            b.lap = LAP["b2"] * (B2_LAYERS - 1)
            b.drained("down", (N_FF - 1, 1, 1))
            last_norm(6, 32, xn4, sem("result"))


def _k_major(w):
    k, n = w.shape
    return w.reshape(k // P, P, n).transpose(1, 0, 2).reshape(P, -1)

def _lay_out(a):
    f = np.float32
    stream = np.zeros((N_CHUNKS, P, CHUNK), f)

    def put(at, *parts):
        off = 0
        for part in parts:
            stream[at, :, off:off + part.shape[1]] = part
            off += part.shape[1]

    def columns(name, w, width=NCOL, first=0):
        for n in range(w.shape[1] // width):
            put(CHUNK_AT[name, first + n], _k_major(w[:, n * width:(n + 1) * width]))

    heads = [h + 4 * s for h in range(4) for s in range(2)]
    in0 = a["ev_w_in"][0]
    kv_cols, q_cols, g_cols = in0[:, :256], in0[:, 256:768].reshape(D, 8, 64)[:, heads].reshape(D, 512), in0[:, 768:]
    in0 = np.concatenate([g_cols, kv_cols[:, 128:], kv_cols[:, :128], q_cols], 1)
    out0 = a["ev_w_out"][0]
    out0 = np.concatenate([out0[:512].reshape(8, 64, D)[heads].reshape(512, D), out0[512:]], 0)
    in1 = a["od_w_in"][0]
    for layer in range(2):
        columns(f"mod{layer}", a["mod_w"][layer])
        at = CHUNK_AT[f"moe{layer}", 0]
        for e in range(N_EXP):
            w1, w3, w2 = (a[n][layer, e] for n in ("exp_w1", "exp_w3", "exp_w2"))
            for c in range(2):
                put(at + 6 * e + 2 * c, _k_major(w1[:, c * 512:(c + 1) * 512]))
                put(at + 6 * e + 2 * c + 1, _k_major(w3[:, c * 512:(c + 1) * 512]))
                put(at + 6 * e + 4 + c, _k_major(w2[c * 512:(c + 1) * 512]))
    columns("evz", in0[:, :1536])
    put(CHUNK_AT["evz", 3], _k_major(in0[:, 1536:]))
    columns("mix0", out0)
    columns("odz", in1[:, :4 * NCOL])
    put(CHUNK_AT["odz", 4], _k_major(in1[:, 4 * NCOL:]), _k_major(a["od_w_uq"][0]))
    put(CHUNK_AT["ukv", 0], _k_major(a["od_w_ukv"][0]))
    columns("mix1", a["od_w_out"][0])
    per = CHUNK_LAP["b2"] * SLOTS
    for i in range(B2_LAYERS):
        w_in = a["w_in_2"][i]
        w_out = np.concatenate([a["w_out_a_2"][i], a["w_out_b_2"][i], a["w_out_c_2"][i]], 0)
        for c in range(9):
            put(CHUNK_AT["qkv", c] + i * per, _k_major(w_in[:, c * NCOL:(c + 1) * NCOL]))
        for c in range(2):
            cols = slice(c * NCOL, (c + 1) * NCOL)
            put(CHUNK_AT["merge", 4 * c] + i * per, _k_major(w_out[:, cols]))
            for g in range(3):
                put(CHUNK_AT["merge", 4 * c + 1 + g] + i * per, _k_major(w_in[:, 3 * B2_W + g * D:3 * B2_W + (g + 1) * D][:, cols]))
        at = 0
        for c, w in enumerate(WO_PIECES):
            put(CHUNK_AT["wo", c] + i * per, _k_major(a["w_o_2"][i][:, at:at + w]))
            at += w
        for j in range(N_FF):
            put(CHUNK_AT["up", j] + i * per, _k_major(a["w_up_2"][i][:, j * 512:(j + 1) * 512]))
            put(CHUNK_AT["down", j] + i * per, _k_major(a["w_down_2"][i][j * 512:(j + 1) * 512]))

    const = shape_constants()
    cols = lambda v: v.reshape(-1, P).T
    rows = lambda v: np.broadcast_to(v.reshape(1, -1), (P, v.size))
    small = [cols(a[n][i]) for n in ("norm1_g", "norm2_g", "norm_mix_2", "norm_mlp_2") for i in range(2)]
    small += [cols(a["od_q_norm_g"][0]), cols(a["od_kv_norm_g"][0])]
    small += [_k_major(a["router_w"][i]) for i in range(2)]
    return {
        "stream": stream,
        "base": const["base"],
        "small": np.concatenate(small, 1),
        "ccols": np.stack([cols(a["c"][0]), cols(a["c_ctx"])], 2),
        "x_in": np.concatenate([a["x"][0], a["ctx"][0]], 0).reshape(2 * TT, P, D).transpose(1, 0, 2),
        "modb": np.stack([a["mod_b"], a["mod_b"]], 1),
        "ev_pack": np.concatenate([const["win"], a["ev_sgu_w"][0].transpose(2, 0, 1).reshape(P, -1), rows(a["ev_sgu_norm_g"][0]),
                                   a["ev_sgu_b"][0].T, rows(a["ev_sink"][0][heads]), const["ev_rope"]], 1),
        "od_rope": const["od_rope"],
        "od_pack": np.concatenate([const["shift"], rows(a["od_conv_w"][0])], 1),
        "b2_masks": const["b2_masks"],
        "b2_rope": const["b2_rope"],
        "gains": np.stack([rows(a["final_g"]), rows(a["norm_final_2"])], 0),
    }

def kernel(**inputs):
    import concourse.bacc as bacc
    from concourse.bass_utils import run_bass_kernel_spmd

    a = {k: np.asarray(v) for k, v in inputs.items()}
    arrays = {"in_" + k: np.ascontiguousarray(v) for k, v in _lay_out(a).items()}
    nc = bacc.Bacc("TRN2", target_bir_lowering=False, num_devices=1)
    args = [nc.dram_tensor(n, v.shape, F32, kind="ExternalInput").ap() for n, v in arrays.items()]
    args.append(nc.dram_tensor("out", (1, SEQ, D), F32, kind="ExternalOutput").ap())
    program(nc, *args)
    r = run_bass_kernel_spmd(nc, [arrays], core_ids=[0])
    return r.results[0]["out"]
```

```python
from contextlib import ExitStack, contextmanager

import numpy as np

import concourse.bass as bass
from concourse import mybir

F32 = mybir.dt.float32
F32R = mybir.dt.float32r
ALU = mybir.AluOpType
ACT = mybir.ActivationFunctionType
AX = mybir.AxisListType

P = 128
D = 1024
SEQ = 256
TT = SEQ // P
KD = D // P
EPS = 1e-6
NEG = -1e30
CHUNK = 4096
SLOTS = 6
BANKS = 8
NCOL = CHUNK // KD
GRID_W = 64

N_EXP = 16
CAP = 2 * SEQ // N_EXP
PER_GROUP = P // CAP
GROUPS = N_EXP // PER_GROUP

EV_PAIRS = 4
EV_SCALE = 64 ** -0.5
WINDOW = 128
OD_HEADS = 8
OD_DIM = 96
OD_SCALE = OD_DIM ** -0.5
Q_LORA, KV_LORA, KR = 384, 256, 32
ZA_W = KV_LORA + KR + Q_LORA
ZB_W = 3 * 512
OD_TAIL = ZA_W + ZB_W - 4 * NCOL
UQ_W = OD_HEADS * OD_DIM

B2_HEADS = 24
B2_ROT = 18
B2_PAIRS = B2_HEADS // 2
B2_W = B2_HEADS * 64
B2_SCALE = 64 ** -0.5
B2_LAYERS = 2
WO_PIECES = (384, 384, 256)
N_FF = 8
MOE_STEPS, B2_STEPS = 7, 52


def steps_of(n, stages):
    last = max(lag for _, lag in stages)
    return [[(name, step - lag) for name, lag in stages if 0 <= step - lag < n] for step in range(n + last)]

def pipeline(n, stages):
    return [x for step in steps_of(n, stages) for x in step]

ATT_LAGS = [("s", 0), ("t", 3), ("o", 4)]
ATT_LAGS_ACT = [("t", 3), ("s", 0), ("o", 4)]
S_BUFS = 4
EV_UNITS = [(h, t) for t in range(2 * TT) for h in range(2 * EV_PAIRS)]
ODZ_ORDER = (1, 2, 3, 4, 0)
OD_UNITS = [(h, t) for t in range(TT) for h in range(OD_HEADS)]
AB_UNITS = [("A", h, t) for h in range(4) for t in range(TT)] + [("B", h, t) for h in range(6) for t in range(TT)]
C_UNITS = list(range(6))

def ab_keys(kind, h, t):
    heads = [4 * g + h for g in range(3)] if kind == "A" else [12 + h]
    return [(hd, kt) for hd in heads for kt in range(t + 1)]

def ab_keys_per_bank(kind, h, t):
    keys = ab_keys(kind, h, t)
    return [keys[i:i + 4] for i in range(0, len(keys), 4)]

MOD_EARLY = 4
EV_MOD = [("m", 0, c) for c in range(MOD_EARLY, 12)] + [("f", 0, n) for n in range(5)] + [("m", 1, c) for c in range(12)]

def ev_schedule(lags):
    left = list(EV_MOD)
    for i, step in enumerate(steps_of(len(EV_UNITS), lags)):
        yield from (("a", *x) for x in step)
        n = 5 if left and left[0][0] == "f" else 1 if i != 9 and i != 10 else 0
        yield from left[:n]
        del left[:n]
    assert not left

C_LAGS = [("s", 0), ("c", 2), ("o", 4)]
C_LAGS_ACT = [("c", 2), ("s", 0), ("o", 4)]
C_LAGS_DVE = [("p", 1), ("s", 0), ("c", 2)]
C_BUFS = 5

def b2_schedule(ab_lags, c_lags):
    c_steps = steps_of(len(C_UNITS), c_lags)
    for i, step in enumerate(steps_of(len(AB_UNITS), ab_lags)):
        for name, u in step:
            for n in range(1 if name == "o" else len(ab_keys_per_bank(*AB_UNITS[u]))):
                yield "ab", name, u, n
        if i >= 2 and i % 2 == 0 and (i - 2) // 2 < len(c_steps):
            for name, u in c_steps[(i - 2) // 2]:
                for n in range(TT if name == "o" else 1):
                    yield "c", name, u, n

FF_ORDER = pipeline(N_FF, [("up", 0), ("down", 1)])

TICKET = {}
LAP = {}

def _tickets():
    n = 0

    def stage(name, keys):
        nonlocal n
        for k in (range(keys) if isinstance(keys, int) else keys):
            TICKET[name, k] = n
            n += 1

    def repeated(name, first, times):
        nonlocal n
        per = n - first
        assert per % BANKS == 0, (name, per)
        LAP[name] = per // BANKS
        n = first + per * times

    def norm(name):
        stage(name, KD)

    for layer in range(2):
        streams = 2 if layer == 0 else 1
        L = str(layer)
        if layer == 0:
            stage("mod0", range(MOD_EARLY))
            stage("modcol0", [0])
        else:
            stage("modrow1", 4)
        norm("n1_" + L)
        if layer == 0:
            stage("evz", [(c, t) for c in range(4) for t in range(4)])
            stage("sgu", 4)
            stage("evqk", 1 + EV_PAIRS)
            for what, *x in ev_schedule(ATT_LAGS):
                if what == "a":
                    stage("evatt", [tuple(x)])
                elif what == "m":
                    stage(f"mod{x[0]}", [x[1]])
                elif x[1] == 0:
                    stage("modcol0", [1])
                else:
                    stage("modrow0", [x[1] - 1])
            stage("modcol1", 2)
        else:
            for c in ODZ_ORDER:
                for t in range(4 if c == 0 else 2):
                    if (c, t) == (0, TT):
                        stage("conv", [(tile, d) for tile in range(TT) for d in range(2)])
                    stage("odz", [(c, t)])
            stage("ckvT", 2)
            stage("cqT", 3)
            stage("uq", [(p, t) for p in range(2) for t in range(TT)])
            stage("ukv", [(p, t) for p in range(2) for t in range(4)])
            stage("odkT", OD_HEADS)
            stage("odqT", OD_HEADS // 2)
            stage("odatt", pipeline(len(OD_UNITS), ATT_LAGS))
        stage("cat" + L, KD)
        stage("mix" + L, [(c, t) for t in range(2 * streams) for c in range(2)])
        norm("n2_" + L)
        stage("logit" + L, 1)
        stage("logitT" + L, 1)
        stage("affT" + L, 1)
        if layer == 0:
            stage("modrow5", 4)
        stage("selT" + L, 1)
        stage("rank" + L, 1)
        first = n
        stage("gather" + L, KD)
        for e in range(PER_GROUP):
            stage("moe" + L, [(e, k) for k in ("gate", "a0", "b0", "a1", "t0", "b1", "y", "t1")])
        stage("comb" + L, 8)
        repeated("moe" + L, first, GROUPS)
    first = n
    norm("nmix")
    stage("qkv", [(c, t) for c in range(9) for t in range(TT)])
    stage("qkT", [(w, j) for w in range(2) for j in range(B2_PAIRS // 2)])
    for which, *key in b2_schedule(ATT_LAGS, C_LAGS):
        stage(which, [tuple(key)])
    stage("ocat", 4)
    stage("merge", [(c, what, k, t) for c in range(2) for what in ("gate", "branch") for k in range(3) for t in range(TT)])
    stage("mergeT", 4)
    stage("wo", [(c, t) for c in range(3) for t in range(TT)])
    norm("nmlp")
    for which, j in FF_ORDER:
        stage(which, [(j, 0), (j, 1)] if which == "up" else [(j, t, h) for t in range(TT) for h in range(2)])
    repeated("b2", first, B2_LAYERS)

_tickets()

CHUNK_AT = {}
CHUNK_LAP = {}

def _chunks():
    n = 0

    def put(name, count):
        nonlocal n
        for k in range(count):
            CHUNK_AT[name, k] = n
            n += 1

    def repeated(name, first, times):
        nonlocal n
        per = n - first
        assert per % SLOTS == 0, (name, per)
        CHUNK_LAP[name] = per // SLOTS
        n = first + per * times

    for c in range(MOD_EARLY):
        CHUNK_AT["mod0", c] = c
    n = MOD_EARLY
    put("evz", 4)
    for what, layer, c in EV_MOD:
        if what == "m":
            CHUNK_AT[f"mod{layer}", c] = n
            n += 1
    put("mix0", 2)
    first = n
    put("moe0", 6 * PER_GROUP)
    repeated("moe0", first, GROUPS)
    for c in ODZ_ORDER:
        CHUNK_AT["odz", c] = n
        n += 1
    put("ukv", 1)
    put("mix1", 2)
    first = n
    put("moe1", 6 * PER_GROUP)
    repeated("moe1", first, GROUPS)
    first = n
    put("qkv", 9)
    put("merge", 8)
    put("wo", 3)
    for which, j in FF_ORDER:
        CHUNK_AT[which, j] = n
        n += 1
    repeated("b2", first, B2_LAYERS)
    return n

N_CHUNKS = _chunks()

PIECE = 1024
PIECES_PER_CHUNK = CHUNK // PIECE
PIECE_BUFS = 3
ATT_CHUNKS = [("qkv", c) for c in range(9)]
MLP_CHUNKS = [("merge", c) for c in range(8)] + [("wo", c) for c in range(3)] + FF_ORDER
BRANCHES = ((0, 2), (2, 5), (5, 8))

def fills_last(name, k, m):
    last = m == PIECES_PER_CHUNK - 1
    if name == "merge" and k % 4 == 3:
        return ("merge", (k // 4, "branch", 0 if m == 0 else 2, 1)) if m == 0 or last else None
    if name == "merge":
        return ("merge", (k // 4, "gate", k % 4, 1)) if last else None
    if name == "up":
        return ("up", (k, m // 2)) if m % 2 else None
    if name == "down":
        return ("down", (k, 1, 1)) if last else None
    return (name, (k, 1)) if last else None

PIECES = [(name, k, m) for name, k in ATT_CHUNKS + MLP_CHUNKS for m in range(PIECES_PER_CHUNK)]
PIECE_AT = {piece: n for n, piece in enumerate(PIECES)}
assert len(PIECES) % PIECE_BUFS == 0
USED_UP_TO = [sum(fills_last(*x) is None for x in PIECES[:n + 1]) for n in range(len(PIECES))]

def split_order(chunks):
    before = None
    for name, k in chunks:
        for m in range(PIECES_PER_CHUNK):
            yield "piece", name, k, m
            if m == 1 and before:
                yield "out", *before, None
            elif m == 2:
                yield ("late", *before, None) if before else ("begin", None, None, None)
        before = (name, k)
    yield "out", *before, None
    yield "late", *before, None


def _rope(n_freq_total, pos_pairs):
    c = np.cos(pos_pairs).astype(np.float32).reshape(TT, P, -1).transpose(1, 0, 2)
    s = np.sin(pos_pairs).astype(np.float32).reshape(TT, P, -1).transpose(1, 0, 2)
    return np.concatenate([c.reshape(P, -1), s.reshape(P, -1)], 1)

def _axial(rot):
    rows = SEQ // GRID_W
    row = np.repeat(np.arange(rows, dtype=np.float32), GRID_W)
    col = np.tile(np.arange(GRID_W, dtype=np.float32), rows)
    n = rot // 4
    inv = np.power(np.float32(10000.0), -np.arange(n, dtype=np.float32) / np.float32(n)).astype(np.float32)
    return _rope(2 * n, np.concatenate([row[:, None] * inv, col[:, None] * inv], 1).astype(np.float32))

def _partial():
    inv = np.exp(np.float32(-np.log(500000.0)) * np.arange(0, 16, 2, dtype=np.float32) / np.float32(16))
    return _rope(8, (np.arange(SEQ, dtype=np.float32)[:, None] * inv.astype(np.float32)[None, :]).astype(np.float32))

def shape_constants():
    p = np.arange(P)[:, None]
    q = np.arange(P)[None, :]
    f = np.float32
    base = np.concatenate([(p == q).astype(f), (p <= q).astype(f), (p >= q).astype(f), np.ones((P, P), f),
                           np.broadcast_to(np.arange(1, CAP + 1, dtype=f), (P, CAP))], 1)
    keys = np.arange(SEQ)[None, :]
    win = []
    for t in range(TT):
        qp = t * P + p
        win += [np.where(np.abs(keys - qp) <= WINDOW, 0, NEG).astype(f), np.zeros((P, SEQ), f)]
    shift = np.concatenate([(p == q - 1), (p == P - 1) & (q == 0), (p == q + 1), (p == 0) & (q == P - 1)], 1).astype(f)
    amask = []
    for t in range(TT):
        kk = np.arange((t + 1) * P)[None, :]
        d = t * P + p - kk
        for span, dil in ((128, 1), (512, 4), (2048, 16)):
            amask.append(np.where((d >= 0) & (d <= span) & (d % dil == 0), 0, NEG).astype(f))
    bmask = np.where(keys <= P + p, 0, NEG).astype(f)
    cmask = np.concatenate([np.where(p < keys, 0, NEG), np.where(p < q, 0, NEG)], 1).astype(f)
    return {"base": base, "win": np.concatenate(win, 1), "ev_rope": _axial(64), "od_rope": _axial(32),
            "shift": shift, "b2_masks": np.concatenate(amask + [bmask, cmask], 1), "b2_rope": _partial()}

IDENT, TRI_LE, TRI_GE, ONES, IOTA = 0, 128, 256, 384, 512
BASE_W = 544
G_N1, G_N2, G_MIX, G_MLP, G_Q, G_KV = 0, 16, 32, 48, 64, 67
ROUTER = 69
SMALL_W = ROUTER + 2 * KD * N_EXP + N_EXP
ARENA = 22668

HT, XN, BC, MROW, MROW5 = 0, 4096, 11264, 13312, 14848
EV_CAT, EV_Z, EV_CATT = 0, 4096, 4096
EV_QT, EV_KT, EV_S, EV_PT, EV_PACK = 15360, 17408, 17920, 19456, 20480
EV_WIN, EV_SGUW, EV_SGUG, EV_SGUB, EV_SINK, EV_ROPE = 20480, 21504, 22016, 22528, 22532, 22540
EV_PACK_W = 2188
MOE_XN, MOE_HT, MOE_YST, MOE_OH, MOE_AFF = 0, 4096, 4096, 8192, 10240
MOE_GW, MOE_XST, MOE_G, MOE_GTR, MOE_GTST = 8704, 17408, 19456, 20480, 21504
MOE_W = 22016
MOE_TMP, MIX_TMP = 6144, 19456
OD_HT, OD_KT, OD_ZA, OD_ZC, OD_CQT, OD_CKVT, OD_ZB, OD_KF, OD_ROPE = 0, 0, 4096, 5440, 6016, 6784, 7808, 7808, 10880
OD_QT, OD_S, OD_PT, OD_SHIFT, OD_CONVW, OD_Q, OD_CAT = 15360, 17408, 18944, 19968, 20480, 20480, 13312
OD_CATT = 4096
B2_Q, B2_K, B2_V, B2_QT, B2_KT = 0, 3072, 6144, 9216, 12288
B2_S, B2_PT, B2_MASK, B2_ROPE, B2_RTMP, B2_CBUF = 15360, 18432, 19968, 21760, 21792, 2048
B2_XN1, B2_XN2, B2_OCAT, B2_SIG, B2_MERGED, B2_SQ = 0, 7168, 0, 0, 7168, 0
B2_AH, B2_AL, B2_OH, B2_OL, B2_WH, B2_WL = 9216, 11264, 3072, 5120, 13824, 16896
FINAL_G = (15360, 1024)

def program(nc, stream, base_c, small_c, ccols, x_in, modb, ev_pack, od_rope, od_pack, b2_masks, b2_rope, gains, out):
    with ExitStack() as ctx:
        def sb(name, shape):
            return ctx.enter_context(nc.sbuf_tensor(name, shape, F32))

        sems = {}

        def sem(name):
            if name not in sems:
                sems[name] = ctx.enter_context(nc.semaphore(name))
            return sems[name]

        ring = sb("ring", [P, SLOTS, CHUNK])
        X = sb("x", [P, 2 * TT, D])
        base = sb("base", [P, BASE_W])
        small = sb("small", [P, SMALL_W])
        sc = sb("silu_c", [P, KD, 32])
        modc = sb("mod_columns", [P, 2, 4, KD, 2])
        A1, B1, A2, B2 = ([modc[:, layer, n] for layer in range(2)] for n in range(4))
        stat = sb("statistics", [P, 584])
        arena_at = nc.sbuf_base
        arena = sb("arena", [P, ARENA])
        psum = [ctx.enter_context(nc.psum_tensor(f"bank{b}", [P, 512], F32)) for b in range(BANKS)]

        slot_loaded = [sem(f"slot_loaded{s}") for s in range(SLOTS)]
        slot_free = [sem(f"slot_free{s}") for s in range(SLOTS)]
        filled_sem = [sem(f"filled{b}") for b in range(BANKS)]
        drained_sem = [sem(f"drained{b}") for b in range(BANKS)]

        def region(off, *shape):
            n = int(np.prod(shape))
            v = arena[:, off:off + n]
            if len(shape) == 2:
                return v.rearrange("p (a b) -> p a b", a=shape[0])
            if len(shape) == 3:
                return v.rearrange("p (a b c) -> p a b c", a=shape[0], b=shape[1])
            return v

        def parts(name, off, *shape):
            return nc.alloc_sbuf_tensor_at(name, [P, *shape], F32R, offset=arena_at + 4 * off)

        ident = base[:, IDENT:IDENT + P]
        tri_le = base[:, TRI_LE:TRI_LE + P]
        tri_ge = base[:, TRI_GE:TRI_GE + P]
        ones = base[:, ONES:ONES + P]
        iota = base[:, IOTA:IOTA + CAP]

        def gain(off, n=KD):
            return small[:, off:off + n]

        def bank(name, key):
            return psum[TICKET[name, key] % BANKS]

        def chunk(name, k):
            return ring[:, CHUNK_AT[name, k] % SLOTS, :]

        def piece_of(name, k, m):
            n = PIECE_AT[name, k, m] % PIECE_BUFS
            if name == "up":
                src, kts, w = chunk(name, k).rearrange("p (k n) -> p k n", k=KD)[:, :, m * P:(m + 1) * P], KD, P
            else:
                kts = 1 if name == "down" else 2
                w = WO_PIECES[k] if name == "wo" else PIECE // kts
                src = chunk(name, k)[:, m * kts * w:(m + 1) * kts * w].rearrange("p (k n) -> p k n", k=kts)
            return src, *(v[:, n, 0:kts * w].rearrange("p (k n) -> p k n", k=kts) for v in (w_hi, w_lo))

        class Banks:

            def __init__(self, eng):
                self.eng, self.lap = eng, 0

            def filled(self, name, key):
                n = TICKET[name, key]
                self.eng.wait_ge(filled_sem[n % BANKS], self.lap + (n // BANKS + 1))

            def drained(self, name, key, back=0):
                n = TICKET[name, key]
                self.eng.wait_ge(drained_sem[n % BANKS], self.lap + (n // BANKS + 1 - back))

            def vacant(self, name, key):
                n = TICKET[name, key]
                if n >= BANKS:
                    self.eng.wait_ge(drained_sem[n % BANKS], self.lap + n // BANKS)

        def frees(name, key):
            return drained_sem[TICKET[name, key] % BANKS]

        def fills(name, key):
            return filled_sem[TICKET[name, key] % BANKS]

        class Steps:

            def __init__(self, eng, semaphore):
                self.eng, self.sem, self.base, self.n = eng, semaphore, 0, 0

            def add(self, ins):
                ins.then_inc(self.sem, 1)
                self.n += 1

            def sync(self):
                self.eng.wait_ge(self.sem, self.base + self.n)

            def do(self, ins):
                self.add(ins)
                self.sync()

            @contextmanager
            def loop(self, times, per):
                before = self.base + self.n
                with self.eng.Fori(0, times) as i:
                    self.base, self.n = i * per + before, 0
                    yield i
                    assert self.n == per, (self.n, per)
                self.base, self.n = before + times * per, 0

        mrow = region(MROW, 12 * P)
        mrow5 = region(MROW5, 2 * P)
        bc = region(BC, 2, D)
        xn4 = region(XN, 4, D)
        ht4 = region(HT, KD, 512)
        ev_z = region(EV_Z, 4, 1792)
        ev_qt = region(EV_QT, EV_PAIRS, 512)
        ev_kt = region(EV_KT, 512)
        ev_s = [region(at, 512) for at in (EV_S, EV_S + 512, EV_S + 1024, EV_SGUW)]
        ev_pt = region(EV_PT, 2, 4, P)
        ev_win = region(EV_WIN, TT, 512)
        ev_sguw = region(EV_SGUW, 4, P)
        ev_sgug = region(EV_SGUG, 512)
        ev_sgub = region(EV_SGUB, 4)
        ev_sink = region(EV_SINK, 8)

        ev_cos = region(EV_ROPE, TT, 32)
        ev_sin = region(EV_ROPE + TT * 32, TT, 32)
        ev_cat = region(EV_CAT, 4, D)
        ev_catt = region(EV_CATT, KD, 512)
        od_za = region(OD_ZA, TT, ZA_W)
        od_zb = region(OD_ZB, TT, ZB_W)
        od_zc = region(OD_ZC, TT, KV_LORA + KR)
        od_cqt = region(OD_CQT, 3, SEQ)
        od_ckvt = region(OD_CKVT, 2, 512)
        od_kf = region(OD_KF, 4, OD_HEADS * OD_DIM)
        od_v = X[:, TT:2 * TT, :].rearrange("p a b -> p (a b)").rearrange("p (t c) -> p t c", t=4)
        od_q = region(OD_Q, TT, UQ_W)
        od_kt = region(OD_KT, OD_HEADS, 512)
        od_qt = region(OD_QT, OD_HEADS, SEQ)
        od_s = [region(at, 512) for at in (OD_S, OD_S + 512, OD_S + 1024, OD_SHIFT)]
        od_pt = region(OD_PT, 2, 4, P)
        od_shift = region(OD_SHIFT, 4, P)
        od_convw = region(OD_CONVW, 3, 512)
        od_cos = region(OD_ROPE, TT, 16)
        od_sin = region(OD_ROPE + TT * 16, TT, 16)
        od_cat = region(OD_CAT, TT, D)
        od_catt = region(OD_CATT, KD, SEQ)
        moe_ht = region(MOE_HT, KD, 512)
        moe_xn = region(MOE_XN, 4, D)
        moe_aff = region(MOE_AFF, 64)
        moe_work = region(MOE_W, 256)
        moe_chosen = region(MOE_W + 256, 256)
        moe_oh = region(MOE_OH, 4, P)
        moe_gw = region(MOE_GW, 4, P)
        moe_gtst = region(MOE_GTST, 512)
        moe_xst = region(MOE_XST, 2 * KD * P)

        def moe_x(streams):
            n = KD * PER_GROUP * streams * CAP
            return moe_xst[:, 0:n].rearrange("p (k e s c) -> p k e s c", k=KD, e=PER_GROUP, s=streams)

        moe_sil = region(MOE_G, 2, 256)
        moe_g = region(MOE_G + 512, 2, 256)
        moe_gtr = region(MOE_GTR, 2, 2, 256)
        moe_yst = region(MOE_YST, 2, D)
        moe_tmp = region(MOE_TMP, 2, 512)
        mix_tmp = region(MIX_TMP, 2, 512)
        b2_q = region(B2_Q, TT, B2_W)
        b2_k = region(B2_K, TT, B2_W)
        b2_v = region(B2_V, TT, B2_W)
        b2_qt = region(B2_QT, B2_PAIRS, SEQ)
        b2_kt = region(B2_KT, B2_PAIRS, SEQ)
        b2_ht = X[:, TT:2 * TT, :].rearrange("p a b -> p (a b)").rearrange("p (k c) -> p k c", k=KD)
        b2_s = region(B2_S, S_BUFS, 768)
        b2_c = region(B2_CBUF, C_BUFS, 768)
        b2_pt = region(B2_PT, 2, 6, P)
        b2_cos = region(B2_ROPE, TT, 8)
        b2_sin = region(B2_ROPE + TT * 8, TT, 8)
        b2_ocat = region(B2_OCAT, TT, D)
        b2_merged = region(B2_MERGED, TT, D)
        b2_sig = region(B2_SIG, 3, TT, 512)
        b2_sq = region(B2_SQ, 2, 512)
        a_hi, a_lo = parts("tokens_high", B2_AH, KD, SEQ), parts("tokens_low", B2_AL, KD, SEQ)
        o_hi, o_lo = parts("hidden_high", B2_OH, KD, SEQ), parts("hidden_low", B2_OL, KD, SEQ)
        w_hi, w_lo = parts("weights_high", B2_WH, PIECE_BUFS, PIECE), parts("weights_low", B2_WL, PIECE_BUFS, PIECE)
        b2_amask = [region(B2_MASK, 384), region(B2_MASK + 384, 768)]
        b2_bmask = [region(B2_MASK, P), region(B2_MASK + 1152, 256)]
        b2_cmask = region(B2_MASK + 1408, 384)
        final_g = [region(at, D) for at in FINAL_G]

        mx, nm, ls, l, rl = (stat[:, 34 * n:34 * n + 34] for n in range(5))
        ss, rstd = stat[:, 170:178], stat[:, 178:186]
        bn, mv = stat[:, 186:210], stat[:, 210:218]
        lg, lge, lgs = stat[:, 218:282], stat[:, 282:346], stat[:, 346:354]
        pos = stat[:, 354:418]
        mkT = stat[:, 418:482]
        mx2 = stat[:, 482:522]
        ev_nsink = mx2[:, 0:8]
        layer_gain = stat[:, 522:538]
        ss2, rstd2 = stat[:, 538:544], stat[:, 544:550]

        root4, eps, idle = stat[:, 550:554], stat[:, 554:555], stat[:, 555:583]

        block = ctx.enter_context(nc.Block())

        @block.sync
        def _(sp):
            sp.dma_start(X[:, :, :], x_in).then_inc(sem("x_in"), 16)
            for s in range(SLOTS):
                sp.dma_start(ring[:, s, :], stream[s]).then_inc(slot_loaded[s], 16)
            rounds = N_CHUNKS // SLOTS
            with sp.Fori(1, rounds) as r:
                for s in range(SLOTS):
                    sp.wait_ge(slot_free[s], r)
                    sp.dma_start(ring[:, s, :], stream[bass.ds(r * SLOTS + s, 1)].rearrange("a p n -> (a p) n"))\
                        .then_inc(slot_loaded[s], 16)
            for s in range(N_CHUNKS - rounds * SLOTS):
                sp.wait_ge(slot_free[s], rounds)
                sp.dma_start(ring[:, s, :], stream[rounds * SLOTS + s]).then_inc(slot_loaded[s], 16)
            sp.wait_ge(sem("result"), TT)
            sp.dma_start(out.rearrange("a (t p) d -> p (a t) d", p=P), xn4[:, 0:TT, :]).then_inc(sem("stored"), 16)
            sp.wait_ge(sem("stored"), 16)

        @block.gpsimd
        def _(pool):
            def load(dst, src, name):
                pool.dma_start(dst, src).then_inc(sem(name), 16)

            load(sc[:, :, :], ccols, "c_in")
            load(mrow, modb[0], "modb_in")
            load(base[:, :], base_c, "base_in")
            load(small[:, :], small_c, "small_in")
            load(region(EV_PACK, EV_PACK_W), ev_pack, "ev_in")
            pool.wait_ge(sem("mod_saved"), 1)
            pool.wait_ge(sem("mod_spread"), 1)
            load(mrow, modb[1], "modb_in")
            pool.wait_ge(sem("x_moe"), GROUPS)
            load(region(OD_SHIFT, 4 * P + 3 * 512), od_pack, "od_in")
            load(region(OD_ROPE, 4 * 16), od_rope, "od_in2")
            pool.wait_ge(sem("x_mix"), 12)
            load(final_g[0], gains[0], "fg_in")
            pool.wait_ge(sem("x_moe"), 2 * GROUPS)
            load(region(B2_MASK, 1792), b2_masks, "b2_in")
            load(region(B2_ROPE, 4 * 8), b2_rope, "b2_in2")
            pool.wait_ge(sem("b2_merged"), B2_LAYERS * 4)
            load(final_g[1], gains[1], "fg_in")

        @block.tensor
        def _(pe):
            b = Banks(pe)
            state = {"chunk_lap": 0}
            owed = []

            def mm(o, lhsT, rhs, start, stop, sig=None):
                ins = pe.matmul(o, lhsT, rhs, start=start, stop=stop)
                if sig is not None:
                    ins.then_inc(sig, 1)
                elif owed:
                    ins.then_inc(slot_free[owed.pop(0)], 1)

            def turn(o, in_, n=P, sig=None):
                ins = pe.transpose(o, in_, base[0:n, IDENT:IDENT + n])
                if sig is not None:
                    ins.then_inc(sig, 1)
                elif owed:
                    ins.then_inc(slot_free[owed.pop(0)], 1)

            def arrived(name, k):
                n = CHUNK_AT[name, k]
                pe.wait_ge(slot_loaded[n % SLOTS], state["chunk_lap"] * 16 + 16 * (n // SLOTS + 1))

            def used(name, k):
                owed.append(CHUNK_AT[name, k] % SLOTS)

            def settle():
                while owed:
                    pe.drain().then_inc(slot_free[owed.pop(0)], 1)

            def norm(name, xn, tiles, ready, count):
                for t in range(tiles):
                    pe.wait_ge(ready, count - tiles + t + 1)
                    for k in range(KD):
                        if t == 0:
                            b.vacant(name, k)
                        turn(bank(name, k)[:, t * P:(t + 1) * P], xn[:, t, k * P:(k + 1) * P],
                             sig=fills(name, k) if t == tiles - 1 else None)

            def product(name, key, lhs, rhs, kts, width, sig=True, col=0):
                o = bank(name, key)[:, col:col + width]
                for n in range(kts):
                    mm(o, lhs(n), rhs(n), n == 0, n == kts - 1, fills(name, key) if sig and n == kts - 1 else None)

            def mod_chunk(layer, c):
                name = f"mod{layer}"
                arrived(name, c)
                b.vacant(name, c)
                w = chunk(name, c).rearrange("p (k n) -> p k n", k=KD)
                for k in range(KD):
                    for q in range(4):
                        mm(bank(name, c)[32 * q:32 * q + 32, 0:P], sc[:, k, :], w[:, k, q * P:(q + 1) * P], k == 0, k == KD - 1,
                           fills(name, c) if k == KD - 1 and q == 3 else None)
                used(name, c)

            def mod_cols(layer, half):
                name = f"modcol{layer}"
                b.vacant(name, half)
                for n, v in enumerate(((1, 0), (4, 3))[half]):
                    for cc in range(2):
                        at = (2 * n + cc) * P
                        turn(bank(name, half)[:, at:at + P], mrow[:, (2 * v + cc) * P:(2 * v + cc + 1) * P],
                             sig=fills(name, half) if (n, cc) == (1, 1) else None)

            def mod_row(name, n, src, s):
                b.vacant(name, n)
                for qq in range(2):
                    at = 32 * (2 * (n % 2) + qq) + s
                    mm(bank(name, n)[:, qq * 256:(qq + 1) * 256], ident[:, at:at + 1].to_broadcast([P, P]), src, True, True,
                       fills(name, n) if qq == 1 else None)

            def attention(name, schedule, score, nk, value, p, pt, ready):
                for what, *x in schedule:
                    if what == "m":
                        mod_chunk(*x)
                        continue
                    if what == "f":
                        n = x[1]
                        if n == 0:
                            b.drained("mod0", 11)
                            mod_cols(0, 1)
                        else:
                            mod_row("modrow0", n - 1, mrow[:, 4 * P:6 * P], (n - 1) // 2)
                        continue
                    kind, u = x
                    b.vacant(name, (kind, u))
                    o = bank(name, (kind, u))
                    if kind == "s":
                        score(u, o)
                    elif kind == "t":
                        ready(u)
                        for n in range(nk(u)):
                            turn(o[:, n * P:(n + 1) * P], p[u % S_BUFS][:, n * P:(n + 1) * P],
                                 sig=fills(name, (kind, u)) if n == nk(u) - 1 else None)
                    else:
                        b.drained(name, ("t", u))
                        for n in range(nk(u)):
                            mm(o[:, 0:64], pt[:, u % 2, n, :], value(u, n), n == 0, n == nk(u) - 1,
                               fills(name, (kind, u)) if n == nk(u) - 1 else None)

            def cat_turns(name, src, tiles):
                for k in range(KD):
                    b.vacant(name, k)
                    for t in range(tiles):
                        turn(bank(name, k)[:, t * P:(t + 1) * P], src[:, t, k * P:(k + 1) * P],
                             sig=fills(name, k) if t == tiles - 1 else None)

            def mix(layer, catt, tiles):
                L = str(layer)
                for k in (6, 7):
                    b.drained("cat" + L, k)
                for t in range(tiles):
                    for c in range(2):
                        if t == 0:
                            arrived("mix" + L, c)
                        w = chunk("mix" + L, c).rearrange("p (k n) -> p k n", k=KD)
                        b.vacant("mix" + L, (c, t))
                        product("mix" + L, (c, t), lambda k: catt[:, k, t * P:(t + 1) * P], lambda k: w[:, k, :], KD, 512)
                        if t == tiles - 1:
                            used("mix" + L, c)

            def experts(layer):
                L = str(layer)
                streams = 2 - layer
                tiles = TT * streams
                rows = streams * CAP
                parts = P // rows
                moe = "moe" + L
                b.vacant("logit" + L, 0)
                o = bank("logit" + L, 0)
                for k in range(KD):
                    b.drained("n2_" + L, k)
                    at = ROUTER + (layer * KD + k) * N_EXP
                    for q in range(tiles):
                        t = q % streams * TT + q // streams
                        mm(o[32 * q:32 * q + 32, 0:P], small[:, at:at + 32], moe_ht[:, k, t * P:(t + 1) * P], k == 0, k == KD - 1,
                           fills("logit" + L, 0) if q == tiles - 1 and k == KD - 1 else None)
                b.drained("logit" + L, 0)
                b.vacant("logitT" + L, 0)
                turn(bank("logitT" + L, 0)[:, 0:32 * tiles], moe_work[0:32 * tiles, 0:P], 32 * tiles, fills("logitT" + L, 0))
                ne = streams * N_EXP
                pe.wait_ge(sem("aff"), layer + 1)
                b.vacant("affT" + L, 0)
                for t in range(TT):
                    turn(bank("affT" + L, 0)[0:ne, t * P:(t + 1) * P], moe_aff[:, t * ne:(t + 1) * ne],
                         sig=fills("affT" + L, 0) if t == TT - 1 else None)
                if layer == 0:
                    for n in range(4):
                        mod_row("modrow5", n, mrow5, n // 2)
                pe.wait_ge(sem("chosen"), layer + 1)
                b.vacant("selT" + L, 0)
                for t in range(TT):
                    turn(bank("selT" + L, 0)[:, t * ne:(t + 1) * ne], moe_chosen[0:ne, t * P:(t + 1) * P], ne,
                         fills("selT" + L, 0) if t == TT - 1 else None)
                b.drained("selT" + L, 0)
                b.vacant("rank" + L, 0)
                o = bank("rank" + L, 0)
                mm(o[:, 0:ne], tri_le, mkT[:, 0:ne], True, True)
                mm(o[:, ne:2 * ne], ones, mkT[:, 0:ne], True, False)
                mm(o[:, ne:2 * ne], tri_le, mkT[:, ne:2 * ne], False, True, fills("rank" + L, 0))
                settle()
                with pe.Fori(0, GROUPS) as i:
                    b.lap = i * LAP[moe]
                    state["chunk_lap"] = i * CHUNK_LAP[moe]
                    pe.wait_ge(sem("hot" + L), i * tiles + tiles)
                    for k in range(KD):
                        b.vacant("gather" + L, k)
                        for s in range(streams):
                            for t in range(TT):
                                tok = s * TT + t
                                mm(bank("gather" + L, k)[:, s * P:(s + 1) * P], moe_xn[:, tok, k * P:(k + 1) * P], moe_oh[:, tok, :],
                                   t == 0, t == TT - 1,
                                   fills("gather" + L, k) if (s, t) == (streams - 1, TT - 1) else None)
                    pe.wait_ge(sem("gated" + L), i * tiles + tiles)
                    for e in range(PER_GROUP):
                        xs = moe_x(streams)[:, :, e].rearrange("p k s c -> p k (s c)")
                        width = NCOL // parts

                        def hidden(key, c):
                            arrived(moe, e * 6 + c)
                            b.vacant(moe, (e, key))
                            w = chunk(moe, e * 6 + c).rearrange("p (k n) -> p k n", k=KD)
                            o = bank(moe, (e, key))
                            for k in range(KD):
                                if e == 0 and c == 0:
                                    b.drained("gather" + L, k)
                                for q in range(parts):
                                    last = k == KD - 1 and q == parts - 1
                                    mm(o[q * rows:(q + 1) * rows, 0:width], xs[:, k, :], w[:, k, q * width:(q + 1) * width],
                                       k == 0, k == KD - 1, fills(moe, (e, key)) if last else None)
                            used(moe, e * 6 + c)

                        def turn_hidden(c):
                            b.drained(moe, (e, f"b{c}"))
                            b.vacant(moe, (e, f"t{c}"))
                            for j in range(width // P):
                                turn(bank(moe, (e, f"t{c}"))[:, j * P:(j + 1) * P], moe_g[:, c, j * P:(j + 1) * P],
                                     sig=fills(moe, (e, f"t{c}")) if j == width // P - 1 else None)

                        def down(c, kts):
                            w = chunk(moe, e * 6 + 4 + c).rearrange("p (k n) -> p k n", k=4)
                            o = bank(moe, (e, "y"))
                            yw = D // parts
                            for kt in kts:
                                q, j = kt // (width // P), kt % (width // P)
                                lhs = moe_gtr[:, e % 2, c, j * P + q * rows:j * P + (q + 1) * rows]
                                for n in range(parts):
                                    last = c == 1 and kt == 3 and n == parts - 1
                                    mm(o[n * rows:(n + 1) * rows, 0:yw], lhs, w[:, kt, n * yw:(n + 1) * yw],
                                       c == 0 and kt == 0, c == 1 and kt == 3, fills(moe, (e, "y")) if last else None)

                        b.vacant(moe, (e, "gate"))
                        for t in range(tiles):
                            turn(bank(moe, (e, "gate"))[0:CAP, t * P:(t + 1) * P], moe_gw[:, t, e * CAP:(e + 1) * CAP],
                                 sig=fills(moe, (e, "gate")) if t == tiles - 1 else None)
                        hidden("a0", 0)
                        hidden("b0", 1)
                        hidden("a1", 2)
                        turn_hidden(0)
                        hidden("b1", 3)
                        arrived(moe, e * 6 + 4)
                        b.vacant(moe, (e, "y"))
                        b.drained(moe, (e, "t0"))
                        down(0, (0, 1))
                        turn_hidden(1)
                        down(0, (2, 3))
                        used(moe, e * 6 + 4)
                        arrived(moe, e * 6 + 5)
                        b.drained(moe, (e, "t1"))
                        down(1, (0, 1, 2, 3))
                        used(moe, e * 6 + 5)
                    settle()
                    b.drained(moe, (PER_GROUP - 1, "gate"))
                    b.drained(moe, (PER_GROUP - 1, "y"))
                    pieces = 8 // tiles
                    w = D // pieces
                    for n in range(8):
                        t, c = n // pieces, n % pieces
                        b.vacant("comb" + L, n)
                        mm(bank("comb" + L, n)[:, 0:w], moe_gtst[:, t * P:(t + 1) * P],
                           moe_yst[:, t // TT, c * w:(c + 1) * w], True, True, fills("comb" + L, n))
                b.lap = 0
                state["chunk_lap"] = 0

            pe.wait_ge(sem("silu_c"), 1)
            for c in range(MOD_EARLY):
                mod_chunk(0, c)
            pe.wait_ge(sem("base_in"), 16)
            b.drained("mod0", MOD_EARLY - 1)
            mod_cols(0, 0)
            norm("n1_0", xn4, 4, sem("xn"), 4)
            for k in (6, 7):
                b.drained("n1_0", k)
            for c in range(4):
                arrived("evz", c)
                width = 512 if c < 3 else 256
                w = chunk("evz", c)[:, 0:KD * width].rearrange("p (k n) -> p k n", k=KD)
                for t in range(4):
                    b.vacant("evz", (c, t))
                    product("evz", (c, t), lambda k: ht4[:, k, t * P:(t + 1) * P], lambda k: w[:, k, :], KD, width)
                used("evz", c)
            pe.wait_ge(sem("ev_in"), 16)
            for t in range(4):
                pe.wait_ge(sem("sgu_v"), t + 1)
                b.vacant("sgu", t)
                for g in range(4):
                    mm(bank("sgu", t)[:, g * P:(g + 1) * P], ev_sguw[:, g, :], ev_z[:, t, 512 + g * P:512 + (g + 1) * P],
                       True, True, fills("sgu", t) if g == 3 else None)
            b.drained("evz", (3, 3))
            pe.wait_ge(sem("ev_rope"), TT)
            for j in range(1 + EV_PAIRS):
                b.vacant("evqk", j)
                for t in range(4):
                    turn(bank("evqk", j)[:, t * P:(t + 1) * P], ev_z[:, t, 1152 + j * P:1152 + (j + 1) * P],
                         sig=fills("evqk", j) if t == 3 else None)

            def ev_score(u, o):
                h, t = EV_UNITS[u]
                r = 64 * (h % 2)
                if u == 0:
                    b.drained("evqk", EV_PAIRS)
                first = 0 if t < TT else SEQ
                mm(o[:, 0:512 - first], ev_qt[r:r + 64, h // 2, t * P:(t + 1) * P], ev_kt[r:r + 64, first:512],
                   True, True, fills("evatt", ("s", u)))

            def ev_keys(u):
                return 4 if EV_UNITS[u][1] < TT else 2

            def ev_value(u, n):
                h, t = EV_UNITS[u]
                return ev_z[:, n + (0 if t < TT else TT), 1024 + 64 * (h % 2):1088 + 64 * (h % 2)]

            attention("evatt", ev_schedule(ATT_LAGS), ev_score, ev_keys, ev_value, ev_s, ev_pt,
                      lambda u: pe.wait_ge(sem("ev_p"), u + 1))
            b.drained("evatt", ("o", len(EV_UNITS) - 1))
            b.drained("sgu", 3)
            b.drained("mod1", 11)
            for half in range(2):
                mod_cols(1, half)
            cat_turns("cat0", ev_cat, 4)
            mix(0, ev_catt, 4)
            norm("n2_0", moe_xn, 4, sem("xn"), 8)
            experts(0)

            for n in range(4):
                v = 2 + 3 * (n // 2)
                mod_row("modrow1", n, mrow[:, 2 * v * P:(2 * v + 2) * P], 0)
            norm("n1_1", xn4, 4, sem("xn"), 12)
            for k in (6, 7):
                b.drained("n1_1", k)

            def convolution():
                pe.wait_ge(sem("od_in"), 16)
                pe.wait_ge(sem("conv_u"), TT)
                for t in range(TT):
                    for d in range(2):
                        b.vacant("conv", (t, d))
                        o = bank("conv", (t, d))[:, :]
                        seam = t == 1 - d
                        mm(o, od_shift[:, 2 * d, :], od_zb[:, t, 512:1024], True, not seam, None if seam else fills("conv", (t, d)))
                        if seam:
                            mm(o, od_shift[:, 2 * d + 1, :], od_zb[:, 1 - t, 512:1024], False, True, fills("conv", (t, d)))

            for c in ODZ_ORDER:
                arrived("odz", c)
                width = 512 if c < 4 else OD_TAIL
                w = chunk("odz", c)[:, 0:KD * width].rearrange("p (k n) -> p k n", k=KD)
                for t in range(4 if c == 0 else 2):
                    if (c, t) == (0, TT):
                        convolution()
                    n = width if t < TT else KV_LORA + KR
                    b.vacant("odz", (c, t))
                    product("odz", (c, t), lambda k: ht4[:, k, t * P:(t + 1) * P], lambda k: w[:, k, 0:n], KD, n)
                if c < 4:
                    used("odz", c)
            pe.wait_ge(sem("lora_n"), 6)
            for j in range(2):
                b.vacant("ckvT", j)
                for t in range(4):
                    src = od_za[:, t, :] if t < TT else od_zc[:, t - TT, :]
                    turn(bank("ckvT", j)[:, t * P:(t + 1) * P], src[:, j * P:(j + 1) * P],
                         sig=fills("ckvT", j) if t == 3 else None)
            for j in range(3):
                b.vacant("cqT", j)
                for t in range(TT):
                    at = KV_LORA + KR + j * P
                    turn(bank("cqT", j)[:, t * P:(t + 1) * P], od_za[:, t, at:at + P],
                         sig=fills("cqT", j) if t == TT - 1 else None)
            uq = chunk("odz", 4)[:, KD * OD_TAIL:KD * OD_TAIL + 3 * UQ_W].rearrange("p (k n) -> p k n", k=3)
            b.drained("cqT", 2)
            for p in range(2):
                for t in range(TT):
                    b.vacant("uq", (p, t))
                    product("uq", (p, t), lambda k: od_cqt[:, k, t * P:(t + 1) * P],
                            lambda k: uq[:, k, p * 384:(p + 1) * 384], 3, 384)
            used("odz", 4)
            arrived("ukv", 0)
            ukv = chunk("ukv", 0)[:, 0:2 * D].rearrange("p (k n) -> p k n", k=2)
            for p in range(2):
                for t in range(4):
                    b.vacant("ukv", (p, t))
                    product("ukv", (p, t), lambda k: od_ckvt[:, k, t * P:(t + 1) * P],
                            lambda k: ukv[:, k, p * 512:(p + 1) * 512], 2, 512)
            used("ukv", 0)
            b.drained("ukv", (1, 3))
            pe.wait_ge(sem("od_kr"), 4)
            for h in range(OD_HEADS):
                b.vacant("odkT", h)
                for t in range(4):
                    turn(bank("odkT", h)[0:OD_DIM, t * P:(t + 1) * P], od_kf[:, t, h * OD_DIM:(h + 1) * OD_DIM],
                         sig=fills("odkT", h) if t == 3 else None)
            pe.wait_ge(sem("od_rope"), TT)
            for j in range(OD_HEADS // 2):
                b.vacant("odqT", j)
                for n in range(2):
                    for t in range(TT):
                        h = 2 * j + n
                        turn(bank("odqT", j)[0:OD_DIM, (n * TT + t) * P:(n * TT + t + 1) * P],
                             od_q[:, t, h * OD_DIM:(h + 1) * OD_DIM],
                             sig=fills("odqT", j) if n == 1 and t == TT - 1 else None)

            def od_score(u, o):
                h, t = OD_UNITS[u]
                if u == 0:
                    b.drained("odqT", OD_HEADS // 2 - 1)
                    b.drained("odkT", OD_HEADS - 1)
                mm(o[:, :], od_qt[0:OD_DIM, h, t * P:(t + 1) * P], od_kt[0:OD_DIM, h, :], True, True, fills("odatt", ("s", u)))

            attention("odatt", [("a", *x) for x in pipeline(len(OD_UNITS), ATT_LAGS)], od_score, lambda u: 4,
                      lambda u, n: od_v[:, n, OD_UNITS[u][0] * 64:OD_UNITS[u][0] * 64 + 64], od_s, od_pt,
                      lambda u: b.drained("odatt", ("s", u)))
            b.drained("odatt", ("o", len(OD_UNITS) - 1))
            pe.wait_ge(sem("conv_done"), TT)
            cat_turns("cat1", od_cat, TT)
            mix(1, od_catt, TT)
            norm("n2_1", moe_xn, TT, sem("xn"), 14)
            experts(1)

            with pe.Fori(0, B2_LAYERS) as i:
                b.lap = i * LAP["b2"]
                state["chunk_lap"] = i * CHUNK_LAP["b2"]
                norm("nmix", region(B2_XN1, TT, D), TT, sem("b2_xn"), i * 4 + 2)

                def split_piece(name, k, m, products):
                    p = PIECE_AT[name, k, m]
                    pe.wait_ge(sem("w_lo"), i * len(PIECES) + p + 1)
                    _, wh, wl = piece_of(name, k, m)
                    for n, (xh, xl, kt, cols, o, start, stop, ticket) in enumerate(products):
                        passes = [(xh, wh[:, kt, cols]), (xh, wl[:, kt, cols]), (xl, wh[:, kt, cols])]
                        for q, (x, w) in enumerate(passes):
                            sig = None
                            if q == 2 and ticket is not None:
                                sig = fills(*ticket)
                            elif q == 2 and n == len(products) - 1:
                                sig = sem("piece_used")
                            lhs, rhs = (w, x) if name == "up" else (x, w)
                            mm(o, lhs, rhs, start and q == 0, stop and q == 2, sig)
                    if m == PIECES_PER_CHUNK - 1:
                        used(name, k)

                def by_tokens(name, k, m, xh, xl, key, span, width):
                    out = []
                    for kt in (2 * m, 2 * m + 1):
                        for t in range(TT):
                            first, last = span(kt)
                            ticket = (name, key(kt, t))
                            cols = slice(t * P, (t + 1) * P)
                            out.append((xh[:, kt, cols], xl[:, kt, cols], kt - 2 * m, slice(0, width), bank(*ticket)[:, 0:width],
                                        kt == first, kt == last - 1, ticket if kt == last - 1 else None))
                    split_piece(name, k, m, out)

                whole = lambda kt: (0, KD)
                for c in range(9):
                    for t in range(TT):
                        b.vacant("qkv", (c, t))
                    for m in range(PIECES_PER_CHUNK):
                        if c == 0:
                            pe.wait_ge(sem("a_lo"), i * 12 + m + 1)
                        by_tokens("qkv", c, m, a_hi, a_lo, lambda kt, t: (c, t), whole, 512)
                for wh in range(2):
                    src = (b2_q, b2_k)[wh]
                    pe.wait_ge(sem("b2_rope"), i * 4 + 2 + 2 * wh)
                    b.drained("qkv", (2 + 3 * wh, 1))
                    for j in range(B2_PAIRS // 2):
                        b.vacant("qkT", (wh, j))
                        for n in range(2):
                            for t in range(TT):
                                turn(bank("qkT", (wh, j))[:, (n * TT + t) * P:(n * TT + t + 1) * P],
                                     src[:, t, (2 * j + n) * P:(2 * j + n + 1) * P],
                                     sig=fills("qkT", (wh, j)) if n == 1 and t == TT - 1 else None)
                for j in (B2_PAIRS // 2 - 2, B2_PAIRS // 2 - 1):
                    b.drained("qkT", (1, j))
                b.drained("qkv", (8, 1))
                def softmax_unit(kind, u, n):
                    key = (kind, u, n)
                    unit = AB_UNITS[u]
                    t = unit[2]
                    per_bank = ab_keys_per_bank(*unit)
                    b.vacant("ab", key)
                    o = bank("ab", key)
                    if kind == "s":
                        blocks = per_bank[n]
                        heads = list(dict.fromkeys(hd for hd, _ in blocks))
                        for q, hd in enumerate(heads):
                            at = [m for m, x in enumerate(blocks) if x[0] == hd]
                            kts = [blocks[m][1] for m in at]
                            r = 64 * (hd % 2)
                            mm(o[:, at[0] * P:(at[-1] + 1) * P], b2_qt[r:r + 64, hd // 2, t * P:(t + 1) * P],
                               b2_kt[r:r + 64, hd // 2, kts[0] * P:(kts[-1] + 1) * P], True, True,
                               fills("ab", key) if q == len(heads) - 1 else None)
                    elif kind == "t":
                        if n == 0:
                            pe.wait_ge(sem("b2_p"), i * len(AB_UNITS) + u + 1)
                        for m in range(len(per_bank[n])):
                            turn(o[:, m * P:(m + 1) * P], b2_s[:, u % S_BUFS, (4 * n + m) * P:(4 * n + m + 1) * P],
                                 sig=fills("ab", key) if m == len(per_bank[n]) - 1 else None)
                    else:
                        for m in range(len(per_bank)):
                            b.drained("ab", ("t", u, m))
                        keys = ab_keys(*unit)
                        for m, (hd, kt) in enumerate(keys):
                            mm(o[:, 0:64], b2_pt[:, u % 2, m, :], b2_v[:, kt, hd * 64:(hd + 1) * 64], m == 0, m == len(keys) - 1,
                               fills("ab", key) if m == len(keys) - 1 else None)

                def stick_unit(kind, u, n):
                    key = (kind, u, n)
                    hd = 18 + u
                    r = 64 * (hd % 2)
                    b.vacant("c", key)
                    o = bank("c", key)
                    buf = b2_c[:, u % C_BUFS, :]
                    if kind == "s":
                        mm(o[:, 0:SEQ], b2_kt[r:r + 64, hd // 2, 0:P], b2_qt[r:r + 64, hd // 2, :], True, True)
                        mm(o[:, SEQ:SEQ + P], b2_kt[r:r + 64, hd // 2, P:SEQ], b2_qt[r:r + 64, hd // 2, P:SEQ], True, True, fills("c", key))
                    elif kind == "c":
                        pe.wait_ge(sem("c_softplus"), i * len(C_UNITS) + u + 1)
                        mm(o[:, 0:SEQ], tri_ge, buf[:, 384:384 + SEQ], True, False)
                        mm(o[:, P:SEQ], ones, buf[:, 384 + SEQ:768], False, True)
                        mm(o[:, SEQ:SEQ + P], tri_ge, buf[:, 384 + SEQ:768], True, True, fills("c", key))
                    else:
                        if n == 0:
                            pe.wait_ge(sem("c_weights"), i * len(C_UNITS) + u + 1)
                        for kt in range(n + 1):
                            at = 384 + (n * P if kt == 0 else SEQ)
                            mm(o[:, 0:64], buf[:, at:at + P], b2_v[:, kt, hd * 64:(hd + 1) * 64], kt == 0, kt == n,
                               fills("c", key) if kt == n else None)

                for which, kind, u, n in b2_schedule(ATT_LAGS, C_LAGS):
                    (softmax_unit if which == "ab" else stick_unit)(kind, u, n)
                b.drained("c", ("o", 5, 1))
                b.drained("ab", ("o", len(AB_UNITS) - 1, 0))
                for j in range(4):
                    b.vacant("ocat", j)
                    for n in range(2):
                        for t in range(TT):
                            k = 2 * j + n
                            turn(bank("ocat", j)[:, (n * TT + t) * P:(n * TT + t + 1) * P], b2_ocat[:, t, k * P:(k + 1) * P],
                                 sig=fills("ocat", j) if n == 1 and t == TT - 1 else None)
                for c in range(2):
                    for k in range(3):
                        for t in range(TT):
                            b.vacant("merge", (c, "gate", k, t))
                        for m in range(PIECES_PER_CHUNK):
                            if c == 0 and k == 0:
                                pe.wait_ge(sem("a_lo"), i * 12 + 4 + m + 1)
                            by_tokens("merge", 4 * c + k, m, a_hi, a_lo, lambda kt, t: (c, "gate", k, t), whole, 512)
                    if c == 0:
                        for j in range(4):
                            b.drained("ocat", j)
                    for k in range(3):
                        for t in range(TT):
                            b.vacant("merge", (c, "branch", k, t))
                    branch = lambda kt: 0 if kt < 2 else 1 if kt < 5 else 2
                    for m in range(PIECES_PER_CHUNK):
                        by_tokens("merge", 4 * c + 3, m, o_hi, o_lo, lambda kt, t: (c, "branch", branch(kt), t),
                                  lambda kt: BRANCHES[branch(kt)], 512)
                pe.wait_ge(sem("b2_merged"), i * 4 + 4)
                for j in range(4):
                    b.vacant("mergeT", j)
                    for n in range(2):
                        for t in range(TT):
                            k = 2 * j + n
                            turn(bank("mergeT", j)[:, (n * TT + t) * P:(n * TT + t + 1) * P], b2_merged[:, t, k * P:(k + 1) * P],
                                 sig=fills("mergeT", j) if n == 1 and t == TT - 1 else None)
                for j in (2, 3):
                    b.drained("mergeT", j)
                for c in range(3):
                    for t in range(TT):
                        b.vacant("wo", (c, t))
                    for m in range(PIECES_PER_CHUNK):
                        by_tokens("wo", c, m, a_hi, a_lo, lambda kt, t: (c, t), whole, WO_PIECES[c])
                norm("nmlp", region(B2_XN2, TT, D), TT, sem("b2_xn"), i * 4 + 4)
                pe.wait_ge(sem("a_lo"), i * 12 + 12)

                def up(j):
                    for m in range(PIECES_PER_CHUNK):
                        n, half = m // 2, m % 2
                        if half == 0:
                            b.vacant("up", (j, n))
                        o = bank("up", (j, n))[:, half * SEQ:(half + 1) * SEQ]
                        split_piece("up", j, m, [(a_hi[:, k, :], a_lo[:, k, :], k, slice(0, P), o, k == 0, k == KD - 1,
                                                  ("up", (j, n)) if half and k == KD - 1 else None) for k in range(KD)])

                def down_ff(j):
                    pe.wait_ge(sem("b2_hidden"), i * (2 * N_FF) + 2 * j + 2)
                    for t in range(TT):
                        for h in range(2):
                            b.vacant("down", (j, t, h))
                    for m in range(PIECES_PER_CHUNK):
                        last = m == PIECES_PER_CHUNK - 1
                        k = j % 2 * 4 + m
                        split_piece("down", j, m, [(o_hi[:, k, t * P:(t + 1) * P], o_lo[:, k, t * P:(t + 1) * P], 0,
                                                    slice(h * 512, (h + 1) * 512), bank("down", (j, t, h))[:, :], m == 0, last,
                                                    ("down", (j, t, h)) if last else None) for t in range(TT) for h in range(2)])

                for which, j in FF_ORDER:
                    (up if which == "up" else down_ff)(j)
                settle()

        @block.scalar
        def _(act):
            b = Banks(act)
            squares = [0]

            def copy(o, i, sig=None):
                ins = act.activation(o, i, ACT.Copy)
                if sig is not None:
                    ins.then_inc(sig, 1)

            def root(v, width, sig):
                act.activation(v, v, ACT.Sqrt, bias=eps, scale=1.0 / width).then_inc(sig, 1)

            warm = [0]

            def warm_up(before):
                act.activation(ss[:, 0:1], eps, ACT.Sqrt).then_inc(sem("warm"), 1)
                act.wait_ge(sem("warm"), before + 1)

            def square_sums(x, junk, tiles, ready=None, after=None):
                warm_up(warm[0])
                warm[0] += 1
                if after is not None:
                    after()
                for t in range(tiles):
                    if ready is not None:
                        act.wait_ge(sem("x_mix"), ready + 2 * (t + 1))
                    act.activation(junk[:, t, :], x[:, t, :], ACT.Square, accum_out=ss[:, t:t + 1]).then_inc(sem("sq"), 1)
                    squares[0] += 1
                    act.wait_ge(sem("sq"), squares[0])
                    root(ss[:, t:t + 1], D, sem("root"))

            def norm_out(name, dst, tiles, scale, shift):
                for k in range(0, KD, 2):
                    b.filled(name, k)
                    for s in range(tiles // TT):
                        cols = slice(s * SEQ, (s + 1) * SEQ)
                        ins = act.activation(dst[:, k, cols], bank(name, k)[:, cols], ACT.Identity,
                                             bias=shift[:, k, s:s + 1], scale=scale[:, k, s:s + 1])
                    ins.then_inc(frees(name, k), 1)

            def mod_row(name, n):
                b.filled(name, n)
                dst = bc[:, n // 2, :].rearrange("p (c q j) -> p q c j", c=2, q=4)[:, 2 * (n % 2):2 * (n % 2) + 2]
                copy(dst, bank(name, n)[:, :].rearrange("p (q c j) -> p q c j", q=2, c=2), frees(name, n))

            def cat_out(name, dst, width):
                for k in range(0, KD, 2):
                    b.filled(name, k)
                    copy(dst[:, k, :], bank(name, k)[:, 0:width], frees(name, k))

            def probs_out(name, u, pt, nk):
                b.filled(name, ("t", u))
                if u >= 2:
                    b.filled(name, ("o", u - 2))
                copy(pt[:, u % 2, 0:nk, :], bank(name, ("t", u))[:, 0:nk * P].rearrange("p (n q) -> p n q", n=nk),
                     frees(name, ("t", u)))

            def experts(layer):
                L = str(layer)
                moe = "moe" + L
                streams = 2 - layer
                tiles = TT * streams
                rows = streams * CAP
                parts = P // rows
                width, yw = NCOL // parts, D // parts
                b.drained("logitT" + L, 0)
                act.activation(lge[:, 0:tiles * N_EXP], lg[:, 0:tiles * N_EXP], ACT.Exp).then_inc(sem("lgt_exp"), 1)
                if layer == 0:
                    act.wait_ge(sem("x_mix"), 8)
                    for n in range(4):
                        mod_row("modrow5", n)
                with act.Fori(0, GROUPS) as i:
                    b.lap = i * LAP[moe]
                    for e in range(PER_GROUP):
                        b.filled(moe, (e, "gate"))
                        copy(moe_gtst[e * CAP:(e + 1) * CAP, 0:tiles * P], bank(moe, (e, "gate"))[0:CAP, 0:tiles * P], frees(moe, (e, "gate")))
                        for c in range(2):
                            b.filled(moe, (e, f"a{c}"))
                            act.activation(moe_sil[:, c, 0:width], bank(moe, (e, f"a{c}"))[:, 0:width], ACT.Silu)\
                                .then_inc(frees(moe, (e, f"a{c}")), 1)
                        for c in range(2):
                            b.filled(moe, (e, f"t{c}"))
                            copy(moe_gtr[:, e % 2, c, 0:width], bank(moe, (e, f"t{c}"))[:, 0:width], frees(moe, (e, f"t{c}")))
                        b.filled(moe, (e, "y"))
                        for n in range(parts):
                            for s in range(streams):
                                last = n == parts - 1 and s == streams - 1
                                at = n * rows + s * CAP
                                copy(moe_yst[e * CAP:(e + 1) * CAP, s, n * yw:(n + 1) * yw],
                                     bank(moe, (e, "y"))[at:at + CAP, 0:yw], frees(moe, (e, "y")) if last else None)
                b.lap = 0

            act.wait_ge(sem("eps"), 1)
            act.wait_ge(sem("c_in"), 16)
            act.activation(sc[:, :, :], sc[:, :, :], ACT.Silu).then_inc(sem("silu_c"), 1)

            act.wait_ge(sem("x_in"), 16)
            square_sums(X, xn4, 4)
            b.drained("modcol0", 0)
            norm_out("n1_0", ht4, 4, A1[0], B1[0])
            for c in range(4):
                for t in range(4):
                    b.filled("evz", (c, t))
                    w = 512 if c < 3 else 256
                    act.activation(ev_z[:, t, c * 512:c * 512 + w], bank("evz", (c, t))[:, 0:w],
                                   ACT.Gelu_apprx_tanh if c < 2 else ACT.Copy).then_inc(frees("evz", (c, t)), 1)
                if c == 2:
                    act.wait_ge(sem("sgu_var"), 4)
                    root(root4, 1, sem("sgu_root"))
            for j in range(1 + EV_PAIRS):
                b.filled("evqk", j)
                copy(ev_kt[:, :] if j == 0 else ev_qt[:, j - 1, :], bank("evqk", j)[:, :], frees("evqk", j))
            for what, *x in ev_schedule(ATT_LAGS_ACT):
                if what == "f" and x[1] > 0:
                    mod_row("modrow0", x[1] - 1)
                    if x[1] == 4:
                        b.drained("modrow0", 3)
                        act.sem_inc(sem("mod_spread"), 1)
                if what != "a":
                    continue
                kind, u = x
                h, t = EV_UNITS[u]
                n = 512 if t < TT else SEQ
                s = ev_s[u % S_BUFS][:, 0:n]
                if kind == "s":
                    act.wait_ge(sem("ev_nm"), u + 1)
                    act.activation(s, s, ACT.Exp, bias=nm[:, u:u + 1], scale=EV_SCALE,
                                   accum_out=l[:, u:u + 1]).then_inc(sem("ev_p"), 1)
                    act.activation(ls[:, u:u + 1], ev_sink[:, h:h + 1], ACT.Exp, bias=nm[:, u:u + 1]).then_inc(sem("ev_ls"), 1)
                elif kind == "t":
                    probs_out("evatt", u, ev_pt, n // P)
            cat_out("cat0", ev_catt, 512)
            square_sums(X, moe_xn, 4, 0)
            b.drained("modcol0", 1)
            norm_out("n2_0", moe_ht, 4, A2[0], B2[0])
            experts(0)

            def moe_added():
                act.wait_ge(sem("x_moe"), GROUPS)
                for n in range(4):
                    mod_row("modrow1", n)

            square_sums(X, xn4, 4, after=moe_added)
            b.drained("modcol1", 1)
            norm_out("n1_1", ht4, 4, A1[1], B1[1])
            n_sq = [0]

            def lora_squares(parts):
                for src, col in parts:
                    act.activation(od_s[2][:, 0:src.shape[-1]], src, ACT.Square, accum_out=ss2[:, col:col + 1]).then_inc(sem("lora_sq"), 1)
                    n_sq[0] += 1
                    act.wait_ge(sem("lora_sq"), n_sq[0])

            for c in ODZ_ORDER:
                for t in range(4 if c == 0 else 2):
                    b.filled("odz", (c, t))
                    o = bank("odz", (c, t))
                    done = frees("odz", (c, t))
                    if c == 0 and t >= TT:
                        copy(od_zc[:, t - TT, :], o[:, 0:KV_LORA + KR], done)
                    elif c == 0:
                        copy(od_za[:, t, 0:512], o[:, :], done)
                    elif c == 1:
                        copy(od_za[:, t, 512:ZA_W], o[:, 0:ZA_W - 512])
                        copy(od_zb[:, t, 0:1024 - ZA_W], o[:, ZA_W - 512:512], done)
                    else:
                        at = c * 512 - ZA_W
                        w = 512 if c < 4 else OD_TAIL
                        copy(od_zb[:, t, at:at + w], o[:, 0:w], done)
                    if (c, t) == (0, TT - 1):
                        for tile in range(TT):
                            b.drained("odz", (0, tile))
                        lora_squares([(od_za[:, tile, 0:KV_LORA], tile) for tile in range(TT)])
                        lora_squares([(od_za[:, tile, KV_LORA + KR:], 4 + tile) for tile in range(TT)])
                        root(ss2[:, 0:TT], KV_LORA, sem("lora_root"))
                        root(ss2[:, 4:6], Q_LORA, sem("lora_root"))
            for tile in range(TT):
                b.drained("odz", (0, TT + tile))
            lora_squares([(od_zc[:, tile, 0:KV_LORA], TT + tile) for tile in range(TT)])
            root(ss2[:, TT:4], KV_LORA, sem("lora_root"))
            act.wait_ge(sem("conv_done"), TT)
            for p in range(2):
                for t in range(TT):
                    b.filled("uq", (p, t))
                    copy(od_q[:, t, p * 384:(p + 1) * 384], bank("uq", (p, t))[:, 0:384], frees("uq", (p, t)))
            for p in range(2):
                for t in range(4):
                    b.filled("ukv", (p, t))
                    o = bank("ukv", (p, t))[:, :].rearrange("p (h d) -> p h d", h=4)
                    kf = od_kf[:, t, :].rearrange("p (h d) -> p h d", h=OD_HEADS)
                    copy(kf[:, 4 * p:4 * p + 4, 0:64], o[:, :, 0:64])
                    copy(od_v[:, t, p * 256:(p + 1) * 256].rearrange("p (h d) -> p h d", h=4), o[:, :, 64:128], frees("ukv", (p, t)))
            for h in range(OD_HEADS):
                b.filled("odkT", h)
                copy(od_kt[0:OD_DIM, h, :], bank("odkT", h)[0:OD_DIM, :], frees("odkT", h))
            for kind, u in pipeline(len(OD_UNITS), ATT_LAGS_ACT):
                if kind == "s":
                    act.wait_ge(sem("od_nm"), u + 1)
                    if u >= S_BUFS:
                        b.filled("odatt", ("t", u - S_BUFS))
                    act.activation(od_s[u % S_BUFS][:, :], bank("odatt", ("s", u))[:, :], ACT.Exp, bias=nm[:, u:u + 1], scale=OD_SCALE,
                                   accum_out=l[:, u:u + 1]).then_inc(frees("odatt", ("s", u)), 1)
                elif kind == "t":
                    probs_out("odatt", u, od_pt, 4)
            cat_out("cat1", od_catt, SEQ)
            square_sums(X, moe_xn, TT, 8)
            norm_out("n2_1", moe_ht, TT, A2[1], B2[1])
            experts(1)

            square_sums(X, xn4, TT, after=lambda: act.wait_ge(sem("x_moe"), 2 * GROUPS))
            act.wait_ge(sem("x_final"), TT)

            with act.Fori(0, B2_LAYERS) as i:
                b.lap = i * LAP["b2"]

                def squares2(junk, at, last):
                    warm_up(i * 2 + (warm[0] + at // 2))
                    b.drained(*last)
                    for t in range(TT):
                        act.activation(junk[:, t, :], X[:, t, :], ACT.Square, accum_out=ss[:, t:t + 1]).then_inc(sem("b2_sq"), 1)
                        act.wait_ge(sem("b2_sq"), i * 4 + at + t + 1)
                        root(ss[:, t:t + 1], D, sem("b2_root"))

                def split_weights(name, k, m):
                    p = PIECE_AT[name, k, m]
                    if m == 0:
                        n = CHUNK_AT[name, k]
                        act.wait_ge(slot_loaded[n % SLOTS], i * (CHUNK_LAP["b2"] * 16) + 16 * (n // SLOTS + 1))
                    if p >= PIECE_BUFS:
                        before = fills_last(*PIECES[p - PIECE_BUFS])
                        if before:
                            b.filled(*before)
                        else:
                            act.wait_ge(sem("piece_used"), i * USED_UP_TO[-1] + USED_UP_TO[p - PIECE_BUFS])
                    src, high, _ = piece_of(name, k, m)
                    copy(high, src, sem("w_hi"))

                def split_tokens(pair):
                    copy(a_hi[:, 2 * pair:2 * pair + 2, :], b2_ht[:, 2 * pair:2 * pair + 2, :], sem("a_hi"))

                def gain_out(name, off):
                    for k in range(0, KD + 2, 2):
                        if k < KD:
                            b.filled(name, k)
                            act.activation(b2_ht[:, k, :], bank(name, k)[:, 0:SEQ], ACT.Identity,
                                           scale=layer_gain[:, off + k:off + k + 1]).then_inc(frees(name, k), 1)
                        if k >= 2:
                            b.drained(name, k - 2)
                            b.drained(name, k - 1)
                            split_tokens(k // 2 - 1)

                squares2(region(B2_XN1, TT, D), 0, ("down", (N_FF - 1, 1, 1), LAP["b2"]))
                act.wait_ge(sem("b2_gain"), i * 2 + 2)
                for what, name, k, m in split_order(ATT_CHUNKS):
                    if what == "piece":
                        split_weights(name, k, m)
                    elif what == "begin":
                        gain_out("nmix", 0)
                    elif what == "out":
                        for t in range(TT):
                            b.filled("qkv", (k, t))
                            dst = (b2_q, b2_k, b2_v)[k // 3]
                            copy(dst[:, t, k % 3 * 512:(k % 3 + 1) * 512], bank("qkv", (k, t))[:, :], frees("qkv", (k, t)))
                for wh in range(2):
                    for j in range(B2_PAIRS // 2):
                        b.filled("qkT", (wh, j))
                        copy((b2_qt, b2_kt)[wh][:, 2 * j:2 * j + 2, :],
                             bank("qkT", (wh, j))[:, :].rearrange("p (n q) -> p n q", n=2), frees("qkT", (wh, j)))
                def softmax_unit(kind, u, n):
                    per_bank = ab_keys_per_bank(*AB_UNITS[u])
                    s = b2_s[:, u % S_BUFS, 0:P * len(ab_keys(*AB_UNITS[u]))]
                    if kind == "s" and n == len(per_bank) - 1:
                        act.wait_ge(sem("b2_nm"), i * len(AB_UNITS) + u + 1)
                        act.activation(s, s, ACT.Exp, bias=nm[:, u:u + 1], scale=B2_SCALE,
                                       accum_out=l[:, u:u + 1]).then_inc(sem("b2_p"), 1)
                    elif kind == "t":
                        b.filled("ab", (kind, u, n))
                        if u >= 2:
                            b.filled("ab", ("o", u - 2, 0))
                        m = len(per_bank[n])
                        copy(b2_pt[:, u % 2, 4 * n:4 * n + m, :],
                             bank("ab", (kind, u, n))[:, 0:m * P].rearrange("p (n q) -> p n q", n=m), frees("ab", (kind, u, n)))

                def stick_unit(kind, u, n):
                    buf = b2_c[:, u % C_BUFS, :]
                    k = i * len(C_UNITS) + u + 1
                    if kind == "s":
                        act.wait_ge(sem("c_abs"), k)
                        act.activation(buf[:, 384:768], buf[:, 384:768], ACT.Exp).then_inc(sem("c_exp"), 1)
                        act.wait_ge(sem("c_exp"), k)
                        act.activation(buf[:, 384:768], buf[:, 384:768], ACT.Ln, bias=1.0).then_inc(sem("c_ln"), 1)
                    elif kind == "c":
                        b.drained("c", (kind, u, 0))
                        act.activation(buf[:, 384:768], buf[:, 0:384], ACT.Exp).then_inc(sem("c_weights"), 1)
                    else:
                        b.filled("c", (kind, u, n))
                        copy(b2_ocat[:, n, 640 + u * 64:640 + (u + 1) * 64], bank("c", (kind, u, n))[:, 0:64], frees("c", (kind, u, n)))

                for which, kind, u, n in b2_schedule(ATT_LAGS_ACT, C_LAGS_ACT):
                    (softmax_unit if which == "ab" else stick_unit)(kind, u, n)
                def split_bank(name, j, dst, sig):
                    b.filled(name, j)
                    copy(dst[:, 2 * j:2 * j + 2, :], bank(name, j)[:, :].rearrange("p (n q) -> p n q", n=2), sig)

                b.filled("ocat", 0)
                for what, name, k, m in split_order(MLP_CHUNKS):
                    if what == "piece":
                        split_weights(name, k, m)
                    elif what == "begin":
                        for pair in range(KD // 2):
                            split_tokens(pair)
                        for j in range(4):
                            split_bank("ocat", j, o_hi, sem("ocat_hi"))
                    elif what == "out" and name == "merge" and k % 4 < 3:
                        c = k // 4
                        if c:
                            act.wait_ge(sem("b2_merged"), i * 4 + 2)
                        for t in range(TT):
                            key = (c, "gate", k % 4, t)
                            b.filled("merge", key)
                            act.activation(b2_sig[:, k % 4, t, :], bank("merge", key)[:, :], ACT.Sigmoid).then_inc(frees("merge", key), 1)
                    elif what == "out" and name == "up":
                        if k:
                            act.wait_ge(sem("b2_hidden"), i * (2 * N_FF) + 2 * k)
                        for n in range(2):
                            b.filled("up", (k, n))
                            act.activation(b2_sq[:, n, :], bank("up", (k, n))[:, :], ACT.Relu).then_inc(frees("up", (k, n)), 1)
                    elif what == "late" and name == "up":
                        for n in range(2):
                            act.wait_ge(sem("b2_squared"), i * (2 * N_FF) + 2 * k + n + 1)
                            at = k % 2 * 4 + 2 * n
                            copy(o_hi[:, at:at + 2, :], b2_sq[:, n, :].rearrange("p (m q) -> p m q", m=2), sem("hidden_hi"))
                    elif what == "late" and (name, k) == ("merge", 7):
                        for j in range(4):
                            split_bank("mergeT", j, a_hi, sem("merge_hi"))
                    elif what == "late" and (name, k) == ("wo", 2):
                        squares2(region(B2_XN2, TT, D), 2, ("wo", (2, 1)))
                        gain_out("nmlp", KD)
            b.lap = LAP["b2"] * (B2_LAYERS - 1)
            warm[0] += 2 * B2_LAYERS
            square_sums(X, xn4, TT, after=lambda: b.drained("down", (N_FF - 1, 1, 1)))

        @block.vector
        def _(dve):
            b = Banks(dve)
            steps = Steps(dve, sem("dve_step"))
            dve.memset(eps, EPS).then_inc(sem("eps"), 1)

            def norm(name, x, xn, tiles, n_root, dst, scale, shift):
                for t in range(tiles):
                    dve.wait_ge(sem("root"), n_root - tiles + t + 1)
                    steps.do(dve.reciprocal(rstd[:, t:t + 1], ss[:, t:t + 1]))
                    dve.tensor_scalar(xn[:, t, :], x[:, t, :], rstd[:, t:t + 1], None, ALU.mult).then_inc(sem("xn"), 1)
                for k in range(1, KD, 2):
                    b.filled(name, k)
                    for s in range(tiles // TT):
                        cols = slice(s * SEQ, (s + 1) * SEQ)
                        ins = dve.tensor_scalar(dst[:, k, cols], bank(name, k)[:, cols], scale[:, k, s:s + 1],
                                                shift[:, k, s:s + 1], ALU.mult, ALU.add)
                    ins.then_inc(frees(name, k), 1)

            def mod_chunk(layer, c):
                name = f"mod{layer}"
                if c == 0:
                    dve.wait_ge(sem("modb_in"), 16 * (layer + 1))
                b.filled(name, c)
                cols = mrow[:, c * P:(c + 1) * P]
                dve.tensor_tensor(cols, bank(name, c)[:, 0:P], cols, ALU.add).then_inc(frees(name, c), 1)

            def mod_cols(layer, half):
                name = f"modcol{layer}"
                b.filled(name, half)
                cols = bank(name, half)[:, :].rearrange("p (v k r) -> p v k r", v=2, k=KD)
                g = gain((G_N1, G_N2)[half] + layer * KD).unsqueeze(2).to_broadcast([P, KD, 2])
                dve.scalar_tensor_tensor(out=modc[:, layer, 2 * half], in0=cols[:, 0, :, 0:2], scalar=1.0, in1=g, op0=ALU.add, op1=ALU.mult)
                dve.tensor_copy(modc[:, layer, 2 * half + 1], cols[:, 1, :, 0:2]).then_inc(frees(name, half), 1)
                b.drained(name, half)

            def rope(x1, x2, cos, sin, tmp, sig):
                steps.add(dve.tensor_tensor(tmp[0], x1, cos, ALU.mult))
                steps.add(dve.tensor_tensor(tmp[1], x2, sin, ALU.mult))
                steps.add(dve.tensor_tensor(tmp[2], x2, cos, ALU.mult))
                steps.do(dve.tensor_tensor(tmp[3], x1, sin, ALU.mult))
                steps.add(dve.tensor_tensor(x1, tmp[0], tmp[1], ALU.subtract))
                dve.tensor_tensor(x2, tmp[2], tmp[3], ALU.add).then_inc(sig, 1)

            def heads_tmp(off, n, w):
                return [region(off + m * n * w, n, w) for m in range(4)]

            def over_heads(c, n, w):
                return c.unsqueeze(1).to_broadcast([P, n, w])

            def cat_out(name, dst, width):
                for k in range(1, KD, 2):
                    b.filled(name, k)
                    dve.tensor_copy(dst[:, k, :], bank(name, k)[:, 0:width]).then_inc(frees(name, k), 1)

            def add_gated(name, key, gate, x, tmp, width, sig=None):
                b.filled(name, key)
                dve.tensor_tensor(tmp[:, 0:width], bank(name, key)[:, 0:width], gate, ALU.mult).then_inc(frees(name, key), 1)
                b.drained(name, key)
                ins = dve.tensor_tensor(x, x, tmp[:, 0:width], ALU.add)
                if sig is None:
                    steps.do(ins)
                else:
                    ins.then_inc(sig, 1)

            def mix(layer):
                L = str(layer)
                streams = 2 - layer
                for t in range(TT * streams):
                    for c in range(2):
                        cols = slice(c * 512, (c + 1) * 512)
                        add_gated("mix" + L, (c, t), bc[:, t // TT, cols], X[:, t, cols], mix_tmp[:, c], 512, sem("x_mix"))

            def experts(layer):
                L = str(layer)
                moe = "moe" + L
                streams = 2 - layer
                tiles = TT * streams
                rows = streams * CAP
                parts = P // rows
                width = NCOL // parts
                ne = streams * N_EXP
                b.filled("logit" + L, 0)
                dve.tensor_copy(moe_work[0:32 * tiles, 0:P], bank("logit" + L, 0)[0:32 * tiles, 0:P]).then_inc(frees("logit" + L, 0), 1)
                b.filled("logitT" + L, 0)
                groups = lambda v: v[:, 0:tiles * N_EXP].rearrange("p (g e) -> p g e", g=tiles)
                each = lambda v: v[:, 0:tiles].unsqueeze(2).to_broadcast([P, tiles, N_EXP])
                logits = bank("logitT" + L, 0)[:, 0:32 * tiles].rearrange("p (g e) -> p g e", g=tiles)[:, :, 0:N_EXP]
                steps.do(dve.tensor_reduce(lgs[:, 0:tiles], logits, AX.X, ALU.max))
                dve.tensor_tensor(groups(lg), logits, each(lgs), ALU.subtract).then_inc(frees("logitT" + L, 0), 1)
                dve.wait_ge(sem("lgt_exp"), layer + 1)
                steps.do(dve.tensor_reduce(lgs[:, 0:tiles], groups(lge), AX.X, ALU.add))
                steps.do(dve.reciprocal(lgs[:, 0:tiles], lgs[:, 0:tiles]))
                dve.tensor_tensor(groups(moe_aff), groups(lge), each(lgs), ALU.mult).then_inc(sem("aff"), 1)
                b.filled("affT" + L, 0)
                work = moe_work[0:ne, :]
                top = mx2[0:ne, 0:8]
                dve.tensor_copy(work, bank("affT" + L, 0)[0:ne, 0:SEQ]).then_inc(frees("affT" + L, 0), 1)
                b.drained("affT" + L, 0)
                for _ in range(CAP // 8):
                    steps.do(dve.max(top, work))
                    steps.do(dve.match_replace(work, top, work, -1.0))
                dve.tensor_scalar(moe_chosen[0:ne, :], work, 0.0, None, ALU.is_lt).then_inc(sem("chosen"), 1)
                b.filled("selT" + L, 0)
                dve.tensor_copy(mkT[:, 0:2 * ne], bank("selT" + L, 0)[:, 0:2 * ne]).then_inc(frees("selT" + L, 0), 1)
                b.filled("rank" + L, 0)
                b.drained("selT" + L, 0)
                dve.tensor_tensor(pos[:, 0:2 * ne], bank("rank" + L, 0)[:, 0:2 * ne], mkT[:, 0:2 * ne], ALU.mult)\
                    .then_inc(frees("rank" + L, 0), 1)
                b.drained("rank" + L, 0)
                dve.wait_ge(sem("aff"), layer + 1)
                scale, shift = (modc[:, layer, n].rearrange("p k s -> p (k s)") if streams == 2 else modc[:, layer, n, :, 0] for n in (2, 3))
                with steps.loop(GROUPS, MOE_STEPS) as i:
                    b.lap = i * LAP[moe]
                    by_expert = lambda v: v.rearrange("p (e c) -> p e c", e=PER_GROUP)
                    slots = iota.unsqueeze(1).to_broadcast([P, PER_GROUP, CAP])
                    for weigh in (False, True):
                        for tok in range(tiles):
                            at = tok % TT * ne + tok // TT * N_EXP
                            spread = lambda v: v[:, bass.ds(i * PER_GROUP + at, PER_GROUP)].unsqueeze(2).to_broadcast([P, PER_GROUP, CAP])
                            hot = by_expert(moe_oh[:, tok, :])
                            if weigh:
                                dve.wait_ge(sem("hot" + L), i * tiles + tok + 1)
                                dve.tensor_tensor(by_expert(moe_gw[:, tok, :]), hot, spread(moe_aff), ALU.mult).then_inc(sem("gated" + L), 1)
                            else:
                                dve.tensor_tensor(hot, spread(pos), slots, ALU.is_equal).then_inc(sem("hot" + L), 1)
                    for k in range(KD):
                        b.filled("gather" + L, k)
                        for s in range(streams):
                            ks = k * streams + s
                            ins = dve.tensor_scalar(moe_x(streams)[:, k, :, s, :], by_expert(bank("gather" + L, k)[:, s * P:(s + 1) * P]),
                                                    scale[:, ks:ks + 1], shift[:, ks:ks + 1], ALU.mult, ALU.add)
                        ins.then_inc(frees("gather" + L, k), 1)
                    for e in range(PER_GROUP):
                        for c in range(2):
                            b.filled(moe, (e, f"b{c}"))
                            b.drained(moe, (e, f"a{c}"))
                            dve.tensor_tensor(moe_g[:, c, 0:width], moe_sil[:, c, 0:width], bank(moe, (e, f"b{c}"))[:, 0:width], ALU.mult)\
                                .then_inc(frees(moe, (e, f"b{c}")), 1)
                    pieces = 8 // tiles
                    w = D // pieces
                    for n in range(8):
                        t, c = n // pieces, n % pieces
                        cols = slice(c * w, (c + 1) * w)
                        add_gated("comb" + L, n, bc[:, t // TT if streams == 2 else 1, cols], X[:, t, cols], moe_tmp[:, n % 2], w,
                                  sem("x_moe") if n == 7 else None)
                b.lap = 0
                dve.wait_ge(sem("x_moe"), GROUPS * (layer + 1))

            def weights_out(name, u, dst):
                b.filled(name, u)
                steps.do(dve.reciprocal(rl[:, u[1]:u[1] + 1], l[:, u[1]:u[1] + 1]))
                dve.tensor_scalar(dst, bank(name, u)[:, 0:64], rl[:, u[1]:u[1] + 1], None, ALU.mult).then_inc(frees(name, u), 1)

            for c in range(MOD_EARLY):
                mod_chunk(0, c)
            dve.wait_ge(sem("small_in"), 16)
            mod_cols(0, 0)
            norm("n1_0", X, xn4, 4, 4, ht4, A1[0], B1[0])
            dve.wait_ge(sem("ev_in"), 16)
            steps.add(dve.tensor_scalar(ev_nsink, ev_sink[:, :], -1.0, None, ALU.mult))
            for t in range(4):
                b.filled("evz", (1, t))
                b.drained("evz", (1, t))
                v = ev_z[:, t, 512:1024]
                var = mv[:, 2 * t + 1:2 * t + 2]
                steps.do(dve.bn_stats(bn[:, 6 * t:6 * t + 6], v))
                steps.do(dve.bn_aggr(mv[:, 2 * t:2 * t + 2], bn[:, 6 * t:6 * t + 6]))
                dve.tensor_copy(root4[:, t:t + 1], var).then_inc(sem("sgu_var"), 1)
            dve.wait_ge(sem("sgu_root"), 1)
            steps.do(dve.reciprocal(root4, root4))
            for t in range(4):
                v = ev_z[:, t, 512:1024]
                steps.do(dve.tensor_scalar(v, v, mv[:, 2 * t:2 * t + 1], root4[:, t:t + 1], ALU.subtract, ALU.mult))
                dve.tensor_tensor(v, v, ev_sgug[:, :], ALU.mult).then_inc(sem("sgu_v"), 1)
            b.drained("evz", (3, 1))
            for t in range(TT):
                x = ev_z[:, t, 1152:1792].rearrange("p (h d) -> p h d", d=64)
                rope(x[:, :, 0:32], x[:, :, 32:64], over_heads(ev_cos[:, t, :], 10, 32), over_heads(ev_sin[:, t, :], 10, 32),
                     heads_tmp(EV_S, 10, 32), sem("ev_rope"))
                dve.wait_ge(sem("ev_rope"), t + 1)
            for t in range(4):
                b.filled("sgu", t)
                for g in range(4):
                    cols = slice(g * P, (g + 1) * P)
                    ins = dve.scalar_tensor_tensor(out=ev_cat[:, t, 512 + g * P:512 + (g + 1) * P], in0=bank("sgu", t)[:, cols],
                                                   scalar=ev_sgub[:, g:g + 1], in1=ev_z[:, t, cols], op0=ALU.add, op1=ALU.mult)
                ins.then_inc(frees("sgu", t), 1)
            for what, *x in ev_schedule(ATT_LAGS):
                if what == "m":
                    mod_chunk(*x)
                    continue
                if what == "f":
                    if x[1] == 0:
                        dve.tensor_copy(mrow5, mrow[:, 10 * P:12 * P]).then_inc(sem("mod_saved"), 1)
                        mod_cols(0, 1)
                    continue
                kind, u = x
                h, t = EV_UNITS[u]
                first = 0 if t < TT else SEQ
                n = 512 - first
                if kind == "s":
                    b.filled("evatt", ("s", u))
                    if u >= S_BUFS:
                        b.filled("evatt", ("t", u - S_BUFS))
                    dve.tensor_tensor_reduce(ev_s[u % S_BUFS][:, 0:n], bank("evatt", ("s", u))[:, 0:n], ev_win[:, t % TT, first:512], 1.0, -3e38,
                                             ALU.add, ALU.max, mx[:, u:u + 1]).then_inc(frees("evatt", ("s", u)), 1)
                    b.drained("evatt", ("s", u))
                    dve.tensor_scalar(nm[:, u:u + 1], mx[:, u:u + 1], -EV_SCALE, ev_nsink[:, h:h + 1], ALU.mult, ALU.min)\
                        .then_inc(sem("ev_nm"), 1)
                elif kind == "o":
                    dve.wait_ge(sem("ev_ls"), u + 1)
                    steps.do(dve.tensor_tensor(l[:, u:u + 1], l[:, u:u + 1], ls[:, u:u + 1], ALU.add))
                    weights_out("evatt", ("o", u), ev_cat[:, t, h * 64:(h + 1) * 64])
            for half in range(2):
                mod_cols(1, half)
            cat_out("cat0", ev_catt, 512)
            mix(0)
            norm("n2_0", X, moe_xn, 4, 8, moe_ht, A2[0], B2[0])
            experts(0)

            norm("n1_1", X, xn4, 4, 12, ht4, A1[1], B1[1])
            b.drained("odz", (4, 1))
            for t in range(TT):
                gb, gc, hh = (od_zb[:, t, n * 512:(n + 1) * 512] for n in range(3))
                dve.tensor_tensor(gc, gc, hh, ALU.mult).then_inc(sem("conv_u"), 1)
            dve.wait_ge(sem("od_in"), 16)
            for t in range(TT):
                gb, u = od_zb[:, t, 0:512], od_zb[:, t, 512:1024]
                acc, tmp = od_s[0], od_s[1]
                b.filled("conv", (t, 0))
                dve.tensor_tensor(acc, bank("conv", (t, 0))[:, :], od_convw[:, 0, :], ALU.mult).then_inc(frees("conv", (t, 0)), 1)
                steps.do(dve.tensor_tensor(tmp, u, od_convw[:, 1, :], ALU.mult))
                b.drained("conv", (t, 0))
                steps.do(dve.tensor_tensor(acc, acc, tmp, ALU.add))
                b.filled("conv", (t, 1))
                dve.tensor_tensor(tmp, bank("conv", (t, 1))[:, :], od_convw[:, 2, :], ALU.mult).then_inc(frees("conv", (t, 1)), 1)
                b.drained("conv", (t, 1))
                steps.do(dve.tensor_tensor(acc, acc, tmp, ALU.add))
                dve.tensor_tensor(od_cat[:, t, 512:1024], acc, gb, ALU.mult).then_inc(sem("conv_done"), 1)
                dve.wait_ge(sem("conv_done"), t + 1)
            dve.wait_ge(sem("lora_root"), 3)
            steps.do(dve.reciprocal(rstd2[:, :], ss2[:, :]))
            for n in range(6):
                part = od_za[:, n, 0:KV_LORA] if n < TT else od_zc[:, n - TT, 0:KV_LORA] if n < 4 else od_za[:, n - 4, KV_LORA + KR:]
                dve.tensor_scalar(part, part, rstd2[:, n:n + 1], None, ALU.mult).then_inc(sem("lora_n"), 1)
            dve.wait_ge(sem("od_in2"), 16)
            for t in range(TT):
                x = od_za[:, t, KV_LORA:KV_LORA + KR].unsqueeze(1)
                rope(x[:, :, 0:16], x[:, :, 16:32], over_heads(od_cos[:, t, :], 1, 16), over_heads(od_sin[:, t, :], 1, 16),
                     heads_tmp(OD_S + 1024, 1, 16), sem("od_krope"))
                dve.wait_ge(sem("od_krope"), t + 1)
            for j in range(2):
                b.filled("ckvT", j)
                dve.tensor_scalar(od_ckvt[:, j, :], bank("ckvT", j)[:, :], gain(G_KV + j, 1), None, ALU.mult).then_inc(frees("ckvT", j), 1)
            for j in range(3):
                b.filled("cqT", j)
                dve.tensor_scalar(od_cqt[:, j, :], bank("cqT", j)[:, 0:SEQ], gain(G_Q + j, 1), None, ALU.mult).then_inc(frees("cqT", j), 1)
            for t in range(4):
                src = od_za[:, t, KV_LORA:KV_LORA + KR] if t < TT else od_zc[:, t - TT, KV_LORA:]
                kf = od_kf[:, t, :].rearrange("p (h d) -> p h d", h=OD_HEADS)
                dve.tensor_copy(kf[:, :, 64:96], over_heads(src, OD_HEADS, KR)).then_inc(sem("od_kr"), 1)
            b.drained("uq", (1, 1))
            for t in range(TT):
                x = od_q[:, t, :].rearrange("p (h d) -> p h d", h=OD_HEADS)
                rope(x[:, :, 64:80], x[:, :, 80:96], over_heads(od_cos[:, t, :], 8, 16), over_heads(od_sin[:, t, :], 8, 16),
                     heads_tmp(OD_S, 8, 16), sem("od_rope"))
                dve.wait_ge(sem("od_rope"), t + 1)
            for j in range(OD_HEADS // 2):
                b.filled("odqT", j)
                dve.tensor_copy(od_qt[0:OD_DIM, 2 * j:2 * j + 2, :],
                                bank("odqT", j)[0:OD_DIM, :].rearrange("p (n q) -> p n q", n=2)).then_inc(frees("odqT", j), 1)
            for kind, u in pipeline(len(OD_UNITS), ATT_LAGS):
                h, t = OD_UNITS[u]
                if kind == "s":
                    b.filled("odatt", ("s", u))
                    steps.do(dve.tensor_reduce(mx[:, u:u + 1], bank("odatt", ("s", u))[:, :], AX.X, ALU.max))
                    dve.tensor_scalar(nm[:, u:u + 1], mx[:, u:u + 1], -OD_SCALE, None, ALU.mult).then_inc(sem("od_nm"), 1)
                elif kind == "o":
                    weights_out("odatt", ("o", u), od_cat[:, t, h * 64:(h + 1) * 64])
            cat_out("cat1", od_catt, SEQ)
            mix(1)
            norm("n2_1", X, moe_xn, TT, 14, moe_ht, A2[1], B2[1])
            experts(1)

            def last_norm(n_root, n_gain, dst, sig):
                dve.wait_ge(sem("fg_in"), n_gain)
                for t in range(TT):
                    dve.wait_ge(sem("root"), n_root - TT + t + 1)
                    steps.do(dve.reciprocal(rstd[:, t:t + 1], ss[:, t:t + 1]))
                    dve.scalar_tensor_tensor(out=dst[:, t, :], in0=X[:, t, :], scalar=rstd[:, t:t + 1], in1=final_g[n_gain // 32][:, :],
                                             op0=ALU.mult, op1=ALU.mult).then_inc(sig, 1)

            last_norm(16, 16, X, sem("x_final"))
            dve.wait_ge(sem("x_final"), TT)

            with steps.loop(B2_LAYERS, B2_STEPS) as i:
                b.lap = i * LAP["b2"]
                for n, off in enumerate((G_MIX, G_MLP)):
                    dve.tensor_copy(layer_gain[:, n * KD:(n + 1) * KD], small[:, bass.ds(i * KD + off, KD)]).then_inc(sem("b2_gain"), 1)

                def scale_tokens(xn, at):
                    for t in range(TT):
                        dve.wait_ge(sem("b2_root"), i * 4 + at + t + 1)
                        steps.do(dve.reciprocal(rstd[:, t:t + 1], ss[:, t:t + 1]))
                        dve.tensor_scalar(xn[:, t, :], X[:, t, :], rstd[:, t:t + 1], None, ALU.mult).then_inc(sem("b2_xn"), 1)

                def low_part(dst, whole, high, sig):
                    dve.tensor_tensor(dst, whole, high.bitcast(F32), ALU.subtract).then_inc(sig, 1)

                def split_weights(name, k, m):
                    dve.wait_ge(sem("w_hi"), i * len(PIECES) + PIECE_AT[name, k, m] + 1)
                    src, high, low = piece_of(name, k, m)
                    low_part(low, src, high, sem("w_lo"))

                def split_tokens(event, pair):
                    dve.wait_ge(sem("a_hi"), i * 12 + 4 * event + pair + 1)
                    at = slice(2 * pair, 2 * pair + 2)
                    low_part(a_lo[:, at, :], b2_ht[:, at, :], a_hi[:, at, :], sem("a_lo"))

                def gain_out(name, off, event):
                    dve.wait_ge(sem("b2_gain"), i * 2 + 2)
                    for k in range(1, KD + 2, 2):
                        if k < KD:
                            b.filled(name, k)
                            dve.tensor_scalar(b2_ht[:, k, :], bank(name, k)[:, 0:SEQ], layer_gain[:, off + k:off + k + 1], None, ALU.mult)\
                                .then_inc(frees(name, k), 1)
                        if k > 1:
                            split_tokens(event, k // 2 - 1)

                def rope2(wh, t):
                    dve.wait_ge(sem("b2_in2"), 16)
                    b.drained("qkv", (2 + 3 * wh, 1))
                    x = (b2_q, b2_k)[wh][:, t, :].rearrange("p (h d) -> p h d", d=64)[:, 0:B2_ROT, :]
                    rope(x[:, :, 0:8], x[:, :, 8:16], over_heads(b2_cos[:, t, :], B2_ROT, 8),
                         over_heads(b2_sin[:, t, :], B2_ROT, 8), heads_tmp(B2_RTMP, B2_ROT, 8), sem("b2_rope"))
                    dve.wait_ge(sem("b2_rope"), i * 4 + wh * 2 + t + 1)

                scale_tokens(region(B2_XN1, TT, D), 0)
                for what, name, k, m in split_order(ATT_CHUNKS):
                    if what == "piece":
                        split_weights(name, k, m)
                    elif what == "begin":
                        gain_out("nmix", 0, 0)
                    elif what == "late" and k in (2, 3, 5, 6):
                        rope2(k // 4, k % 3 != 2)
                def softmax_unit(kind, u, n):
                    unit = AB_UNITS[u]
                    which, h, t = unit
                    per_bank = ab_keys_per_bank(*unit)
                    if kind == "s":
                        mask = (b2_amask if which == "A" else b2_bmask)[t]
                        w = P * len(per_bank[n])
                        b.filled("ab", (kind, u, n))
                        if u >= S_BUFS and n == 0:
                            b.filled("ab", ("t", u - S_BUFS, len(ab_keys_per_bank(*AB_UNITS[u - S_BUFS])) - 1))
                        dve.memset(idle[:, u + 20 * n:u + 20 * n + 1], 0.0)
                        top = mx[:, u:u + 1] if len(per_bank) == 1 else mx2[:, 2 * u + n:2 * u + n + 1]
                        dve.tensor_tensor_reduce(b2_s[:, u % S_BUFS, n * 512:n * 512 + w], bank("ab", (kind, u, n))[:, 0:w],
                                                 mask[:, n * 512:n * 512 + w], 1.0, -3e38, ALU.add, ALU.max, top)\
                            .then_inc(frees("ab", (kind, u, n)), 1)
                        if n == len(per_bank) - 1:
                            b.drained("ab", (kind, u, n))
                            if n:
                                steps.do(dve.tensor_reduce(mx[:, u:u + 1], mx2[:, 2 * u:2 * u + 2], AX.X, ALU.max))
                            dve.tensor_scalar(nm[:, u:u + 1], mx[:, u:u + 1], -B2_SCALE, None, ALU.mult).then_inc(sem("b2_nm"), 1)
                    elif kind == "o":
                        at = h * 64 + (0 if which == "A" else 256)
                        weights_out("ab", (kind, u, n), b2_ocat[:, t, at:at + 64])

                def stick_unit(kind, u, n):
                    buf = b2_c[:, u % C_BUFS, :]
                    zm, sp = buf[:, 0:384], buf[:, 384:768]
                    if kind == "s":
                        b.filled("c", (kind, u, n))
                        if u >= C_BUFS:
                            b.filled("c", ("o", u - C_BUFS, 1))
                        dve.scalar_tensor_tensor(out=zm, in0=bank("c", (kind, u, n))[:, 0:384], scalar=B2_SCALE, in1=b2_cmask[:, :],
                                                 op0=ALU.mult, op1=ALU.add).then_inc(frees("c", (kind, u, n)), 1)
                        b.drained("c", (kind, u, n))
                        dve.scalar_tensor_tensor(out=sp, in0=zm, scalar=-1.0, in1=zm, op0=ALU.mult, op1=ALU.min).then_inc(sem("c_abs"), 1)
                    elif kind == "p":
                        dve.wait_ge(sem("c_ln"), i * len(C_UNITS) + u + 1)
                        dve.scalar_tensor_tensor(out=sp, in0=zm, scalar=0.0, in1=sp, op0=ALU.max, op1=ALU.add)\
                            .then_inc(sem("c_softplus"), 1)
                    elif kind == "c":
                        b.filled("c", (kind, u, n))
                        dve.tensor_tensor(zm, zm, bank("c", (kind, u, n))[:, 0:384], ALU.subtract).then_inc(frees("c", (kind, u, n)), 1)

                dve.wait_ge(sem("b2_in"), 16)
                for which, kind, u, n in b2_schedule(ATT_LAGS, C_LAGS_DVE):
                    (softmax_unit if which == "ab" else stick_unit)(kind, u, n)
                def split_bank(name, j, high, low, sig):
                    dve.wait_ge(sig, i * 4 + j + 1)
                    at = slice(2 * j, 2 * j + 2)
                    low_part(low[:, at, :], bank(name, j)[:, :].rearrange("p (n q) -> p n q", n=2), high[:, at, :], frees(name, j))

                for what, name, k, m in split_order(MLP_CHUNKS):
                    if what == "piece":
                        split_weights(name, k, m)
                    elif what == "begin":
                        for pair in range(KD // 2):
                            split_tokens(1, pair)
                        for j in range(4):
                            split_bank("ocat", j, o_hi, o_lo, sem("ocat_hi"))
                    elif what == "out" and name == "merge" and k % 4 == 3:
                        c = k // 4
                        for n in range(3):
                            for t in range(TT):
                                gate, key = (c, "gate", n, t), (c, "branch", n, t)
                                b.filled("merge", key)
                                b.drained("merge", gate)
                                part = b2_sig[:, n, t, :]
                                dve.tensor_tensor(part, bank("merge", key)[:, :], part, ALU.mult).then_inc(frees("merge", key), 1)
                        for t in range(TT):
                            total = b2_merged[:, t, c * 512:(c + 1) * 512]
                            b.drained("merge", (c, "branch", 2, t))
                            b.drained("merge", (c, "branch", 1, t))
                            steps.do(dve.tensor_tensor(total, b2_sig[:, 0, t, :], b2_sig[:, 1, t, :], ALU.add))
                            dve.tensor_tensor(total, total, b2_sig[:, 2, t, :], ALU.add).then_inc(sem("b2_merged"), 1)
                    elif what == "late" and (name, k) == ("merge", 7):
                        for j in range(4):
                            split_bank("mergeT", j, a_hi, a_lo, sem("merge_hi"))
                    elif what == "out" and name == "wo":
                        at, w = sum(WO_PIECES[:k]), WO_PIECES[k]
                        for t in range(TT):
                            b.filled("wo", (k, t))
                            x = X[:, t, at:at + w]
                            dve.tensor_tensor(x, x, bank("wo", (k, t))[:, 0:w], ALU.add).then_inc(frees("wo", (k, t)), 1)
                    elif what == "late" and (name, k) == ("wo", 2):
                        scale_tokens(region(B2_XN2, TT, D), 2)
                        gain_out("nmlp", KD, 2)
                    elif what == "out" and name == "up":
                        for n in range(2):
                            b.drained("up", (k, n))
                            dve.tensor_tensor(b2_sq[:, n, :], b2_sq[:, n, :], b2_sq[:, n, :], ALU.mult).then_inc(sem("b2_squared"), 1)
                    elif what == "late" and name == "up":
                        for n in range(2):
                            dve.wait_ge(sem("hidden_hi"), i * (2 * N_FF) + 2 * k + n + 1)
                            at = slice(k % 2 * 4 + 2 * n, k % 2 * 4 + 2 * n + 2)
                            low_part(o_lo[:, at, :], b2_sq[:, n, :].rearrange("p (m q) -> p m q", m=2), o_hi[:, at, :], sem("b2_hidden"))
                    elif what == "out" and name == "down":
                        for t in range(TT):
                            for h in range(2):
                                b.filled("down", (k, t, h))
                                if k:
                                    b.drained("down", (k - 1, t, h))
                                x = X[:, t, h * 512:(h + 1) * 512]
                                dve.tensor_tensor(x, x, bank("down", (k, t, h))[:, :], ALU.add).then_inc(frees("down", (k, t, h)), 1)
            b.lap = LAP["b2"] * (B2_LAYERS - 1)
            b.drained("down", (N_FF - 1, 1, 1))
            last_norm(18, 32, xn4, sem("result"))


def _k_major(w):
    k, n = w.shape
    return w.reshape(k // P, P, n).transpose(1, 0, 2).reshape(P, -1)

def _lay_out(a):
    f = np.float32
    stream = np.zeros((N_CHUNKS, P, CHUNK), f)

    def put(at, *parts):
        off = 0
        for part in parts:
            stream[at, :, off:off + part.shape[1]] = part
            off += part.shape[1]

    def columns(name, w, width=NCOL, first=0):
        for n in range(w.shape[1] // width):
            put(CHUNK_AT[name, first + n], _k_major(w[:, n * width:(n + 1) * width]))

    heads = [h + 4 * s for h in range(4) for s in range(2)]
    in0 = a["ev_w_in"][0]
    kv_cols, q_cols, g_cols = in0[:, :256], in0[:, 256:768].reshape(D, 8, 64)[:, heads].reshape(D, 512), in0[:, 768:]
    in0 = np.concatenate([g_cols, kv_cols[:, 128:], kv_cols[:, :128], q_cols], 1)
    out0 = a["ev_w_out"][0]
    out0 = np.concatenate([out0[:512].reshape(8, 64, D)[heads].reshape(512, D), out0[512:]], 0)
    in1 = a["od_w_in"][0]
    for layer in range(2):
        columns(f"mod{layer}", a["mod_w"][layer])
        at = CHUNK_AT[f"moe{layer}", 0]
        for e in range(N_EXP):
            w1, w3, w2 = (a[n][layer, e] for n in ("exp_w1", "exp_w3", "exp_w2"))
            for c in range(2):
                put(at + 6 * e + 2 * c, _k_major(w1[:, c * 512:(c + 1) * 512]))
                put(at + 6 * e + 2 * c + 1, _k_major(w3[:, c * 512:(c + 1) * 512]))
                put(at + 6 * e + 4 + c, _k_major(w2[c * 512:(c + 1) * 512]))
    columns("evz", in0[:, :1536])
    put(CHUNK_AT["evz", 3], _k_major(in0[:, 1536:]))
    columns("mix0", out0)
    columns("odz", in1[:, :4 * NCOL])
    put(CHUNK_AT["odz", 4], _k_major(in1[:, 4 * NCOL:]), _k_major(a["od_w_uq"][0]))
    put(CHUNK_AT["ukv", 0], _k_major(a["od_w_ukv"][0]))
    columns("mix1", a["od_w_out"][0])
    per = CHUNK_LAP["b2"] * SLOTS
    for i in range(B2_LAYERS):
        w_in = a["w_in_2"][i]
        w_out = np.concatenate([a["w_out_a_2"][i], a["w_out_b_2"][i], a["w_out_c_2"][i]], 0)
        for c in range(9):
            put(CHUNK_AT["qkv", c] + i * per, _k_major(w_in[:, c * NCOL:(c + 1) * NCOL]))
        for c in range(2):
            cols = slice(c * NCOL, (c + 1) * NCOL)
            put(CHUNK_AT["merge", 4 * c + 3] + i * per, _k_major(w_out[:, cols]))
            for g in range(3):
                put(CHUNK_AT["merge", 4 * c + g] + i * per, _k_major(w_in[:, 3 * B2_W + g * D:3 * B2_W + (g + 1) * D][:, cols]))
        at = 0
        for c, w in enumerate(WO_PIECES):
            put(CHUNK_AT["wo", c] + i * per, _k_major(a["w_o_2"][i][:, at:at + w]))
            at += w
        for j in range(N_FF):
            put(CHUNK_AT["up", j] + i * per, _k_major(a["w_up_2"][i][:, j * 512:(j + 1) * 512]))
            put(CHUNK_AT["down", j] + i * per, _k_major(a["w_down_2"][i][j * 512:(j + 1) * 512]))

    const = shape_constants()
    cols = lambda v: v.reshape(-1, P).T
    rows = lambda v: np.broadcast_to(v.reshape(1, -1), (P, v.size))
    small = [cols(a[n][i]) for n in ("norm1_g", "norm2_g", "norm_mix_2", "norm_mlp_2") for i in range(2)]
    small += [cols(a["od_q_norm_g"][0]), cols(a["od_kv_norm_g"][0])]
    small += [_k_major(a["router_w"][i]) for i in range(2)] + [np.zeros((P, N_EXP), f)]
    return {
        "stream": stream,
        "base": const["base"],
        "small": np.concatenate(small, 1),
        "ccols": np.concatenate([np.stack([cols(a["c"][0]), cols(a["c_ctx"])], 2), np.zeros((P, KD, 30), f)], 2),
        "x_in": np.concatenate([a["x"][0], a["ctx"][0]], 0).reshape(2 * TT, P, D).transpose(1, 0, 2),
        "modb": np.repeat(a["mod_b"].reshape(2, 12, 4, P).transpose(0, 2, 1, 3).reshape(2, 4, 1, 12 * P), 32, 2).reshape(2, P, 12 * P),
        "ev_pack": np.concatenate([const["win"], a["ev_sgu_w"][0].transpose(2, 0, 1).reshape(P, -1), rows(a["ev_sgu_norm_g"][0]),
                                   a["ev_sgu_b"][0].T, rows(a["ev_sink"][0][heads]), const["ev_rope"]], 1),
        "od_rope": const["od_rope"],
        "od_pack": np.concatenate([const["shift"], rows(a["od_conv_w"][0])], 1),
        "b2_masks": const["b2_masks"],
        "b2_rope": const["b2_rope"],
        "gains": np.stack([rows(a["final_g"]), rows(a["norm_final_2"])], 0),
    }

def kernel(**inputs):
    import concourse.bacc as bacc
    from concourse.bass_utils import run_bass_kernel_spmd

    a = {k: np.asarray(v) for k, v in inputs.items()}
    arrays = {"in_" + k: np.ascontiguousarray(v) for k, v in _lay_out(a).items()}
    nc = bacc.Bacc("TRN2", target_bir_lowering=False, num_devices=1)
    args = [nc.dram_tensor(n, v.shape, F32, kind="ExternalInput").ap() for n, v in arrays.items()]
    args.append(nc.dram_tensor("out", (1, SEQ, D), F32, kind="ExternalOutput").ap())
    program(nc, *args)
    r = run_bass_kernel_spmd(nc, [arrays], core_ids=[0])
    return r.results[0]["out"]
```

```python
from contextlib import ExitStack, contextmanager

import numpy as np

import concourse.bass as bass
from concourse import mybir

F32 = mybir.dt.float32
F32R = mybir.dt.float32r
ALU = mybir.AluOpType
ACT = mybir.ActivationFunctionType
AX = mybir.AxisListType

P = 128
D = 1024
SEQ = 256
TT = SEQ // P
KD = D // P
EPS = 1e-6
NEG = -1e30
CHUNK = 4096
SLOTS = 6
BANKS = 8
NCOL = CHUNK // KD
GRID_W = 64

N_EXP = 16
CAP = 2 * SEQ // N_EXP
PER_GROUP = P // CAP
GROUPS = N_EXP // PER_GROUP

EV_PAIRS = 4
EV_SCALE = 64 ** -0.5
WINDOW = 128
OD_HEADS = 8
OD_DIM = 96
OD_SCALE = OD_DIM ** -0.5
Q_LORA, KV_LORA, KR = 384, 256, 32
ZA_W = KV_LORA + KR + Q_LORA
ZB_W = 3 * 512
OD_TAIL = ZA_W + ZB_W - 4 * NCOL
UQ_W = OD_HEADS * OD_DIM

B2_HEADS = 24
B2_ROT = 18
B2_PAIRS = B2_HEADS // 2
B2_W = B2_HEADS * 64
B2_SCALE = 64 ** -0.5
B2_LAYERS = 2
WO_PIECES = (384, 384, 256)
N_FF = 8
X_MOE = (GROUPS * 2 * TT, GROUPS * 3 * TT)
MOE_STEPS, B2_STEPS = (4, 6), 52


def steps_of(n, stages):
    last = max(lag for _, lag in stages)
    return [[(name, step - lag) for name, lag in stages if 0 <= step - lag < n] for step in range(n + last)]

def pipeline(n, stages):
    return [x for step in steps_of(n, stages) for x in step]

ATT_LAGS = [("s", 0), ("t", 3), ("o", 5)]
ATT_LAGS_ACT = [("t", 3), ("s", 0), ("o", 5)]
S_BUFS = 4
EV_UNITS = [(h, t) for t in range(2 * TT) for h in range(2 * EV_PAIRS)]
ODZ_ORDER = (1, 2, 3, 4, 0)
OD_UNITS = [(h, t) for t in range(TT) for h in range(OD_HEADS)]
AB_UNITS = [("A", h, t) for h in range(4) for t in range(TT)] + [("B", h, t) for h in range(6) for t in range(TT)]
C_UNITS = list(range(6))

def ab_keys(kind, h, t):
    heads = [4 * g + h for g in range(3)] if kind == "A" else [12 + h]
    return [(hd, kt) for hd in heads for kt in range(t + 1)]

def ab_keys_per_bank(kind, h, t):
    keys = ab_keys(kind, h, t)
    return [keys[i:i + 4] for i in range(0, len(keys), 4)]

MOD_EARLY = 4
MOD_IN_EVZ = {**{(c, k): 1 for c in range(2) for k in (1, 3, 5, 7)}, (2, 2): 4, (3, 2): 1}
EV_MOD = [("m", 0, c) for c in range(MOD_EARLY, 12)] + [("f", 0, n) for n in range(5)] + [("m", 1, c) for c in range(12)]

def evz_schedule(late=0):
    left, due = list(EV_MOD), []
    for c in range(4):
        for k in range(KD):
            yield "w", c, k
            if c and k == 1:
                yield from (("z", c - 1, t) for t in range(4))
            n = MOD_IN_EVZ.get((c, k), 0)
            due.append(left[:n])
            del left[:n]
            if len(due) > late:
                yield from due.pop(0)
    for items in due:
        yield from items
    yield from (("z", 3, t) for t in range(4))

def odz_schedule():
    before = None
    for c in ODZ_ORDER:
        for k in range(KD):
            yield "w", c, k
            if before is not None and k == 1:
                yield from (("z", before, t) for t in range(z_tiles("odz", before)))
        before = c
    yield "tail", None, None
    yield from (("z", before, t) for t in range(z_tiles("odz", before)))

def z_tiles(name, c):
    return 4 if name in ("evz", "mix0") or (name, c) == ("odz", 0) else TT

def ev_schedule(lags):
    left = EV_MOD[sum(MOD_IN_EVZ.values()):]
    for step in steps_of(len(EV_UNITS), lags):
        yield from (("a", *x) for x in step)
        yield from left[:1]
        del left[:1]
    assert not left

C_STEPS = [[("s", 2 * n), ("s", 2 * n + 1)] for n in range(3)] + [[("l", u) for u in C_UNITS], [("p", u) for u in C_UNITS] + [("c", 0)]]
C_STEPS += [[("c", u + 1), ("o", u)] for u in range(5)] + [[("o", 5)]]

def b2_schedule(ab_lags, c_kinds="sco"):
    c_steps = list(C_STEPS)
    for i, step in enumerate(steps_of(len(AB_UNITS), ab_lags)):
        for name, u in step:
            for n in range(1 if name == "o" else len(ab_keys_per_bank(*AB_UNITS[u]))):
                yield "ab", name, u, n
        if i >= 2 and i % 2 == 0 and c_steps:
            for name, u in c_steps.pop(0):
                if name in c_kinds:
                    for n in range(TT if name == "o" else 1):
                        yield "c", name, u, n
    assert not c_steps

FF_ORDER = pipeline(N_FF, [("up", 0), ("down", 1)])

TICKET = {}
LAP = {}

def _tickets():
    n = 0

    def stage(name, keys):
        nonlocal n
        for k in (range(keys) if isinstance(keys, int) else keys):
            TICKET[name, k] = n
            n += 1

    def repeated(name, first, times):
        nonlocal n
        per = n - first
        assert per % BANKS == 0, (name, per)
        LAP[name] = per // BANKS
        n = first + per * times

    def norm(name):
        stage(name, KD)

    for layer in range(2):
        streams = 2 if layer == 0 else 1
        L = str(layer)
        if layer == 0:
            stage("mod0", range(MOD_EARLY))
            stage("modcol0", [0])
        else:
            stage("modrow1", 4)
        norm("n1_" + L)
        if layer == 0:
            def mixed(name, what, x):
                if what == "a":
                    stage(name, [tuple(x)])
                elif what == "w":
                    stage(name, [(x[0], t) for t in range(4)] if x[1] == 0 else [])
                elif what == "z":
                    pass
                elif what == "m":
                    stage(f"mod{x[0]}", [x[1]])
                elif x[1] == 0:
                    stage("modcol0", [1])
                else:
                    stage("modrow0", [x[1] - 1])

            for what, *x in evz_schedule():
                mixed("evz", what, x)
            stage("sgu", 4)
            stage("evqk", 1 + EV_PAIRS)
            for what, *x in ev_schedule(ATT_LAGS):
                mixed("evatt", what, x)
            stage("modcol1", 2)
        else:
            for c in ODZ_ORDER:
                stage("odz", [(c, t) for t in range(z_tiles("odz", c))])
            stage("conv", [(t, d) for t in range(TT) for d in range(2)])
            stage("ckvT", 2)
            stage("cqT", 3)
            stage("uq", [(p, t) for p in range(2) for t in range(TT)])
            stage("ukv", [(p, t) for p in range(2) for t in range(4)])
            stage("odkT", OD_HEADS)
            stage("odqT", OD_HEADS // 2)
            stage("odatt", pipeline(len(OD_UNITS), ATT_LAGS))
        stage("cat" + L, KD)
        stage("mix" + L, [(c, t) for c in range(2) for t in range(2 * streams)])
        norm("n2_" + L)
        stage("logit" + L, 1)
        stage("logitT" + L, 1)
        stage("affT" + L, 1)
        if layer == 0:
            stage("modrow5", 4)
        stage("selT" + L, 1)
        stage("rank" + L, 1)
        first = n
        stage("gather" + L, KD)
        for e in range(PER_GROUP):
            stage("moe" + L, [(e, k) for k in ("gate", "a0", "b0", "a1", "t0", "b1", "y", "t1")])
        stage("comb" + L, 8)
        repeated("moe" + L, first, GROUPS)
    first = n
    norm("nmix")
    stage("qkv", [(c, t) for c in range(9) for t in range(TT)])
    stage("qkT", [(w, j) for w in range(2) for j in range(B2_PAIRS // 2)])
    for which, *key in b2_schedule(ATT_LAGS):
        stage(which, [tuple(key)])
    stage("ocat", 4)
    stage("merge", [(c, what, k, t) for c in range(2) for what in ("gate", "branch") for k in range(3) for t in range(TT)])
    stage("mergeT", 4)
    stage("wo", [(c, t) for c in range(3) for t in range(TT)])
    norm("nmlp")
    for which, j in FF_ORDER:
        stage(which, [(j, 0), (j, 1)] if which == "up" else [(j, t, h) for t in range(TT) for h in range(2)])
    repeated("b2", first, B2_LAYERS)

_tickets()

CHUNK_AT = {}
CHUNK_LAP = {}

def _chunks():
    n = 0

    def put(name, count):
        nonlocal n
        for k in range(count):
            CHUNK_AT[name, k] = n
            n += 1

    def repeated(name, first, times):
        nonlocal n
        per = n - first
        assert per % SLOTS == 0, (name, per)
        CHUNK_LAP[name] = per // SLOTS
        n = first + per * times

    for c in range(MOD_EARLY):
        CHUNK_AT["mod0", c] = c
    n = MOD_EARLY
    order = [("evz", x[0]) if what == "w" else (f"mod{x[0]}", x[1])
             for what, *x in list(evz_schedule()) + EV_MOD[sum(MOD_IN_EVZ.values()):] if what == "m" or what == "w" and x[1] == 0]
    for key in order:
        CHUNK_AT[key] = n
        n += 1
    put("mix0", 2)
    first = n
    put("moe0", 6 * PER_GROUP)
    repeated("moe0", first, GROUPS)
    for c in ODZ_ORDER:
        CHUNK_AT["odz", c] = n
        n += 1
    put("ukv", 1)
    put("mix1", 2)
    first = n
    put("moe1", 6 * PER_GROUP)
    repeated("moe1", first, GROUPS)
    first = n
    put("qkv", 9)
    put("merge", 8)
    put("wo", 3)
    for which, j in FF_ORDER:
        CHUNK_AT[which, j] = n
        n += 1
    repeated("b2", first, B2_LAYERS)
    return n

N_CHUNKS = _chunks()

Z_CHUNKS = [("evz", c) for c in range(4)] + [("mix0", c) for c in range(2)] + [("odz", c) for c in ODZ_ORDER] + [("mix1", c) for c in range(2)]
Z_PIECES = [(name, c, k) for name, c in Z_CHUNKS for k in range(KD)]
Z_AT = {piece: n for n, piece in enumerate(Z_PIECES)}
Z_BUFS = {"evz": 2, "mix0": 3, "odz": 3, "mix1": 3}
EARLY_SPLIT = 2
Z_FIRST = {name: min(n for n, x in enumerate(Z_PIECES) if x[0] == name) for name in Z_BUFS}
Z_USED_UP_TO = [sum(k < KD - 1 for _, _, k in Z_PIECES[:n + 1]) for n in range(len(Z_PIECES))]

def early_split(name, c, k):
    return Z_AT[name, c, k] < Z_FIRST[name] + EARLY_SPLIT

def z_width(name, c):
    return {("evz", 3): 256, ("odz", 4): OD_TAIL}.get((name, c), 512)

PIECE = 1024
PIECES_PER_CHUNK = CHUNK // PIECE
PIECE_BUFS = 3
ATT_CHUNKS = [("qkv", c) for c in range(9)]
MLP_CHUNKS = [("merge", c) for c in range(8)] + [("wo", c) for c in range(3)] + FF_ORDER
BRANCHES = ((0, 2), (2, 5), (5, 8))

def fills_last(name, k, m):
    last = m == PIECES_PER_CHUNK - 1
    if name == "merge" and k % 4 == 3:
        return ("merge", (k // 4, "branch", 0 if m == 0 else 2, 1)) if m == 0 or last else None
    if name == "merge":
        return ("merge", (k // 4, "gate", k % 4, 1)) if last else None
    if name == "up":
        return ("up", (k, m // 2)) if m % 2 else None
    if name == "down":
        return ("down", (k, 1, 1)) if last else None
    return (name, (k, 1)) if last else None

PIECES = [(name, k, m) for name, k in ATT_CHUNKS + MLP_CHUNKS for m in range(PIECES_PER_CHUNK)]
PIECE_AT = {piece: n for n, piece in enumerate(PIECES)}
assert len(PIECES) % PIECE_BUFS == 0
USED_UP_TO = [sum(fills_last(*x) is None for x in PIECES[:n + 1]) for n in range(len(PIECES))]

def split_order(chunks):
    before = None
    for name, k in chunks:
        for m in range(PIECES_PER_CHUNK):
            yield "piece", name, k, m
            if m == 1 and before:
                yield "out", *before, None
            elif m == 2:
                yield ("late", *before, None) if before else ("begin", None, None, None)
        before = (name, k)
    yield "out", *before, None
    yield "late", *before, None


def _rope(n_freq_total, pos_pairs):
    c = np.cos(pos_pairs).astype(np.float32).reshape(TT, P, -1).transpose(1, 0, 2)
    s = np.sin(pos_pairs).astype(np.float32).reshape(TT, P, -1).transpose(1, 0, 2)
    return np.concatenate([c.reshape(P, -1), s.reshape(P, -1)], 1)

def _axial(rot):
    rows = SEQ // GRID_W
    row = np.repeat(np.arange(rows, dtype=np.float32), GRID_W)
    col = np.tile(np.arange(GRID_W, dtype=np.float32), rows)
    n = rot // 4
    inv = np.power(np.float32(10000.0), -np.arange(n, dtype=np.float32) / np.float32(n)).astype(np.float32)
    return _rope(2 * n, np.concatenate([row[:, None] * inv, col[:, None] * inv], 1).astype(np.float32))

def _partial():
    inv = np.exp(np.float32(-np.log(500000.0)) * np.arange(0, 16, 2, dtype=np.float32) / np.float32(16))
    return _rope(8, (np.arange(SEQ, dtype=np.float32)[:, None] * inv.astype(np.float32)[None, :]).astype(np.float32))

def shape_constants():
    p = np.arange(P)[:, None]
    q = np.arange(P)[None, :]
    f = np.float32
    base = np.concatenate([(p == q).astype(f), (p <= q).astype(f), (p >= q).astype(f), np.ones((P, P), f),
                           np.broadcast_to(np.arange(1, CAP + 1, dtype=f), (P, CAP))], 1)
    keys = np.arange(SEQ)[None, :]
    win = []
    for t in range(TT):
        qp = t * P + p
        win += [np.where(np.abs(keys - qp) <= WINDOW, 0, NEG).astype(f), np.zeros((P, SEQ), f)]
    shift = np.concatenate([(p == q - 1), (p == P - 1) & (q == 0), (p == q + 1), (p == 0) & (q == P - 1)], 1).astype(f)
    amask = []
    for t in range(TT):
        kk = np.arange((t + 1) * P)[None, :]
        d = t * P + p - kk
        for span, dil in ((128, 1), (512, 4), (2048, 16)):
            amask.append(np.where((d >= 0) & (d <= span) & (d % dil == 0), 0, NEG).astype(f))
    bmask = np.where(keys <= P + p, 0, NEG).astype(f)
    cmask = np.concatenate([np.where(p < keys, 0, NEG), np.where(p < q, 0, NEG)], 1).astype(f)
    return {"base": base, "win": np.concatenate(win, 1), "ev_rope": _axial(64), "od_rope": _axial(32),
            "shift": shift, "b2_masks": np.concatenate(amask + [bmask, cmask], 1), "b2_rope": _partial()}

IDENT, TRI_LE, TRI_GE, ONES, IOTA = 0, 128, 256, 384, 512
BASE_W = 544
G_N1, G_N2, G_MIX, G_MLP, G_Q, G_KV = 0, 16, 32, 48, 64, 67
ROUTER = 69
SMALL_W = ROUTER + 2 * KD * N_EXP + N_EXP
ARENA = 22668

XN, BC, MROW, MROW5 = 4096, 11264, 13312, 14848
EV_CAT, EV_Z, EV_CATT = 0, 4096, 4096
EV_QT, EV_KT, EV_S, EV_PT = 15360, 17408, 17920, 19456
EV_WIN, EV_SGUW, EV_SGUG, EV_SGUB, EV_SINK, EV_ROPE = 20480, 21504, 22016, 22528, 22532, 22540
EV_PACK_W = 2188
Z_HI, Z_LO, Z_TOKENS = 0, 15360, 8192
MIX_WEIGHTS = ((8192, 8704), (9216, 9728), (10240, 10752))
EV_WEIGHTS = ((19456, 19968), (20480, 20992))
OD_WEIGHTS = ((13312, 14336), (7040, 19456), (6528, 22016))
OD_CONV = 6016
MOE_XN, MOE_HT, MOE_YST, MOE_OH, MOE_AFF = 0, 4096, 4096, 8192, 10240
MOE_GW, MOE_XST, MOE_G, MOE_GTR, MOE_GTST = 8704, 17408, 19456, 20480, 21504
MOE_W = 22016
MOE_TMP, MIX_TMP = 6144, 19456
OD_KT, OD_ZA, OD_ZC, OD_CQT, OD_CKVT, OD_ZB, OD_KF, OD_ROPE = 0, 4096, 5440, 6016, 6784, 7808, 7808, 10880
OD_QT, OD_S, OD_PT, OD_SHIFT, OD_CONVW, OD_Q, OD_CAT = 15360, 17408, 18944, 19968, 20480, 20480, 13312
B2_Q, B2_K, B2_V, B2_QT, B2_KT = 0, 3072, 6144, 9216, 12288
B2_S, B2_PT, B2_MASK, B2_ROPE, B2_RTMP = 15360, 18432, 19968, 21760, 21792
B2_CBUF = [2048 + 768 * u for u in range(5)] + [21792]
B2_XN1, B2_XN2, B2_OCAT, B2_SIG, B2_MERGED, B2_SQ = 0, 7168, 0, 0, 7168, 0
B2_AH, B2_AL, B2_OH, B2_OL, B2_WH, B2_WL = 9216, 11264, 3072, 5120, 13824, 16896
FINAL_G = (15360, 1024)

def program(nc, stream, base_c, small_c, ccols, x_in, modb, ev_pack, od_rope, od_pack, b2_masks, b2_rope, gains, out):
    with ExitStack() as ctx:
        def sb(name, shape):
            return ctx.enter_context(nc.sbuf_tensor(name, shape, F32))

        sems = {}

        def sem(name):
            if name not in sems:
                sems[name] = ctx.enter_context(nc.semaphore(name))
            return sems[name]

        ring = sb("ring", [P, SLOTS, CHUNK])
        X = sb("x", [P, 2 * TT, D])
        base = sb("base", [P, BASE_W])
        small = sb("small", [P, SMALL_W])
        sc = sb("silu_c", [P, KD, 32])
        modc = sb("mod_columns", [P, 2, 4, KD, 2])
        A1, B1, A2, B2 = ([modc[:, layer, n] for layer in range(2)] for n in range(4))
        stat = sb("statistics", [P, 584])
        arena_at = nc.sbuf_base
        arena = sb("arena", [P, ARENA])
        psum = [ctx.enter_context(nc.psum_tensor(f"bank{b}", [P, 512], F32)) for b in range(BANKS)]

        slot_loaded = [sem(f"slot_loaded{s}") for s in range(SLOTS)]
        slot_free = [sem(f"slot_free{s}") for s in range(SLOTS)]
        filled_sem = [sem(f"filled{b}") for b in range(BANKS)]
        drained_sem = [sem(f"drained{b}") for b in range(BANKS)]

        def region(off, *shape):
            n = int(np.prod(shape))
            v = arena[:, off:off + n]
            if len(shape) == 2:
                return v.rearrange("p (a b) -> p a b", a=shape[0])
            if len(shape) == 3:
                return v.rearrange("p (a b c) -> p a b c", a=shape[0], b=shape[1])
            return v

        def parts(name, off, *shape):
            return nc.alloc_sbuf_tensor_at(name, [P, *shape], F32R, offset=arena_at + 4 * off)

        ident = base[:, IDENT:IDENT + P]
        tri_le = base[:, TRI_LE:TRI_LE + P]
        tri_ge = base[:, TRI_GE:TRI_GE + P]
        ones = base[:, ONES:ONES + P]
        iota = base[:, IOTA:IOTA + CAP]

        def gain(off, n=KD):
            return small[:, off:off + n]

        def bank(name, key):
            return psum[TICKET[name, key] % BANKS]

        def chunk(name, k):
            return ring[:, CHUNK_AT[name, k] % SLOTS, :]

        def piece_of(name, k, m):
            n = PIECE_AT[name, k, m] % PIECE_BUFS
            if name == "up":
                src, kts, w = chunk(name, k).rearrange("p (k n) -> p k n", k=KD)[:, :, m * P:(m + 1) * P], KD, P
            else:
                kts = 1 if name == "down" else 2
                w = WO_PIECES[k] if name == "wo" else PIECE // kts
                src = chunk(name, k)[:, m * kts * w:(m + 1) * kts * w].rearrange("p (k n) -> p k n", k=kts)
            return src, *(v[:, n, 0:kts * w].rearrange("p (k n) -> p k n", k=kts) for v in (w_hi, w_lo))

        class Banks:

            def __init__(self, eng):
                self.eng, self.lap = eng, 0

            def filled(self, name, key):
                n = TICKET[name, key]
                self.eng.wait_ge(filled_sem[n % BANKS], self.lap + (n // BANKS + 1))

            def drained(self, name, key, back=0):
                n = TICKET[name, key]
                self.eng.wait_ge(drained_sem[n % BANKS], self.lap + (n // BANKS + 1 - back))

            def vacant(self, name, key):
                n = TICKET[name, key]
                if n >= BANKS:
                    self.eng.wait_ge(drained_sem[n % BANKS], self.lap + n // BANKS)

        def frees(name, key):
            return drained_sem[TICKET[name, key] % BANKS]

        def fills(name, key):
            return filled_sem[TICKET[name, key] % BANKS]

        class Steps:

            def __init__(self, eng, semaphore):
                self.eng, self.sem, self.base, self.n = eng, semaphore, 0, 0

            def add(self, ins):
                ins.then_inc(self.sem, 1)
                self.n += 1

            def sync(self):
                self.eng.wait_ge(self.sem, self.base + self.n)

            def do(self, ins):
                self.add(ins)
                self.sync()

            @contextmanager
            def loop(self, times, per):
                before = self.base + self.n
                with self.eng.Fori(0, times) as i:
                    self.base, self.n = i * per + before, 0
                    yield i
                    assert self.n == per, (self.n, per)
                self.base, self.n = before + times * per, 0

        mrow = region(MROW, 12 * P)
        mrow5 = region(MROW5, 2 * P)
        bc = region(BC, 2, D)
        xn4 = region(XN, 4, D)
        z_tokens = region(Z_TOKENS, 4, 512)
        ev_z = region(EV_Z, 4, 1792)
        ev_qt = region(EV_QT, EV_PAIRS, 512)
        ev_kt = region(EV_KT, 512)
        ev_s = [region(at, 512) for at in (EV_S, EV_S + 512, EV_S + 1024, EV_SGUW)]
        ev_pt = region(EV_PT, 2, 4, P)
        ev_win = region(EV_WIN, TT, 512)
        ev_sguw = region(EV_SGUW, 4, P)
        ev_sgug = region(EV_SGUG, 512)
        ev_sgub = region(EV_SGUB, 4)
        ev_sink = region(EV_SINK, 8)

        ev_cos = region(EV_ROPE, TT, 32)
        ev_sin = region(EV_ROPE + TT * 32, TT, 32)
        ev_cat = region(EV_CAT, 4, D)
        od_za = region(OD_ZA, TT, ZA_W)
        od_zb = region(OD_ZB, TT, ZB_W)
        od_zc = region(OD_ZC, TT, KV_LORA + KR)
        od_cqt = region(OD_CQT, 3, SEQ)
        od_ckvt = region(OD_CKVT, 2, 512)
        od_kf = region(OD_KF, 4, OD_HEADS * OD_DIM)
        od_v = X[:, TT:2 * TT, :].rearrange("p a b -> p (a b)").rearrange("p (t c) -> p t c", t=4)
        od_q = region(OD_Q, TT, UQ_W)
        od_kt = region(OD_KT, OD_HEADS, 512)
        od_qt = region(OD_QT, OD_HEADS, SEQ)
        od_s = [region(at, 512) for at in (OD_S, OD_S + 512, OD_S + 1024, OD_SHIFT)]
        od_pt = region(OD_PT, 2, 4, P)
        od_shift = region(OD_SHIFT, 4, P)
        od_convw = region(OD_CONVW, 3, 512)
        od_cos = region(OD_ROPE, TT, 16)
        od_sin = region(OD_ROPE + TT * 16, TT, 16)
        od_cat = region(OD_CAT, TT, D)
        moe_ht = region(MOE_HT, KD, 512)
        moe_xn = region(MOE_XN, 4, D)
        moe_aff = region(MOE_AFF, 64)
        moe_work = region(MOE_W, 256)
        moe_chosen = region(MOE_W + 256, 256)
        moe_oh = region(MOE_OH, 4, P)
        moe_gw = region(MOE_GW, 4, P)
        moe_gtst = region(MOE_GTST, 512)
        moe_xst = region(MOE_XST, 2 * KD * P)

        def moe_x(streams):
            n = KD * PER_GROUP * streams * CAP
            return moe_xst[:, 0:n].rearrange("p (k e s c) -> p k e s c", k=KD, e=PER_GROUP, s=streams)

        moe_sil = region(MOE_G, 2, 256)
        moe_g = region(MOE_G + 512, 2, 256)
        moe_gtr = region(MOE_GTR, 2, 2, 256)
        moe_yst = region(MOE_YST, 2, D)
        moe_tmp = region(MOE_TMP, 2, 512)
        mix_tmp = region(MIX_TMP, 2, 512)
        b2_q = region(B2_Q, TT, B2_W)
        b2_k = region(B2_K, TT, B2_W)
        b2_v = region(B2_V, TT, B2_W)
        b2_qt = region(B2_QT, B2_PAIRS, SEQ)
        b2_kt = region(B2_KT, B2_PAIRS, SEQ)
        b2_ht = X[:, TT:2 * TT, :].rearrange("p a b -> p (a b)").rearrange("p (k c) -> p k c", k=KD)
        b2_s = region(B2_S, S_BUFS, 768)
        b2_c = [region(at, 768) for at in B2_CBUF]
        b2_pt = region(B2_PT, 2, 6, P)
        b2_cos = region(B2_ROPE, TT, 8)
        b2_sin = region(B2_ROPE + TT * 8, TT, 8)
        b2_ocat = region(B2_OCAT, TT, D)
        b2_merged = region(B2_MERGED, TT, D)
        b2_sig = region(B2_SIG, 3, TT, 512)
        b2_sq = region(B2_SQ, 2, 512)
        a_hi, a_lo = parts("tokens_high", B2_AH, KD, SEQ), parts("tokens_low", B2_AL, KD, SEQ)
        o_hi, o_lo = parts("hidden_high", B2_OH, KD, SEQ), parts("hidden_low", B2_OL, KD, SEQ)
        w_hi, w_lo = parts("weights_high", B2_WH, PIECE_BUFS, PIECE), parts("weights_low", B2_WL, PIECE_BUFS, PIECE)
        b2_amask = [region(B2_MASK, 384), region(B2_MASK + 384, 768)]
        b2_bmask = [region(B2_MASK, P), region(B2_MASK + 1152, 256)]
        b2_cmask = region(B2_MASK + 1408, 384)
        final_g = [region(at, D) for at in FINAL_G]

        z_hi, z_lo = parts("tokens4_high", Z_HI, KD, 512), parts("tokens4_low", Z_LO, KD, 512)
        z_weights = {name: [[parts(f"{name}_{part}{n}", at, 512) for part, at in zip(("high", "low"), ats)] for n, ats in enumerate(places)]
                     for name, places in (("evz", EV_WEIGHTS), ("odz", OD_WEIGHTS), ("mix", MIX_WEIGHTS))}
        z_weights["mix0"] = z_weights["mix1"] = z_weights["mix"]
        cat_hi = parts("mixed_high", EV_CATT, KD, 512)

        def z_piece(name, c, k):
            w = z_width(name, c)
            return chunk(name, c)[:, k * w:(k + 1) * w], *(v[:, 0:w] for v in z_weights[name][(Z_AT[name, c, k] - Z_FIRST[name]) % Z_BUFS[name]])

        mx, nm, ls, l, rl = (stat[:, 34 * n:34 * n + 34] for n in range(5))
        ss, rstd = stat[:, 170:178], stat[:, 178:186]
        bn, mv = stat[:, 186:210], stat[:, 210:218]
        lg, lge, lgs = stat[:, 218:282], stat[:, 282:346], stat[:, 346:354]
        pos = stat[:, 354:418]
        mkT = stat[:, 418:482]
        mx2 = stat[:, 482:522]
        ev_nsink = mx2[:, 0:8]
        layer_gain = stat[:, 522:538]
        ss2, rstd2 = stat[:, 538:544], stat[:, 544:550]

        root4, eps, idle = stat[:, 550:554], stat[:, 554:555], stat[:, 555:583]

        block = ctx.enter_context(nc.Block())

        @block.sync
        def _(sp):
            for dst, src, name in ((sc, ccols, "c_in"), (base, base_c, "base_in"), (small, small_c, "small_in"), (X, x_in, "x_in")):
                sp.dma_start(dst[:], src).then_inc(sem(name), 16)
            sp.wait_ge(sem("mod_clear"), 1)
            for q in range(4):
                sp.dma_start(mrow[32 * q:32 * q + 2, :], modb[0, q]).then_inc(sem("modb_in"), 16)
            for s in range(SLOTS):
                sp.dma_start(ring[:, s, :], stream[s]).then_inc(slot_loaded[s], 16)
            rounds = N_CHUNKS // SLOTS
            with sp.Fori(1, rounds) as r:
                for s in range(SLOTS):
                    sp.wait_ge(slot_free[s], r)
                    sp.dma_start(ring[:, s, :], stream[bass.ds(r * SLOTS + s, 1)].rearrange("a p n -> (a p) n"))\
                        .then_inc(slot_loaded[s], 16)
            for s in range(N_CHUNKS - rounds * SLOTS):
                sp.wait_ge(slot_free[s], rounds)
                sp.dma_start(ring[:, s, :], stream[rounds * SLOTS + s]).then_inc(slot_loaded[s], 16)
            sp.wait_ge(sem("result"), TT)
            sp.dma_start(out.rearrange("a (t p) d -> p (a t) d", p=P), xn4[:, 0:TT, :]).then_inc(sem("stored"), 16)
            sp.wait_ge(sem("stored"), 16)

        @block.gpsimd
        def _(pool):
            def load(dst, src, name):
                pool.dma_start(dst, src).then_inc(sem(name), 16)

            windows = EV_SGUW - EV_WIN
            pool.wait_ge(sem("z_w_hi"), 1)
            load(region(EV_SGUW, EV_PACK_W - windows), ev_pack[:, windows:], "ev_in")
            pool.wait_ge(sem("mod_saved"), 1)
            pool.wait_ge(sem("mod_spread"), 1)
            for q in range(4):
                load(mrow[32 * q:32 * q + 2, :], modb[1, q], "modb_in2")
            Banks(pool).filled("evz", (3, 3))
            load(region(EV_WIN, windows), ev_pack[:, 0:windows], "ev_in2")
            pool.wait_ge(sem("x_moe"), X_MOE[0])
            load(region(OD_SHIFT, 4 * P + 3 * 512), od_pack, "od_in")
            load(region(OD_ROPE, 4 * 16), od_rope, "od_in2")
            pool.wait_ge(sem("x_mix"), 12)
            load(final_g[0], gains[0], "fg_in")
            pool.wait_ge(sem("x_moe"), X_MOE[1])
            load(region(B2_MASK, 1792), b2_masks, "b2_in")
            load(region(B2_ROPE, 4 * 8), b2_rope, "b2_in2")
            pool.wait_ge(sem("b2_merged"), B2_LAYERS * 4)
            load(final_g[1], gains[1], "fg_in")

        @block.tensor
        def _(pe):
            b = Banks(pe)
            state = {"chunk_lap": 0}
            owed = []

            def mm(o, lhsT, rhs, start, stop, sig=None):
                ins = pe.matmul(o, lhsT, rhs, start=start, stop=stop)
                if sig is not None:
                    ins.then_inc(sig, 1)
                elif owed:
                    ins.then_inc(slot_free[owed.pop(0)], 1)

            def turn(o, in_, n=P, sig=None):
                ins = pe.transpose(o, in_, base[0:n, IDENT:IDENT + n])
                if sig is not None:
                    ins.then_inc(sig, 1)
                elif owed:
                    ins.then_inc(slot_free[owed.pop(0)], 1)

            def arrived(name, k):
                n = CHUNK_AT[name, k]
                pe.wait_ge(slot_loaded[n % SLOTS], state["chunk_lap"] * 16 + 16 * (n // SLOTS + 1))

            def used(name, k):
                owed.append(CHUNK_AT[name, k] % SLOTS)

            def settle():
                while owed:
                    pe.drain().then_inc(slot_free[owed.pop(0)], 1)

            def norm(name, xn, tiles, ready, count):
                for t in range(tiles):
                    pe.wait_ge(ready, count - tiles + t + 1)
                    for k in range(KD):
                        if t == 0:
                            b.vacant(name, k)
                        turn(bank(name, k)[:, t * P:(t + 1) * P], xn[:, t, k * P:(k + 1) * P],
                             sig=fills(name, k) if t == tiles - 1 else None)

            def product(name, key, lhs, rhs, kts, width, sig=True, col=0):
                o = bank(name, key)[:, col:col + width]
                for n in range(kts):
                    mm(o, lhs(n), rhs(n), n == 0, n == kts - 1, fills(name, key) if sig and n == kts - 1 else None)

            def z_product(name, c, k):
                tiles, n = z_tiles(name, c), Z_AT[name, c, k]
                if k == 0:
                    for t in range(tiles):
                        b.vacant(name, (c, t))
                pe.wait_ge(sem("z_w_lo"), n + 1)
                high = cat_hi if "mix" in name else z_hi
                if n < Z_FIRST[name] + KD and "mix" in name:
                    b.drained("cat" + name[3], k)
                elif n < Z_FIRST[name] + KD:
                    pe.wait_ge(sem("z_tok_lo"), (8 if name == "odz" else 0) + k + 1)
                _, wh, wl = z_piece(name, c, k)
                for t in range(tiles):
                    width = z_width(name, c) if t < TT or name != "odz" else KV_LORA + KR
                    o = bank(name, (c, t))[:, 0:width]
                    cols = slice(t * P, (t + 1) * P)
                    for q, (x, w) in enumerate(((high, wh), (high, wl), (z_lo, wh))):
                        sig = None
                        if q == 2 and k == KD - 1:
                            sig = fills(name, (c, t))
                        elif q == 2 and t == tiles - 1:
                            sig = sem("z_used")
                        mm(o, x[:, k, cols], w[:, 0:width], k == 0 and q == 0, k == KD - 1 and q == 2, sig)
                if k == KD - 1 and (name, c) != ("odz", 4):
                    used(name, c)

            def mod_chunk(layer, c):
                name = f"mod{layer}"
                arrived(name, c)
                b.vacant(name, c)
                w = chunk(name, c).rearrange("p (k n) -> p k n", k=KD)
                for k in range(KD):
                    for q in range(4):
                        mm(bank(name, c)[32 * q:32 * q + 32, 0:P], sc[:, k, :], w[:, k, q * P:(q + 1) * P], k == 0, k == KD - 1,
                           fills(name, c) if k == KD - 1 and q == 3 else None)
                used(name, c)

            def mod_cols(layer, half):
                name = f"modcol{layer}"
                b.vacant(name, half)
                for n, v in enumerate(((1, 0), (4, 3))[half]):
                    for cc in range(2):
                        at = (2 * n + cc) * P
                        turn(bank(name, half)[:, at:at + P], mrow[:, (2 * v + cc) * P:(2 * v + cc + 1) * P],
                             sig=fills(name, half) if (n, cc) == (1, 1) else None)

            def mod_row(name, n, src, s):
                b.vacant(name, n)
                for qq in range(2):
                    at = 32 * (2 * (n % 2) + qq) + s
                    mm(bank(name, n)[:, qq * 256:(qq + 1) * 256], ident[:, at:at + 1].to_broadcast([P, P]), src, True, True,
                       fills(name, n) if qq == 1 else None)

            def modulation(what, layer, n):
                if what == "m":
                    mod_chunk(layer, n)
                elif n == 0:
                    b.drained("mod0", 11)
                    mod_cols(0, 1)
                else:
                    mod_row("modrow0", n - 1, mrow[:, 4 * P:6 * P], (n - 1) // 2)

            def attention(name, schedule, score, nk, value, p, pt, ready):
                for what, *x in schedule:
                    if what != "a":
                        modulation(what, *x)
                        continue
                    kind, u = x
                    b.vacant(name, (kind, u))
                    o = bank(name, (kind, u))
                    if kind == "s":
                        score(u, o)
                    elif kind == "t":
                        ready(u)
                        for n in range(nk(u)):
                            turn(o[:, n * P:(n + 1) * P], p[u % S_BUFS][:, n * P:(n + 1) * P],
                                 sig=fills(name, (kind, u)) if n == nk(u) - 1 else None)
                    else:
                        b.drained(name, ("t", u))
                        for n in range(nk(u)):
                            mm(o[:, 0:64], pt[:, u % 2, n, :], value(u, n), n == 0, n == nk(u) - 1,
                               fills(name, (kind, u)) if n == nk(u) - 1 else None)

            def cat_turns(name, src, tiles):
                for k in range(KD):
                    b.vacant(name, k)
                    for t in range(tiles):
                        turn(bank(name, k)[:, t * P:(t + 1) * P], src[:, t, k * P:(k + 1) * P],
                             sig=fills(name, k) if t == tiles - 1 else None)

            def mix(layer):
                for c in range(2):
                    for k in range(KD):
                        z_product(f"mix{layer}", c, k)

            def experts(layer):
                L = str(layer)
                streams = 2 - layer
                tiles = TT * streams
                rows = streams * CAP
                parts = P // rows
                moe = "moe" + L
                b.vacant("logit" + L, 0)
                o = bank("logit" + L, 0)
                for k in range(KD):
                    b.drained("n2_" + L, k)
                    at = ROUTER + (layer * KD + k) * N_EXP
                    for q in range(tiles):
                        t = q % streams * TT + q // streams
                        mm(o[32 * q:32 * q + 32, 0:P], small[:, at:at + 32], moe_ht[:, k, t * P:(t + 1) * P], k == 0, k == KD - 1,
                           fills("logit" + L, 0) if q == tiles - 1 and k == KD - 1 else None)
                b.drained("logit" + L, 0)
                b.vacant("logitT" + L, 0)
                turn(bank("logitT" + L, 0)[:, 0:32 * tiles], moe_work[0:32 * tiles, 0:P], 32 * tiles, fills("logitT" + L, 0))
                ne = streams * N_EXP
                pe.wait_ge(sem("aff"), layer + 1)
                b.vacant("affT" + L, 0)
                for t in range(TT):
                    turn(bank("affT" + L, 0)[0:ne, t * P:(t + 1) * P], moe_aff[:, t * ne:(t + 1) * ne],
                         sig=fills("affT" + L, 0) if t == TT - 1 else None)
                if layer == 0:
                    for n in range(4):
                        mod_row("modrow5", n, mrow5, n // 2)
                pe.wait_ge(sem("chosen"), layer + 1)
                b.vacant("selT" + L, 0)
                for t in range(TT):
                    turn(bank("selT" + L, 0)[:, t * ne:(t + 1) * ne], moe_chosen[0:ne, t * P:(t + 1) * P], ne,
                         fills("selT" + L, 0) if t == TT - 1 else None)
                b.drained("selT" + L, 0)
                b.vacant("rank" + L, 0)
                o = bank("rank" + L, 0)
                mm(o[:, 0:ne], tri_le, mkT[:, 0:ne], True, True)
                mm(o[:, ne:2 * ne], ones, mkT[:, 0:ne], True, False)
                mm(o[:, ne:2 * ne], tri_le, mkT[:, ne:2 * ne], False, True, fills("rank" + L, 0))
                settle()
                with pe.Fori(0, GROUPS) as i:
                    b.lap = i * LAP[moe]
                    state["chunk_lap"] = i * CHUNK_LAP[moe]
                    pe.wait_ge(sem("hot" + L), i * tiles + tiles)
                    for k in range(KD):
                        b.vacant("gather" + L, k)
                        for s in range(streams):
                            for t in range(TT):
                                tok = s * TT + t
                                mm(bank("gather" + L, k)[:, s * P:(s + 1) * P], moe_xn[:, tok, k * P:(k + 1) * P], moe_oh[:, tok, :],
                                   t == 0, t == TT - 1,
                                   fills("gather" + L, k) if (s, t) == (streams - 1, TT - 1) else None)
                    pe.wait_ge(sem("gated" + L), i * tiles + tiles)
                    for e in range(PER_GROUP):
                        xs = moe_x(streams)[:, :, e].rearrange("p k s c -> p k (s c)")
                        width = NCOL // parts

                        def hidden(key, c):
                            arrived(moe, e * 6 + c)
                            b.vacant(moe, (e, key))
                            w = chunk(moe, e * 6 + c).rearrange("p (k n) -> p k n", k=KD)
                            o = bank(moe, (e, key))
                            for k in range(KD):
                                if e == 0 and c == 0:
                                    b.drained("gather" + L, k)
                                for q in range(parts):
                                    last = k == KD - 1 and q == parts - 1
                                    mm(o[q * rows:(q + 1) * rows, 0:width], xs[:, k, :], w[:, k, q * width:(q + 1) * width],
                                       k == 0, k == KD - 1, fills(moe, (e, key)) if last else None)
                            used(moe, e * 6 + c)

                        def turn_hidden(c):
                            b.drained(moe, (e, f"b{c}"))
                            b.vacant(moe, (e, f"t{c}"))
                            for j in range(width // P):
                                turn(bank(moe, (e, f"t{c}"))[:, j * P:(j + 1) * P], moe_g[:, c, j * P:(j + 1) * P],
                                     sig=fills(moe, (e, f"t{c}")) if j == width // P - 1 else None)

                        def down(c, kts):
                            w = chunk(moe, e * 6 + 4 + c).rearrange("p (k n) -> p k n", k=4)
                            o = bank(moe, (e, "y"))
                            yw = D // parts
                            for kt in kts:
                                q, j = kt // (width // P), kt % (width // P)
                                lhs = moe_gtr[:, e % 2, c, j * P + q * rows:j * P + (q + 1) * rows]
                                for n in range(parts):
                                    last = c == 1 and kt == 3 and n == parts - 1
                                    mm(o[n * rows:(n + 1) * rows, 0:yw], lhs, w[:, kt, n * yw:(n + 1) * yw],
                                       c == 0 and kt == 0, c == 1 and kt == 3, fills(moe, (e, "y")) if last else None)

                        b.vacant(moe, (e, "gate"))
                        for t in range(tiles):
                            turn(bank(moe, (e, "gate"))[0:CAP, t * P:(t + 1) * P], moe_gw[:, t, e * CAP:(e + 1) * CAP],
                                 sig=fills(moe, (e, "gate")) if t == tiles - 1 else None)
                        hidden("a0", 0)
                        hidden("b0", 1)
                        hidden("a1", 2)
                        turn_hidden(0)
                        hidden("b1", 3)
                        arrived(moe, e * 6 + 4)
                        b.vacant(moe, (e, "y"))
                        b.drained(moe, (e, "t0"))
                        down(0, (0, 1))
                        turn_hidden(1)
                        down(0, (2, 3))
                        used(moe, e * 6 + 4)
                        arrived(moe, e * 6 + 5)
                        b.drained(moe, (e, "t1"))
                        down(1, (0, 1, 2, 3))
                        used(moe, e * 6 + 5)
                    settle()
                    b.drained(moe, (PER_GROUP - 1, "gate"))
                    b.drained(moe, (PER_GROUP - 1, "y"))
                    pieces = 8 // tiles
                    w = D // pieces
                    for n in range(8):
                        t, c = n // pieces, n % pieces
                        b.vacant("comb" + L, n)
                        mm(bank("comb" + L, n)[:, 0:w], moe_gtst[:, t * P:(t + 1) * P],
                           moe_yst[:, t // TT, c * w:(c + 1) * w], True, True, fills("comb" + L, n))
                b.lap = 0
                state["chunk_lap"] = 0

            pe.wait_ge(sem("silu_c"), 1)
            for c in range(MOD_EARLY):
                mod_chunk(0, c)
            pe.wait_ge(sem("base_in"), 16)
            b.drained("mod0", MOD_EARLY - 1)
            mod_cols(0, 0)
            norm("n1_0", xn4, 4, sem("xn"), 4)
            for what, *x in evz_schedule():
                if what == "w":
                    z_product("evz", *x)
                elif what != "z":
                    modulation(what, *x)
            pe.wait_ge(sem("ev_in"), 16)
            for t in range(4):
                pe.wait_ge(sem("sgu_v"), t + 1)
                b.vacant("sgu", t)
                for g in range(4):
                    mm(bank("sgu", t)[:, g * P:(g + 1) * P], ev_sguw[:, g, :], ev_z[:, t, 512 + g * P:512 + (g + 1) * P],
                       True, True, fills("sgu", t) if g == 3 else None)
            b.drained("evz", (3, 3))
            pe.wait_ge(sem("ev_rope"), TT)
            for j in range(1 + EV_PAIRS):
                b.vacant("evqk", j)
                for t in range(4):
                    turn(bank("evqk", j)[:, t * P:(t + 1) * P], ev_z[:, t, 1152 + j * P:1152 + (j + 1) * P],
                         sig=fills("evqk", j) if t == 3 else None)

            def ev_score(u, o):
                h, t = EV_UNITS[u]
                r = 64 * (h % 2)
                if u == 0:
                    b.drained("evqk", EV_PAIRS)
                first = 0 if t < TT else SEQ
                mm(o[:, 0:512 - first], ev_qt[r:r + 64, h // 2, t * P:(t + 1) * P], ev_kt[r:r + 64, first:512],
                   True, True, fills("evatt", ("s", u)))

            def ev_keys(u):
                return 4 if EV_UNITS[u][1] < TT else 2

            def ev_value(u, n):
                h, t = EV_UNITS[u]
                return ev_z[:, n + (0 if t < TT else TT), 1024 + 64 * (h % 2):1088 + 64 * (h % 2)]

            attention("evatt", ev_schedule(ATT_LAGS), ev_score, ev_keys, ev_value, ev_s, ev_pt,
                      lambda u: pe.wait_ge(sem("ev_p"), u + 1))
            b.drained("evatt", ("o", len(EV_UNITS) - 1))
            b.drained("sgu", 3)
            b.drained("mod1", 11)
            for half in range(2):
                mod_cols(1, half)
            cat_turns("cat0", ev_cat, 4)
            mix(0)
            norm("n2_0", moe_xn, 4, sem("xn"), 8)
            experts(0)

            for n in range(4):
                v = 2 + 3 * (n // 2)
                mod_row("modrow1", n, mrow[:, 2 * v * P:(2 * v + 2) * P], 0)
            norm("n1_1", xn4, 4, sem("xn"), 12)
            def convolution():
                pe.wait_ge(sem("od_in"), 16)
                pe.wait_ge(sem("conv_u"), TT)
                for t in range(TT):
                    for d in range(2):
                        b.vacant("conv", (t, d))
                        o = bank("conv", (t, d))[:, :]
                        seam = t == 1 - d
                        mm(o, od_shift[:, 2 * d, :], od_zb[:, t, 512:1024], True, not seam, None if seam else fills("conv", (t, d)))
                        if seam:
                            mm(o, od_shift[:, 2 * d + 1, :], od_zb[:, 1 - t, 512:1024], False, True, fills("conv", (t, d)))

            for what, c, k in odz_schedule():
                if what == "w":
                    z_product("odz", c, k)
                    if (c, k) == (0, 2):
                        convolution()
            pe.wait_ge(sem("lora_n"), 6)
            for j in range(2):
                b.vacant("ckvT", j)
                for t in range(4):
                    src = od_za[:, t, :] if t < TT else od_zc[:, t - TT, :]
                    turn(bank("ckvT", j)[:, t * P:(t + 1) * P], src[:, j * P:(j + 1) * P],
                         sig=fills("ckvT", j) if t == 3 else None)
            for j in range(3):
                b.vacant("cqT", j)
                for t in range(TT):
                    at = KV_LORA + KR + j * P
                    turn(bank("cqT", j)[:, t * P:(t + 1) * P], od_za[:, t, at:at + P],
                         sig=fills("cqT", j) if t == TT - 1 else None)
            uq = chunk("odz", 4)[:, KD * OD_TAIL:KD * OD_TAIL + 3 * UQ_W].rearrange("p (k n) -> p k n", k=3)
            b.drained("cqT", 2)
            for p in range(2):
                for t in range(TT):
                    b.vacant("uq", (p, t))
                    product("uq", (p, t), lambda k: od_cqt[:, k, t * P:(t + 1) * P],
                            lambda k: uq[:, k, p * 384:(p + 1) * 384], 3, 384)
            used("odz", 4)
            arrived("ukv", 0)
            ukv = chunk("ukv", 0)[:, 0:2 * D].rearrange("p (k n) -> p k n", k=2)
            for p in range(2):
                for t in range(4):
                    b.vacant("ukv", (p, t))
                    product("ukv", (p, t), lambda k: od_ckvt[:, k, t * P:(t + 1) * P],
                            lambda k: ukv[:, k, p * 512:(p + 1) * 512], 2, 512)
            used("ukv", 0)
            b.drained("ukv", (1, 3))
            pe.wait_ge(sem("od_kr"), 4)
            for h in range(OD_HEADS):
                b.vacant("odkT", h)
                for t in range(4):
                    turn(bank("odkT", h)[0:OD_DIM, t * P:(t + 1) * P], od_kf[:, t, h * OD_DIM:(h + 1) * OD_DIM],
                         sig=fills("odkT", h) if t == 3 else None)
            pe.wait_ge(sem("od_rope"), TT)
            for j in range(OD_HEADS // 2):
                b.vacant("odqT", j)
                for n in range(2):
                    for t in range(TT):
                        h = 2 * j + n
                        turn(bank("odqT", j)[0:OD_DIM, (n * TT + t) * P:(n * TT + t + 1) * P],
                             od_q[:, t, h * OD_DIM:(h + 1) * OD_DIM],
                             sig=fills("odqT", j) if n == 1 and t == TT - 1 else None)

            def od_score(u, o):
                h, t = OD_UNITS[u]
                if u == 0:
                    b.drained("odqT", OD_HEADS // 2 - 1)
                    b.drained("odkT", OD_HEADS - 1)
                mm(o[:, :], od_qt[0:OD_DIM, h, t * P:(t + 1) * P], od_kt[0:OD_DIM, h, :], True, True, fills("odatt", ("s", u)))

            attention("odatt", [("a", *x) for x in pipeline(len(OD_UNITS), ATT_LAGS)], od_score, lambda u: 4,
                      lambda u, n: od_v[:, n, OD_UNITS[u][0] * 64:OD_UNITS[u][0] * 64 + 64], od_s, od_pt,
                      lambda u: b.drained("odatt", ("s", u)))
            b.drained("odatt", ("o", len(OD_UNITS) - 1))
            pe.wait_ge(sem("conv_done"), TT)
            cat_turns("cat1", od_cat, TT)
            mix(1)
            norm("n2_1", moe_xn, TT, sem("xn"), 14)
            experts(1)

            with pe.Fori(0, B2_LAYERS) as i:
                b.lap = i * LAP["b2"]
                state["chunk_lap"] = i * CHUNK_LAP["b2"]
                norm("nmix", region(B2_XN1, TT, D), TT, sem("b2_xn"), i * 4 + 2)

                def split_piece(name, k, m, products):
                    p = PIECE_AT[name, k, m]
                    pe.wait_ge(sem("w_lo"), i * len(PIECES) + p + 1)
                    _, wh, wl = piece_of(name, k, m)
                    for n, (xh, xl, kt, cols, o, start, stop, ticket) in enumerate(products):
                        if (name, k, m) == ("up", 0, 0):
                            b.drained("nmlp", n)
                        passes = [(xh, wh[:, kt, cols]), (xh, wl[:, kt, cols]), (xl, wh[:, kt, cols])]
                        for q, (x, w) in enumerate(passes):
                            sig = None
                            if q == 2 and ticket is not None:
                                sig = fills(*ticket)
                            elif q == 2 and n == len(products) - 1:
                                sig = sem("piece_used")
                            lhs, rhs = (w, x) if name == "up" else (x, w)
                            mm(o, lhs, rhs, start and q == 0, stop and q == 2, sig)
                    if m == PIECES_PER_CHUNK - 1:
                        used(name, k)

                def by_tokens(name, k, m, xh, xl, key, span, width):
                    out = []
                    for kt in (2 * m, 2 * m + 1):
                        for t in range(TT):
                            first, last = span(kt)
                            ticket = (name, key(kt, t))
                            cols = slice(t * P, (t + 1) * P)
                            out.append((xh[:, kt, cols], xl[:, kt, cols], kt - 2 * m, slice(0, width), bank(*ticket)[:, 0:width],
                                        kt == first, kt == last - 1, ticket if kt == last - 1 else None))
                    split_piece(name, k, m, out)

                whole = lambda kt: (0, KD)
                for c in range(9):
                    for t in range(TT):
                        b.vacant("qkv", (c, t))
                    for m in range(PIECES_PER_CHUNK):
                        if c == 0:
                            for k in (2 * m, 2 * m + 1):
                                b.drained("nmix", k)
                        by_tokens("qkv", c, m, a_hi, a_lo, lambda kt, t: (c, t), whole, 512)
                for wh in range(2):
                    src = (b2_q, b2_k)[wh]
                    pe.wait_ge(sem("b2_rope"), i * 4 + 2 + 2 * wh)
                    b.drained("qkv", (2 + 3 * wh, 1))
                    for j in range(B2_PAIRS // 2):
                        b.vacant("qkT", (wh, j))
                        for n in range(2):
                            for t in range(TT):
                                turn(bank("qkT", (wh, j))[:, (n * TT + t) * P:(n * TT + t + 1) * P],
                                     src[:, t, (2 * j + n) * P:(2 * j + n + 1) * P],
                                     sig=fills("qkT", (wh, j)) if n == 1 and t == TT - 1 else None)
                for j in (B2_PAIRS // 2 - 2, B2_PAIRS // 2 - 1):
                    b.drained("qkT", (1, j))
                b.drained("qkv", (8, 1))
                def softmax_unit(kind, u, n):
                    key = (kind, u, n)
                    unit = AB_UNITS[u]
                    t = unit[2]
                    per_bank = ab_keys_per_bank(*unit)
                    b.vacant("ab", key)
                    o = bank("ab", key)
                    if kind == "s":
                        blocks = per_bank[n]
                        heads = list(dict.fromkeys(hd for hd, _ in blocks))
                        for q, hd in enumerate(heads):
                            at = [m for m, x in enumerate(blocks) if x[0] == hd]
                            kts = [blocks[m][1] for m in at]
                            r = 64 * (hd % 2)
                            mm(o[:, at[0] * P:(at[-1] + 1) * P], b2_qt[r:r + 64, hd // 2, t * P:(t + 1) * P],
                               b2_kt[r:r + 64, hd // 2, kts[0] * P:(kts[-1] + 1) * P], True, True,
                               fills("ab", key) if q == len(heads) - 1 else None)
                    elif kind == "t":
                        if n == 0:
                            pe.wait_ge(sem("b2_p"), i * len(AB_UNITS) + u + 1)
                        for m in range(len(per_bank[n])):
                            turn(o[:, m * P:(m + 1) * P], b2_s[:, u % S_BUFS, (4 * n + m) * P:(4 * n + m + 1) * P],
                                 sig=fills("ab", key) if m == len(per_bank[n]) - 1 else None)
                    else:
                        for m in range(len(per_bank)):
                            b.drained("ab", ("t", u, m))
                        keys = ab_keys(*unit)
                        for m, (hd, kt) in enumerate(keys):
                            mm(o[:, 0:64], b2_pt[:, u % 2, m, :], b2_v[:, kt, hd * 64:(hd + 1) * 64], m == 0, m == len(keys) - 1,
                               fills("ab", key) if m == len(keys) - 1 else None)

                def stick_unit(kind, u, n):
                    key = (kind, u, n)
                    hd = 18 + u
                    r = 64 * (hd % 2)
                    b.vacant("c", key)
                    o = bank("c", key)
                    buf = b2_c[u]
                    if kind == "s":
                        mm(o[:, 0:SEQ], b2_kt[r:r + 64, hd // 2, 0:P], b2_qt[r:r + 64, hd // 2, :], True, True)
                        mm(o[:, SEQ:SEQ + P], b2_kt[r:r + 64, hd // 2, P:SEQ], b2_qt[r:r + 64, hd // 2, P:SEQ], True, True, fills("c", key))
                    elif kind == "c":
                        pe.wait_ge(sem("c_softplus"), i * len(C_UNITS) + u + 1)
                        mm(o[:, 0:SEQ], tri_ge, buf[:, 384:384 + SEQ], True, False)
                        mm(o[:, P:SEQ], ones, buf[:, 384 + SEQ:768], False, True)
                        mm(o[:, SEQ:SEQ + P], tri_ge, buf[:, 384 + SEQ:768], True, True, fills("c", key))
                    else:
                        if n == 0:
                            pe.wait_ge(sem("c_weights"), i * len(C_UNITS) + u + 1)
                        for kt in range(n + 1):
                            at = 384 + (n * P if kt == 0 else SEQ)
                            mm(o[:, 0:64], buf[:, at:at + P], b2_v[:, kt, hd * 64:(hd + 1) * 64], kt == 0, kt == n,
                               fills("c", key) if kt == n else None)

                for which, kind, u, n in b2_schedule(ATT_LAGS):
                    (softmax_unit if which == "ab" else stick_unit)(kind, u, n)
                b.drained("c", ("o", 5, 1))
                b.drained("ab", ("o", len(AB_UNITS) - 1, 0))
                for j in range(4):
                    b.vacant("ocat", j)
                    for n in range(2):
                        for t in range(TT):
                            k = 2 * j + n
                            turn(bank("ocat", j)[:, (n * TT + t) * P:(n * TT + t + 1) * P], b2_ocat[:, t, k * P:(k + 1) * P],
                                 sig=fills("ocat", j) if n == 1 and t == TT - 1 else None)
                for c in range(2):
                    for k in range(3):
                        for t in range(TT):
                            b.vacant("merge", (c, "gate", k, t))
                        for m in range(PIECES_PER_CHUNK):
                            if c == 0 and k == 0:
                                pe.wait_ge(sem("a_lo"), i * 4 + m + 1)
                            by_tokens("merge", 4 * c + k, m, a_hi, a_lo, lambda kt, t: (c, "gate", k, t), whole, 512)
                    if c == 0:
                        for j in range(4):
                            b.drained("ocat", j)
                    for k in range(3):
                        for t in range(TT):
                            b.vacant("merge", (c, "branch", k, t))
                    branch = lambda kt: 0 if kt < 2 else 1 if kt < 5 else 2
                    for m in range(PIECES_PER_CHUNK):
                        by_tokens("merge", 4 * c + 3, m, o_hi, o_lo, lambda kt, t: (c, "branch", branch(kt), t),
                                  lambda kt: BRANCHES[branch(kt)], 512)
                for t in range(TT):
                    pe.wait_ge(sem("b2_merged"), i * 4 + TT + t + 1)
                    for j in range(4):
                        if t == 0:
                            b.vacant("mergeT", j)
                        for n in range(2):
                            k = 2 * j + n
                            turn(bank("mergeT", j)[:, (n * TT + t) * P:(n * TT + t + 1) * P], b2_merged[:, t, k * P:(k + 1) * P],
                                 sig=fills("mergeT", j) if n == 1 and t == TT - 1 else None)
                for c in range(3):
                    for t in range(TT):
                        b.vacant("wo", (c, t))
                    for m in range(PIECES_PER_CHUNK):
                        if c == 0:
                            b.drained("mergeT", m)
                        by_tokens("wo", c, m, a_hi, a_lo, lambda kt, t: (c, t), whole, WO_PIECES[c])
                norm("nmlp", region(B2_XN2, TT, D), TT, sem("b2_xn"), i * 4 + 4)

                def up(j):
                    for m in range(PIECES_PER_CHUNK):
                        n, half = m // 2, m % 2
                        if half == 0:
                            b.vacant("up", (j, n))
                        o = bank("up", (j, n))[:, half * SEQ:(half + 1) * SEQ]
                        split_piece("up", j, m, [(a_hi[:, k, :], a_lo[:, k, :], k, slice(0, P), o, k == 0, k == KD - 1,
                                                  ("up", (j, n)) if half and k == KD - 1 else None) for k in range(KD)])

                def down_ff(j):
                    pe.wait_ge(sem("b2_hidden"), i * (2 * N_FF) + 2 * j + 2)
                    for t in range(TT):
                        for h in range(2):
                            b.vacant("down", (j, t, h))
                    for m in range(PIECES_PER_CHUNK):
                        last = m == PIECES_PER_CHUNK - 1
                        k = j % 2 * 4 + m
                        split_piece("down", j, m, [(o_hi[:, k, t * P:(t + 1) * P], o_lo[:, k, t * P:(t + 1) * P], 0,
                                                    slice(h * 512, (h + 1) * 512), bank("down", (j, t, h))[:, :], m == 0, last,
                                                    ("down", (j, t, h)) if last else None) for t in range(TT) for h in range(2)])

                for which, j in FF_ORDER:
                    (up if which == "up" else down_ff)(j)
                settle()

        @block.scalar
        def _(act):
            b = Banks(act)
            squares = [0]

            def copy(o, i, sig=None):
                ins = act.activation(o, i, ACT.Copy)
                if sig is not None:
                    ins.then_inc(sig, 1)

            def root(v, width, sig):
                act.activation(v, v, ACT.Sqrt, bias=eps, scale=1.0 / width).then_inc(sig, 1)

            warm = [0]

            def warm_up(before):
                act.activation(ss[:, 0:1], eps, ACT.Sqrt).then_inc(sem("warm"), 1)
                act.wait_ge(sem("warm"), before + 1)

            def square_sums(x, junk, tiles, ready):
                warm_up(warm[0])
                warm[0] += 1
                for t in range(tiles):
                    ready(t)
                    act.activation(junk[:, t, :], x[:, t, :], ACT.Square, accum_out=ss[:, t:t + 1]).then_inc(sem("sq"), 1)
                    squares[0] += 1
                    act.wait_ge(sem("sq"), squares[0])
                    root(ss[:, t:t + 1], D, sem("root"))

            def norm_out(name, dst, tiles, scale, shift):
                for k in range(0, KD, 2):
                    b.filled(name, k)
                    for s in range(tiles // TT):
                        cols = slice(s * SEQ, (s + 1) * SEQ)
                        ins = act.activation(dst[:, k, cols], bank(name, k)[:, cols], ACT.Identity,
                                             bias=shift[:, k, s:s + 1], scale=scale[:, k, s:s + 1])
                    ins.then_inc(frees(name, k), 1)

            def norm_split(name, scale, shift, before, first):
                for k in range(0, KD + 2, 2):
                    if k < KD:
                        b.filled(name, k)
                        if k >= 4:
                            act.wait_ge(sem("z_tok_lo"), before + k - 3)
                        for s in range(2):
                            cols = slice(s * SEQ, (s + 1) * SEQ)
                            ins = act.activation(z_tokens[:, k % 4, cols], bank(name, k)[:, cols], ACT.Identity,
                                                 bias=shift[:, k, s:s + 1], scale=scale[:, k, s:s + 1])
                        ins.then_inc(frees(name, k), 1)
                    if k >= 2:
                        for m in (k - 2, k - 1):
                            b.drained(name, m)
                            copy(z_hi[:, m, :], z_tokens[:, m % 4, :], sem("z_tok_hi"))
                    if k == 2:
                        b.filled(name, KD - 1)
                        for n in range(EARLY_SPLIT):
                            z_split(*Z_PIECES[first + n])

            def z_split(name, c, k):
                n = Z_AT[name, c, k]
                if k == 0:
                    at = CHUNK_AT[name, c]
                    act.wait_ge(slot_loaded[at % SLOTS], 16 * (at // SLOTS + 1))
                before = n - Z_BUFS[name]
                if before >= Z_FIRST[name]:
                    _, c0, k0 = Z_PIECES[before]
                    if k0 == KD - 1:
                        b.filled(name, (c0, z_tiles(name, c0) - 1))
                    else:
                        act.wait_ge(sem("z_used"), Z_USED_UP_TO[before])
                src, high, _ = z_piece(name, c, k)
                copy(high, src, sem("z_w_hi"))

            def mod_row(name, n):
                b.filled(name, n)
                dst = bc[:, n // 2, :].rearrange("p (c q j) -> p q c j", c=2, q=4)[:, 2 * (n % 2):2 * (n % 2) + 2]
                copy(dst, bank(name, n)[:, :].rearrange("p (q c j) -> p q c j", q=2, c=2), frees(name, n))

            def cat_split(layer, width):
                name = f"mix{layer}"
                for k in range(KD):
                    b.filled(f"cat{layer}", k)
                    copy(cat_hi[:, k, 0:width], bank(f"cat{layer}", k)[:, 0:width], sem("cat_hi"))
                    if k == 1:
                        for n in range(EARLY_SPLIT):
                            z_split(name, 0, n)
                for c in range(2):
                    for k in range(KD):
                        if not early_split(name, c, k):
                            z_split(name, c, k)

            def probs_out(name, u, pt, nk):
                b.filled(name, ("t", u))
                if u >= 2:
                    b.filled(name, ("o", u - 2))
                copy(pt[:, u % 2, 0:nk, :], bank(name, ("t", u))[:, 0:nk * P].rearrange("p (n q) -> p n q", n=nk),
                     frees(name, ("t", u)))

            def experts(layer):
                L = str(layer)
                moe = "moe" + L
                streams = 2 - layer
                tiles = TT * streams
                rows = streams * CAP
                parts = P // rows
                width, yw = NCOL // parts, D // parts
                b.drained("logitT" + L, 0)
                act.activation(lge[:, 0:tiles * N_EXP], lg[:, 0:tiles * N_EXP], ACT.Exp).then_inc(sem("lgt_exp"), 1)
                if layer == 0:
                    act.wait_ge(sem("x_mix"), 8)
                    for n in range(4):
                        mod_row("modrow5", n)
                with act.Fori(0, GROUPS) as i:
                    b.lap = i * LAP[moe]
                    for e in range(PER_GROUP):
                        b.filled(moe, (e, "gate"))
                        copy(moe_gtst[e * CAP:(e + 1) * CAP, 0:tiles * P], bank(moe, (e, "gate"))[0:CAP, 0:tiles * P], frees(moe, (e, "gate")))
                        for c in range(2):
                            b.filled(moe, (e, f"a{c}"))
                            act.activation(moe_sil[:, c, 0:width], bank(moe, (e, f"a{c}"))[:, 0:width], ACT.Silu)\
                                .then_inc(frees(moe, (e, f"a{c}")), 1)
                        for c in range(2):
                            b.filled(moe, (e, f"t{c}"))
                            copy(moe_gtr[:, e % 2, c, 0:width], bank(moe, (e, f"t{c}"))[:, 0:width], frees(moe, (e, f"t{c}")))
                        b.filled(moe, (e, "y"))
                        for n in range(parts):
                            for s in range(streams):
                                last = n == parts - 1 and s == streams - 1
                                at = n * rows + s * CAP
                                copy(moe_yst[e * CAP:(e + 1) * CAP, s, n * yw:(n + 1) * yw],
                                     bank(moe, (e, "y"))[at:at + CAP, 0:yw], frees(moe, (e, "y")) if last else None)
                b.lap = 0

            act.wait_ge(sem("eps"), 1)
            act.wait_ge(sem("c_in"), 16)
            act.activation(sc[:, :, :], sc[:, :, :], ACT.Silu).then_inc(sem("silu_c"), 1)

            square_sums(X, xn4, 4, lambda t: act.wait_ge(sem("x_in"), 16))
            b.drained("modcol0", 0)
            norm_split("n1_0", A1[0], B1[0], 0, Z_FIRST["evz"])
            for what, *x in evz_schedule(late=2):
                if what == "w" and Z_AT["evz", *x] >= Z_FIRST["evz"] + EARLY_SPLIT:
                    if not early_split("evz", *x):
                        z_split("evz", *x)
                if what == "f" and x[1] > 0:
                    mod_row("modrow0", x[1] - 1)
                    if x[1] == 4:
                        b.drained("modrow0", 3)
                        act.sem_inc(sem("mod_spread"), 1)
                if what != "z":
                    continue
                c, t = x
                b.filled("evz", (c, t))
                w = 512 if c < 3 else 256
                act.activation(ev_z[:, t, c * 512:c * 512 + w], bank("evz", (c, t))[:, 0:w],
                               ACT.Gelu_apprx_tanh if c < 2 else ACT.Copy).then_inc(frees("evz", (c, t)), 1)
                if (c, t) == (2, 3):
                    act.wait_ge(sem("sgu_var"), 4)
                    root(root4, 1, sem("sgu_root"))
            for j in range(1 + EV_PAIRS):
                b.filled("evqk", j)
                copy(ev_kt[:, :] if j == 0 else ev_qt[:, j - 1, :], bank("evqk", j)[:, :], frees("evqk", j))
            for what, *x in ev_schedule(ATT_LAGS_ACT):
                if what != "a":
                    continue
                kind, u = x
                h, t = EV_UNITS[u]
                n = 512 if t < TT else SEQ
                s = ev_s[u % S_BUFS][:, 0:n]
                if kind == "s":
                    act.wait_ge(sem("ev_nm"), u + 1)
                    act.activation(s, s, ACT.Exp, bias=nm[:, u:u + 1], scale=EV_SCALE,
                                   accum_out=l[:, u:u + 1]).then_inc(sem("ev_p"), 1)
                    act.activation(ls[:, u:u + 1], ev_sink[:, h:h + 1], ACT.Exp, bias=nm[:, u:u + 1]).then_inc(sem("ev_ls"), 1)
                elif kind == "t":
                    probs_out("evatt", u, ev_pt, n // P)
            cat_split(0, 512)
            square_sums(X, moe_xn, 4, lambda t: act.wait_ge(sem("x_mix"), 4 + t + 1))
            b.drained("modcol0", 1)
            norm_out("n2_0", moe_ht, 4, A2[0], B2[0])
            experts(0)

            square_sums(X, moe_xn, 4, lambda t: act.wait_ge(sem("x_moe"), X_MOE[0] - 4 + t + 1))
            for n in range(4):
                mod_row("modrow1", n)
            b.drained("modcol1", 1)
            norm_split("n1_1", A1[1], B1[1], 8, Z_FIRST["odz"])
            n_sq = [0]

            def lora_squares(parts):
                for src, col in parts:
                    act.activation(od_s[2][:, 0:src.shape[-1]], src, ACT.Square, accum_out=ss2[:, col:col + 1]).then_inc(sem("lora_sq"), 1)
                    n_sq[0] += 1
                    act.wait_ge(sem("lora_sq"), n_sq[0])

            for what, c, t in odz_schedule():
                if what == "w":
                    if not early_split("odz", c, t):
                        z_split("odz", c, t)
                elif what == "z":
                    b.filled("odz", (c, t))
                    o = bank("odz", (c, t))
                    done = frees("odz", (c, t))
                    if c == 0 and t >= TT:
                        copy(od_zc[:, t - TT, :], o[:, 0:KV_LORA + KR], done)
                    elif c == 0:
                        copy(od_za[:, t, 0:512], o[:, :], done)
                    elif c == 1:
                        copy(od_za[:, t, 512:ZA_W], o[:, 0:ZA_W - 512])
                        copy(od_zb[:, t, 0:1024 - ZA_W], o[:, ZA_W - 512:512], done)
                    else:
                        at = c * 512 - ZA_W
                        w = 512 if c < 4 else OD_TAIL
                        copy(od_zb[:, t, at:at + w], o[:, 0:w], done)
            for tile in range(4):
                b.drained("odz", (0, tile))
            lora_squares([(od_za[:, tile, 0:KV_LORA], tile) for tile in range(TT)])
            lora_squares([(od_za[:, tile, KV_LORA + KR:], 4 + tile) for tile in range(TT)])
            lora_squares([(od_zc[:, tile, 0:KV_LORA], TT + tile) for tile in range(TT)])
            root(ss2[:, 0:4], KV_LORA, sem("lora_root"))
            root(ss2[:, 4:6], Q_LORA, sem("lora_root"))
            act.wait_ge(sem("conv_done"), TT)
            for p in range(2):
                for t in range(TT):
                    b.filled("uq", (p, t))
                    copy(od_q[:, t, p * 384:(p + 1) * 384], bank("uq", (p, t))[:, 0:384], frees("uq", (p, t)))
            for p in range(2):
                for t in range(4):
                    b.filled("ukv", (p, t))
                    o = bank("ukv", (p, t))[:, :].rearrange("p (h d) -> p h d", h=4)
                    kf = od_kf[:, t, :].rearrange("p (h d) -> p h d", h=OD_HEADS)
                    copy(kf[:, 4 * p:4 * p + 4, 0:64], o[:, :, 0:64])
                    copy(od_v[:, t, p * 256:(p + 1) * 256].rearrange("p (h d) -> p h d", h=4), o[:, :, 64:128], frees("ukv", (p, t)))
            for h in range(OD_HEADS):
                b.filled("odkT", h)
                copy(od_kt[0:OD_DIM, h, :], bank("odkT", h)[0:OD_DIM, :], frees("odkT", h))
            for kind, u in pipeline(len(OD_UNITS), ATT_LAGS_ACT):
                if kind == "s":
                    act.wait_ge(sem("od_nm"), u + 1)
                    if u >= S_BUFS:
                        b.filled("odatt", ("t", u - S_BUFS))
                    act.activation(od_s[u % S_BUFS][:, :], bank("odatt", ("s", u))[:, :], ACT.Exp, bias=nm[:, u:u + 1], scale=OD_SCALE,
                                   accum_out=l[:, u:u + 1]).then_inc(frees("odatt", ("s", u)), 1)
                elif kind == "t":
                    probs_out("odatt", u, od_pt, 4)
            cat_split(1, SEQ)
            square_sums(X, moe_xn, TT, lambda t: act.wait_ge(sem("x_mix"), 8 + TT + t + 1))
            norm_out("n2_1", moe_ht, TT, A2[1], B2[1])
            experts(1)

            square_sums(X, moe_xn, TT, lambda t: act.wait_ge(sem("x_moe"), X_MOE[1] - TT + t + 1))
            act.wait_ge(sem("x_final"), TT)

            with act.Fori(0, B2_LAYERS) as i:
                b.lap = i * LAP["b2"]

                def squares2(junk, at, ready):
                    for t in range(TT):
                        ready(t)
                        act.activation(junk[:, t, :], X[:, t, :], ACT.Square, accum_out=ss[:, t:t + 1]).then_inc(sem("b2_sq"), 1)
                        act.wait_ge(sem("b2_sq"), i * 4 + at + t + 1)
                        root(ss[:, t:t + 1], D, sem("b2_root"))

                def split_weights(name, k, m):
                    p = PIECE_AT[name, k, m]
                    if m == 0:
                        n = CHUNK_AT[name, k]
                        act.wait_ge(slot_loaded[n % SLOTS], i * (CHUNK_LAP["b2"] * 16) + 16 * (n // SLOTS + 1))
                    if p >= PIECE_BUFS:
                        before = fills_last(*PIECES[p - PIECE_BUFS])
                        if before:
                            b.filled(*before)
                        else:
                            act.wait_ge(sem("piece_used"), i * USED_UP_TO[-1] + USED_UP_TO[p - PIECE_BUFS])
                    src, high, _ = piece_of(name, k, m)
                    copy(high, src, sem("w_hi"))

                def split_tokens(pair):
                    copy(a_hi[:, 2 * pair:2 * pair + 2, :], b2_ht[:, 2 * pair:2 * pair + 2, :], sem("a_hi"))

                def gain_out(name, off):
                    for k in range(KD):
                        b.filled(name, k)
                        act.activation(a_hi[:, k, :], bank(name, k)[:, 0:SEQ], ACT.Identity,
                                       scale=layer_gain[:, off + k:off + k + 1]).then_inc(sem("norm_hi"), 1)

                squares2(region(B2_XN1, TT, D), 0, lambda t: [b.drained("down", (N_FF - 1, t, h), LAP["b2"]) for h in range(2)])
                act.wait_ge(sem("b2_gain"), i * 2 + 2)
                for what, name, k, m in split_order(ATT_CHUNKS):
                    if what == "piece":
                        split_weights(name, k, m)
                    elif what == "begin":
                        gain_out("nmix", 0)
                    elif what == "out":
                        for t in range(TT):
                            b.filled("qkv", (k, t))
                            dst = (b2_q, b2_k, b2_v)[k // 3]
                            copy(dst[:, t, k % 3 * 512:(k % 3 + 1) * 512], bank("qkv", (k, t))[:, :], frees("qkv", (k, t)))
                for wh in range(2):
                    for j in range(B2_PAIRS // 2):
                        b.filled("qkT", (wh, j))
                        copy((b2_qt, b2_kt)[wh][:, 2 * j:2 * j + 2, :],
                             bank("qkT", (wh, j))[:, :].rearrange("p (n q) -> p n q", n=2), frees("qkT", (wh, j)))
                def softmax_unit(kind, u, n):
                    per_bank = ab_keys_per_bank(*AB_UNITS[u])
                    s = b2_s[:, u % S_BUFS, 0:P * len(ab_keys(*AB_UNITS[u]))]
                    if kind == "s" and n == len(per_bank) - 1:
                        act.wait_ge(sem("b2_nm"), i * len(AB_UNITS) + u + 1)
                        act.activation(s, s, ACT.Exp, bias=nm[:, u:u + 1], scale=B2_SCALE,
                                       accum_out=l[:, u:u + 1]).then_inc(sem("b2_p"), 1)
                    elif kind == "t":
                        b.filled("ab", (kind, u, n))
                        if u >= 2:
                            b.filled("ab", ("o", u - 2, 0))
                        m = len(per_bank[n])
                        copy(b2_pt[:, u % 2, 4 * n:4 * n + m, :],
                             bank("ab", (kind, u, n))[:, 0:m * P].rearrange("p (n q) -> p n q", n=m), frees("ab", (kind, u, n)))

                def stick_unit(kind, u, n):
                    buf = b2_c[u]
                    k = i * len(C_UNITS) + u + 1
                    if kind == "s":
                        act.wait_ge(sem("c_abs"), k)
                        act.activation(buf[:, 384:768], buf[:, 384:768], ACT.Exp).then_inc(sem("c_exp"), 1)
                    elif kind == "l":
                        act.wait_ge(sem("c_exp"), k)
                        act.activation(buf[:, 384:768], buf[:, 384:768], ACT.Ln, bias=1.0).then_inc(sem("c_ln"), 1)
                    elif kind == "c":
                        b.drained("c", (kind, u, 0))
                        act.activation(buf[:, 384:768], buf[:, 0:384], ACT.Exp).then_inc(sem("c_weights"), 1)
                    else:
                        b.filled("c", (kind, u, n))
                        copy(b2_ocat[:, n, 640 + u * 64:640 + (u + 1) * 64], bank("c", (kind, u, n))[:, 0:64], frees("c", (kind, u, n)))

                for which, kind, u, n in b2_schedule(ATT_LAGS_ACT, "slco"):
                    (softmax_unit if which == "ab" else stick_unit)(kind, u, n)
                def split_bank(name, j, dst, sig):
                    b.filled(name, j)
                    copy(dst[:, 2 * j:2 * j + 2, :], bank(name, j)[:, :].rearrange("p (n q) -> p n q", n=2), sig)

                b.filled("ab", ("s", len(AB_UNITS) - 1, 0))
                b.filled("c", ("s", C_UNITS[-1], 0))
                act.wait_ge(sem("b2_tokens"), i * 4 + 4)
                for pair in range(KD // 2):
                    split_tokens(pair)
                b.filled("ocat", 0)
                for what, name, k, m in split_order(MLP_CHUNKS):
                    if what == "piece":
                        split_weights(name, k, m)
                    elif what == "begin":
                        for j in range(4):
                            split_bank("ocat", j, o_hi, sem("ocat_hi"))
                    elif what == "out" and name == "merge" and k % 4 < 3:
                        c = k // 4
                        if c:
                            act.wait_ge(sem("b2_merged"), i * 4 + 2)
                        for t in range(TT):
                            key = (c, "gate", k % 4, t)
                            b.filled("merge", key)
                            act.activation(b2_sig[:, k % 4, t, :], bank("merge", key)[:, :], ACT.Sigmoid).then_inc(frees("merge", key), 1)
                    elif what == "out" and name == "up":
                        if k:
                            act.wait_ge(sem("b2_hidden"), i * (2 * N_FF) + 2 * k)
                        for n in range(2):
                            b.filled("up", (k, n))
                            act.activation(b2_sq[:, n, :], bank("up", (k, n))[:, :], ACT.Relu).then_inc(frees("up", (k, n)), 1)
                    elif what == "late" and name == "up":
                        for n in range(2):
                            act.wait_ge(sem("b2_squared"), i * (2 * N_FF) + 2 * k + n + 1)
                            at = k % 2 * 4 + 2 * n
                            copy(o_hi[:, at:at + 2, :], b2_sq[:, n, :].rearrange("p (m q) -> p m q", m=2), sem("hidden_hi"))
                    elif what == "late" and (name, k) == ("merge", 7):
                        for j in range(4):
                            split_bank("mergeT", j, a_hi, sem("merge_hi"))
                        warm_up(i * 2 + warm[0])
                    elif what == "late" and (name, k) == ("down", N_FF - 2):
                        warm_up(i * 2 + (warm[0] + 1))
                    elif what == "late" and (name, k) == ("wo", 2):
                        squares2(region(B2_XN2, TT, D), 2, lambda t: [b.drained("wo", (c, t)) for c in range(3)])
                        gain_out("nmlp", KD)
            b.lap = LAP["b2"] * (B2_LAYERS - 1)
            warm[0] += 2 * B2_LAYERS
            square_sums(X, region(B2_XN2, TT, D), TT, lambda t: [b.drained("down", (N_FF - 1, t, h)) for h in range(2)])

        @block.vector
        def _(dve):
            b = Banks(dve)
            steps = Steps(dve, sem("dve_step"))
            dve.memset(eps, EPS).then_inc(sem("eps"), 1)
            dve.memset(mrow, 0.0).then_inc(sem("mod_clear"), 1)

            def scaled(x, xn, tiles, n_root):
                for t in range(tiles):
                    dve.wait_ge(sem("root"), n_root - tiles + t + 1)
                    steps.do(dve.reciprocal(rstd[:, t:t + 1], ss[:, t:t + 1]))
                    dve.tensor_scalar(xn[:, t, :], x[:, t, :], rstd[:, t:t + 1], None, ALU.mult).then_inc(sem("xn"), 1)

            def norm_out(name, tiles, dst, scale, shift):
                for k in range(1, KD, 2):
                    b.filled(name, k)
                    for s in range(tiles // TT):
                        cols = slice(s * SEQ, (s + 1) * SEQ)
                        ins = dve.tensor_scalar(dst[:, k, cols], bank(name, k)[:, cols], scale[:, k, s:s + 1],
                                                shift[:, k, s:s + 1], ALU.mult, ALU.add)
                    ins.then_inc(frees(name, k), 1)

            def norm_split(name, scale, shift, before, first):
                for k in range(1, KD + 2, 2):
                    if k < KD:
                        b.filled(name, k)
                        if k >= 4:
                            dve.wait_ge(sem("z_tok_lo"), before + k - 3)
                        for s in range(2):
                            cols = slice(s * SEQ, (s + 1) * SEQ)
                            ins = dve.tensor_scalar(z_tokens[:, k % 4, cols], bank(name, k)[:, cols], scale[:, k, s:s + 1],
                                                    shift[:, k, s:s + 1], ALU.mult, ALU.add)
                        ins.then_inc(frees(name, k), 1)
                    if k > 1:
                        for m in (k - 3, k - 2):
                            dve.wait_ge(sem("z_tok_hi"), before + m + 1)
                            dve.tensor_tensor(z_lo[:, m, :], z_tokens[:, m % 4, :], z_hi[:, m, :].bitcast(F32), ALU.subtract)\
                                .then_inc(sem("z_tok_lo"), 1)
                    if k == 3:
                        for n in range(EARLY_SPLIT):
                            z_split(*Z_PIECES[first + n])

            def z_split(name, c, k):
                dve.wait_ge(sem("z_w_hi"), Z_AT[name, c, k] + 1)
                src, high, low = z_piece(name, c, k)
                dve.tensor_tensor(low, src, high.bitcast(F32), ALU.subtract).then_inc(sem("z_w_lo"), 1)

            def mod_chunk(layer, c):
                name = f"mod{layer}"
                if c == 0:
                    dve.wait_ge(sem(("modb_in", "modb_in2")[layer]), 64)
                b.filled(name, c)
                cols = mrow[:, c * P:(c + 1) * P]
                dve.tensor_tensor(cols, bank(name, c)[:, 0:P], cols, ALU.add).then_inc(frees(name, c), 1)

            def mod_cols(layer, half):
                name = f"modcol{layer}"
                b.filled(name, half)
                cols = bank(name, half)[:, :].rearrange("p (v k r) -> p v k r", v=2, k=KD)
                g = gain((G_N1, G_N2)[half] + layer * KD).unsqueeze(2).to_broadcast([P, KD, 2])
                dve.scalar_tensor_tensor(out=modc[:, layer, 2 * half], in0=cols[:, 0, :, 0:2], scalar=1.0, in1=g, op0=ALU.add, op1=ALU.mult)
                dve.tensor_copy(modc[:, layer, 2 * half + 1], cols[:, 1, :, 0:2]).then_inc(frees(name, half), 1)
                b.drained(name, half)

            def rope(x1, x2, cos, sin, tmp, sig):
                steps.add(dve.tensor_tensor(tmp[0], x1, cos, ALU.mult))
                steps.add(dve.tensor_tensor(tmp[1], x2, sin, ALU.mult))
                steps.add(dve.tensor_tensor(tmp[2], x2, cos, ALU.mult))
                steps.do(dve.tensor_tensor(tmp[3], x1, sin, ALU.mult))
                steps.add(dve.tensor_tensor(x1, tmp[0], tmp[1], ALU.subtract))
                dve.tensor_tensor(x2, tmp[2], tmp[3], ALU.add).then_inc(sig, 1)

            def heads_tmp(off, n, w):
                return [region(off + m * n * w, n, w) for m in range(4)]

            def over_heads(c, n, w):
                return c.unsqueeze(1).to_broadcast([P, n, w])

            def add_gated(name, key, gate, x, tmp, width, sig=None):
                b.filled(name, key)
                dve.tensor_tensor(tmp[:, 0:width], bank(name, key)[:, 0:width], gate, ALU.mult).then_inc(frees(name, key), 1)
                b.drained(name, key)
                ins = dve.tensor_tensor(x, x, tmp[:, 0:width], ALU.add)
                if sig is None:
                    steps.do(ins)
                else:
                    ins.then_inc(sig, 1)

            def mix(layer, width):
                name = f"mix{layer}"
                tiles = 2 * TT if layer == 0 else TT

                def add(c, t):
                    cols = slice(c * 512, (c + 1) * 512)
                    add_gated(name, (c, t), bc[:, t // TT, cols], X[:, t, cols], mix_tmp[:, t % 2], 512, sem("x_mix"))

                for k in range(KD):
                    dve.wait_ge(sem("cat_hi"), KD * layer + k + 1)
                    dve.tensor_tensor(z_lo[:, k, 0:width], bank(f"cat{layer}", k)[:, 0:width], cat_hi[:, k, 0:width].bitcast(F32), ALU.subtract)\
                        .then_inc(frees(f"cat{layer}", k), 1)
                    if k == 1:
                        for n in range(EARLY_SPLIT):
                            z_split(name, 0, n)
                for c in range(2):
                    for k in range(KD):
                        if not early_split(name, c, k):
                            z_split(name, c, k)
                        if c == 1 and 2 <= k < 2 + tiles:
                            add(0, k - 2)
                for t in range(tiles):
                    add(1, t)

            def experts(layer):
                L = str(layer)
                moe = "moe" + L
                streams = 2 - layer
                tiles = TT * streams
                rows = streams * CAP
                parts = P // rows
                width = NCOL // parts
                ne = streams * N_EXP
                b.filled("logit" + L, 0)
                dve.tensor_copy(moe_work[0:32 * tiles, 0:P], bank("logit" + L, 0)[0:32 * tiles, 0:P]).then_inc(frees("logit" + L, 0), 1)
                b.filled("logitT" + L, 0)
                groups = lambda v: v[:, 0:tiles * N_EXP].rearrange("p (g e) -> p g e", g=tiles)
                each = lambda v: v[:, 0:tiles].unsqueeze(2).to_broadcast([P, tiles, N_EXP])
                logits = bank("logitT" + L, 0)[:, 0:32 * tiles].rearrange("p (g e) -> p g e", g=tiles)[:, :, 0:N_EXP]
                steps.do(dve.tensor_reduce(lgs[:, 0:tiles], logits, AX.X, ALU.max))
                dve.tensor_tensor(groups(lg), logits, each(lgs), ALU.subtract).then_inc(frees("logitT" + L, 0), 1)
                dve.wait_ge(sem("lgt_exp"), layer + 1)
                steps.do(dve.tensor_reduce(lgs[:, 0:tiles], groups(lge), AX.X, ALU.add))
                steps.do(dve.reciprocal(lgs[:, 0:tiles], lgs[:, 0:tiles]))
                dve.tensor_tensor(groups(moe_aff), groups(lge), each(lgs), ALU.mult).then_inc(sem("aff"), 1)
                b.filled("affT" + L, 0)
                work = moe_work[0:ne, :]
                top = mx2[0:ne, 0:8]
                dve.tensor_copy(work, bank("affT" + L, 0)[0:ne, 0:SEQ]).then_inc(frees("affT" + L, 0), 1)
                b.drained("affT" + L, 0)
                for _ in range(CAP // 8):
                    steps.do(dve.max(top, work))
                    steps.do(dve.match_replace(work, top, work, -1.0))
                dve.tensor_scalar(moe_chosen[0:ne, :], work, 0.0, None, ALU.is_lt).then_inc(sem("chosen"), 1)
                b.filled("selT" + L, 0)
                dve.tensor_copy(mkT[:, 0:2 * ne], bank("selT" + L, 0)[:, 0:2 * ne]).then_inc(frees("selT" + L, 0), 1)
                b.filled("rank" + L, 0)
                b.drained("selT" + L, 0)
                dve.tensor_tensor(pos[:, 0:2 * ne], bank("rank" + L, 0)[:, 0:2 * ne], mkT[:, 0:2 * ne], ALU.mult)\
                    .then_inc(frees("rank" + L, 0), 1)
                b.drained("rank" + L, 0)
                dve.wait_ge(sem("aff"), layer + 1)
                scale, shift = (modc[:, layer, n].rearrange("p k s -> p (k s)") if streams == 2 else modc[:, layer, n, :, 0] for n in (2, 3))
                with steps.loop(GROUPS, MOE_STEPS[layer]) as i:
                    b.lap = i * LAP[moe]
                    by_expert = lambda v: v.rearrange("p (e c) -> p e c", e=PER_GROUP)
                    slots = iota.unsqueeze(1).to_broadcast([P, PER_GROUP, CAP])
                    for weigh in (False, True):
                        for tok in range(tiles):
                            at = tok % TT * ne + tok // TT * N_EXP
                            spread = lambda v: v[:, bass.ds(i * PER_GROUP + at, PER_GROUP)].unsqueeze(2).to_broadcast([P, PER_GROUP, CAP])
                            hot = by_expert(moe_oh[:, tok, :])
                            if weigh:
                                dve.wait_ge(sem("hot" + L), i * tiles + tok + 1)
                                dve.tensor_tensor(by_expert(moe_gw[:, tok, :]), hot, spread(moe_aff), ALU.mult).then_inc(sem("gated" + L), 1)
                            else:
                                dve.tensor_tensor(hot, spread(pos), slots, ALU.is_equal).then_inc(sem("hot" + L), 1)
                    for k in range(KD):
                        b.filled("gather" + L, k)
                        for s in range(streams):
                            ks = k * streams + s
                            ins = dve.tensor_scalar(moe_x(streams)[:, k, :, s, :], by_expert(bank("gather" + L, k)[:, s * P:(s + 1) * P]),
                                                    scale[:, ks:ks + 1], shift[:, ks:ks + 1], ALU.mult, ALU.add)
                        ins.then_inc(frees("gather" + L, k), 1)
                    for e in range(PER_GROUP):
                        for c in range(2):
                            b.filled(moe, (e, f"b{c}"))
                            b.drained(moe, (e, f"a{c}"))
                            dve.tensor_tensor(moe_g[:, c, 0:width], moe_sil[:, c, 0:width], bank(moe, (e, f"b{c}"))[:, 0:width], ALU.mult)\
                                .then_inc(frees(moe, (e, f"b{c}")), 1)
                    pieces = 8 // tiles
                    w = D // pieces
                    for n in range(8):
                        t, c = n // pieces, n % pieces
                        cols = slice(c * w, (c + 1) * w)
                        add_gated("comb" + L, n, bc[:, t // TT if streams == 2 else 1, cols], X[:, t, cols], moe_tmp[:, n % 2], w,
                                  sem("x_moe") if c == pieces - 1 else None)
                    dve.wait_ge(sem("x_moe"), i * tiles + (X_MOE[layer] - GROUPS * tiles + tiles))
                b.lap = 0
                dve.wait_ge(sem("x_moe"), X_MOE[layer])

            def weights_out(name, u, dst):
                b.filled(name, u)
                steps.do(dve.reciprocal(rl[:, u[1]:u[1] + 1], l[:, u[1]:u[1] + 1]))
                dve.tensor_scalar(dst, bank(name, u)[:, 0:64], rl[:, u[1]:u[1] + 1], None, ALU.mult).then_inc(frees(name, u), 1)

            scaled(X, xn4, 4, 4)
            for c in range(MOD_EARLY):
                mod_chunk(0, c)
            dve.wait_ge(sem("small_in"), 16)
            mod_cols(0, 0)
            norm_split("n1_0", A1[0], B1[0], 0, Z_FIRST["evz"])

            def modulation(what, layer, n):
                if what == "m":
                    mod_chunk(layer, n)
                elif n == 0:
                    for c in (10, 11):
                        b.drained("mod0", c)
                    dve.tensor_copy(mrow5, mrow[:, 10 * P:12 * P]).then_inc(sem("mod_saved"), 1)
                    mod_cols(0, 1)

            for what, *x in evz_schedule(late=2):
                if what == "w":
                    if not early_split("evz", *x):
                        z_split("evz", *x)
                    c, k = x
                    if c == 3 and k >= 4:
                        t = k - 4
                        if t == 0:
                            dve.wait_ge(sem("ev_in"), 16)
                            steps.add(dve.tensor_scalar(ev_nsink, ev_sink[:, :], -1.0, None, ALU.mult))
                            dve.wait_ge(sem("sgu_root"), 1)
                            steps.do(dve.reciprocal(root4, root4))
                        v = ev_z[:, t, 512:1024]
                        steps.do(dve.tensor_scalar(v, v, mv[:, 2 * t:2 * t + 1], root4[:, t:t + 1], ALU.subtract, ALU.mult))
                        dve.tensor_tensor(v, v, ev_sgug[:, :], ALU.mult).then_inc(sem("sgu_v"), 1)
                elif what != "z":
                    modulation(what, *x)
                elif x[0] == 1:
                    t = x[1]
                    b.filled("evz", (1, t))
                    b.drained("evz", (1, t))
                    v = ev_z[:, t, 512:1024]
                    var = mv[:, 2 * t + 1:2 * t + 2]
                    steps.do(dve.bn_stats(bn[:, 6 * t:6 * t + 6], v))
                    steps.do(dve.bn_aggr(mv[:, 2 * t:2 * t + 2], bn[:, 6 * t:6 * t + 6]))
                    dve.tensor_copy(root4[:, t:t + 1], var).then_inc(sem("sgu_var"), 1)
            b.drained("evz", (3, 3))
            for t in range(TT):
                x = ev_z[:, t, 1152:1792].rearrange("p (h d) -> p h d", d=64)
                rope(x[:, :, 0:32], x[:, :, 32:64], over_heads(ev_cos[:, t, :], 10, 32), over_heads(ev_sin[:, t, :], 10, 32),
                     heads_tmp(EV_S, 10, 32), sem("ev_rope"))
                dve.wait_ge(sem("ev_rope"), t + 1)
            for t in range(4):
                b.filled("sgu", t)
                for g in range(4):
                    cols = slice(g * P, (g + 1) * P)
                    ins = dve.scalar_tensor_tensor(out=ev_cat[:, t, 512 + g * P:512 + (g + 1) * P], in0=bank("sgu", t)[:, cols],
                                                   scalar=ev_sgub[:, g:g + 1], in1=ev_z[:, t, cols], op0=ALU.add, op1=ALU.mult)
                ins.then_inc(frees("sgu", t), 1)
            dve.wait_ge(sem("ev_in2"), 16)
            for what, *x in ev_schedule(ATT_LAGS):
                if what != "a":
                    modulation(what, *x)
                    continue
                kind, u = x
                h, t = EV_UNITS[u]
                first = 0 if t < TT else SEQ
                n = 512 - first
                if kind == "s":
                    b.filled("evatt", ("s", u))
                    if u >= S_BUFS:
                        b.filled("evatt", ("t", u - S_BUFS))
                    dve.tensor_tensor_reduce(ev_s[u % S_BUFS][:, 0:n], bank("evatt", ("s", u))[:, 0:n], ev_win[:, t % TT, first:512], 1.0, -3e38,
                                             ALU.add, ALU.max, mx[:, u:u + 1]).then_inc(frees("evatt", ("s", u)), 1)
                    b.drained("evatt", ("s", u))
                    dve.tensor_scalar(nm[:, u:u + 1], mx[:, u:u + 1], -EV_SCALE, ev_nsink[:, h:h + 1], ALU.mult, ALU.min)\
                        .then_inc(sem("ev_nm"), 1)
                elif kind == "o":
                    dve.wait_ge(sem("ev_ls"), u + 1)
                    steps.do(dve.tensor_tensor(l[:, u:u + 1], l[:, u:u + 1], ls[:, u:u + 1], ALU.add))
                    weights_out("evatt", ("o", u), ev_cat[:, t, h * 64:(h + 1) * 64])
            for half in range(2):
                mod_cols(1, half)
            mix(0, 512)
            scaled(X, moe_xn, 4, 8)
            norm_out("n2_0", 4, moe_ht, A2[0], B2[0])
            experts(0)

            scaled(X, xn4, 4, 12)
            norm_split("n1_1", A1[1], B1[1], 8, Z_FIRST["odz"])

            def convolve(t, part):
                gb, u = od_zb[:, t, 0:512], od_zb[:, t, 512:1024]
                acc, tmp = od_cat[:, t, 512:1024], region(OD_CONV, 512)
                if part == 0:
                    b.filled("conv", (t, 0))
                    dve.tensor_tensor(acc, bank("conv", (t, 0))[:, :], od_convw[:, 0, :], ALU.mult).then_inc(frees("conv", (t, 0)), 1)
                    steps.do(dve.tensor_tensor(tmp, u, od_convw[:, 1, :], ALU.mult))
                elif part == 1:
                    b.drained("conv", (t, 0))
                    steps.do(dve.tensor_tensor(acc, acc, tmp, ALU.add))
                    b.filled("conv", (t, 1))
                    dve.tensor_tensor(tmp, bank("conv", (t, 1))[:, :], od_convw[:, 2, :], ALU.mult).then_inc(frees("conv", (t, 1)), 1)
                else:
                    b.drained("conv", (t, 1))
                    steps.do(dve.tensor_tensor(acc, acc, tmp, ALU.add))
                    dve.tensor_tensor(acc, acc, gb, ALU.mult).then_inc(sem("conv_done"), 1)
                    dve.wait_ge(sem("conv_done"), t + 1)

            for what, c, k in odz_schedule():
                if what == "w":
                    if not early_split("odz", c, k):
                        z_split("odz", c, k)
                    if c == 0 and k == 0:
                        dve.wait_ge(sem("od_in"), 16)
                    elif c == 0 and k == 1:
                        b.drained("odz", (4, 1))
                        for t in range(TT):
                            gb, gc, hh = (od_zb[:, t, n * 512:(n + 1) * 512] for n in range(3))
                            dve.tensor_tensor(gc, gc, hh, ALU.mult).then_inc(sem("conv_u"), 1)
                    elif c == 0 and k >= 3:
                        convolve((k - 3) // 3, (k - 3) % 3)
                elif what == "tail":
                    convolve(1, 2)
            dve.wait_ge(sem("lora_root"), 2)
            steps.do(dve.reciprocal(rstd2[:, :], ss2[:, :]))
            for n in range(6):
                part = od_za[:, n, 0:KV_LORA] if n < TT else od_zc[:, n - TT, 0:KV_LORA] if n < 4 else od_za[:, n - 4, KV_LORA + KR:]
                dve.tensor_scalar(part, part, rstd2[:, n:n + 1], None, ALU.mult).then_inc(sem("lora_n"), 1)
            dve.wait_ge(sem("od_in2"), 16)
            for t in range(TT):
                x = od_za[:, t, KV_LORA:KV_LORA + KR].unsqueeze(1)
                rope(x[:, :, 0:16], x[:, :, 16:32], over_heads(od_cos[:, t, :], 1, 16), over_heads(od_sin[:, t, :], 1, 16),
                     heads_tmp(OD_S + 1024, 1, 16), sem("od_krope"))
                dve.wait_ge(sem("od_krope"), t + 1)
            for j in range(2):
                b.filled("ckvT", j)
                dve.tensor_scalar(od_ckvt[:, j, :], bank("ckvT", j)[:, :], gain(G_KV + j, 1), None, ALU.mult).then_inc(frees("ckvT", j), 1)
            for j in range(3):
                b.filled("cqT", j)
                dve.tensor_scalar(od_cqt[:, j, :], bank("cqT", j)[:, 0:SEQ], gain(G_Q + j, 1), None, ALU.mult).then_inc(frees("cqT", j), 1)
            for t in range(4):
                src = od_za[:, t, KV_LORA:KV_LORA + KR] if t < TT else od_zc[:, t - TT, KV_LORA:]
                kf = od_kf[:, t, :].rearrange("p (h d) -> p h d", h=OD_HEADS)
                dve.tensor_copy(kf[:, :, 64:96], over_heads(src, OD_HEADS, KR)).then_inc(sem("od_kr"), 1)
            b.drained("uq", (1, 1))
            for t in range(TT):
                x = od_q[:, t, :].rearrange("p (h d) -> p h d", h=OD_HEADS)
                rope(x[:, :, 64:80], x[:, :, 80:96], over_heads(od_cos[:, t, :], 8, 16), over_heads(od_sin[:, t, :], 8, 16),
                     heads_tmp(OD_S, 8, 16), sem("od_rope"))
                dve.wait_ge(sem("od_rope"), t + 1)
            for j in range(OD_HEADS // 2):
                b.filled("odqT", j)
                dve.tensor_copy(od_qt[0:OD_DIM, 2 * j:2 * j + 2, :],
                                bank("odqT", j)[0:OD_DIM, :].rearrange("p (n q) -> p n q", n=2)).then_inc(frees("odqT", j), 1)
            for kind, u in pipeline(len(OD_UNITS), ATT_LAGS):
                h, t = OD_UNITS[u]
                if kind == "s":
                    b.filled("odatt", ("s", u))
                    steps.do(dve.tensor_reduce(mx[:, u:u + 1], bank("odatt", ("s", u))[:, :], AX.X, ALU.max))
                    dve.tensor_scalar(nm[:, u:u + 1], mx[:, u:u + 1], -OD_SCALE, None, ALU.mult).then_inc(sem("od_nm"), 1)
                elif kind == "o":
                    weights_out("odatt", ("o", u), od_cat[:, t, h * 64:(h + 1) * 64])
            mix(1, SEQ)
            scaled(X, moe_xn, TT, 14)
            norm_out("n2_1", TT, moe_ht, A2[1], B2[1])
            experts(1)

            def last_norm(n_root, n_gain, dst, sig):
                dve.wait_ge(sem("fg_in"), n_gain)
                for t in range(TT):
                    dve.wait_ge(sem("root"), n_root - TT + t + 1)
                    steps.do(dve.reciprocal(rstd[:, t:t + 1], ss[:, t:t + 1]))
                    dve.scalar_tensor_tensor(out=dst[:, t, :], in0=X[:, t, :], scalar=rstd[:, t:t + 1], in1=final_g[n_gain // 32][:, :],
                                             op0=ALU.mult, op1=ALU.mult).then_inc(sig, 1)

            last_norm(16, 16, X, sem("x_final"))
            dve.wait_ge(sem("x_final"), TT)

            with steps.loop(B2_LAYERS, B2_STEPS) as i:
                b.lap = i * LAP["b2"]
                for n, off in enumerate((G_MIX, G_MLP)):
                    dve.tensor_copy(layer_gain[:, n * KD:(n + 1) * KD], small[:, bass.ds(i * KD + off, KD)]).then_inc(sem("b2_gain"), 1)

                def scale_tokens(xn, at):
                    for t in range(TT):
                        dve.wait_ge(sem("b2_root"), i * 4 + at + t + 1)
                        steps.do(dve.reciprocal(rstd[:, t:t + 1], ss[:, t:t + 1]))
                        dve.tensor_scalar(xn[:, t, :], X[:, t, :], rstd[:, t:t + 1], None, ALU.mult).then_inc(sem("b2_xn"), 1)

                def low_part(dst, whole, high, sig):
                    dve.tensor_tensor(dst, whole, high.bitcast(F32), ALU.subtract).then_inc(sig, 1)

                def split_weights(name, k, m):
                    dve.wait_ge(sem("w_hi"), i * len(PIECES) + PIECE_AT[name, k, m] + 1)
                    src, high, low = piece_of(name, k, m)
                    low_part(low, src, high, sem("w_lo"))

                def split_tokens(pair):
                    dve.wait_ge(sem("a_hi"), i * 4 + pair + 1)
                    at = slice(2 * pair, 2 * pair + 2)
                    low_part(a_lo[:, at, :], b2_ht[:, at, :], a_hi[:, at, :], sem("a_lo"))

                def gain_out(name, off, event):
                    dve.wait_ge(sem("b2_gain"), i * 2 + 2)
                    for k in range(KD):
                        dve.wait_ge(sem("norm_hi"), i * 16 + 8 * event + k + 1)
                        dve.scalar_tensor_tensor(out=a_lo[:, k, :], in0=bank(name, k)[:, 0:SEQ], scalar=layer_gain[:, off + k:off + k + 1],
                                                 in1=a_hi[:, k, :].bitcast(F32), op0=ALU.mult, op1=ALU.subtract).then_inc(frees(name, k), 1)

                def keep_tokens(pair):
                    for k in (2 * pair, 2 * pair + 1):
                        b.drained("nmix", k)
                    at = slice(2 * pair, 2 * pair + 2)
                    dve.tensor_tensor(b2_ht[:, at, :], a_hi[:, at, :].bitcast(F32), a_lo[:, at, :].bitcast(F32), ALU.add)\
                        .then_inc(sem("b2_tokens"), 1)

                def rope2(wh, t):
                    dve.wait_ge(sem("b2_in2"), 16)
                    b.drained("qkv", (2 + 3 * wh, 1))
                    x = (b2_q, b2_k)[wh][:, t, :].rearrange("p (h d) -> p h d", d=64)[:, 0:B2_ROT, :]
                    rope(x[:, :, 0:8], x[:, :, 8:16], over_heads(b2_cos[:, t, :], B2_ROT, 8),
                         over_heads(b2_sin[:, t, :], B2_ROT, 8), heads_tmp(B2_RTMP, B2_ROT, 8), sem("b2_rope"))
                    dve.wait_ge(sem("b2_rope"), i * 4 + wh * 2 + t + 1)

                scale_tokens(region(B2_XN1, TT, D), 0)
                for what, name, k, m in split_order(ATT_CHUNKS):
                    if what == "piece":
                        split_weights(name, k, m)
                    elif what == "begin":
                        gain_out("nmix", 0, 0)
                    elif what == "late" and k < 2:
                        for pair in (2 * k, 2 * k + 1):
                            keep_tokens(pair)
                    elif what == "late" and k in (2, 3, 5, 6):
                        rope2(k // 4, k % 3 != 2)
                def softmax_unit(kind, u, n):
                    unit = AB_UNITS[u]
                    which, h, t = unit
                    per_bank = ab_keys_per_bank(*unit)
                    if kind == "s":
                        mask = (b2_amask if which == "A" else b2_bmask)[t]
                        w = P * len(per_bank[n])
                        b.filled("ab", (kind, u, n))
                        if u >= S_BUFS and n == 0:
                            b.filled("ab", ("t", u - S_BUFS, len(ab_keys_per_bank(*AB_UNITS[u - S_BUFS])) - 1))
                        dve.memset(idle[:, u + 20 * n:u + 20 * n + 1], 0.0)
                        top = mx[:, u:u + 1] if len(per_bank) == 1 else mx2[:, 2 * u + n:2 * u + n + 1]
                        dve.tensor_tensor_reduce(b2_s[:, u % S_BUFS, n * 512:n * 512 + w], bank("ab", (kind, u, n))[:, 0:w],
                                                 mask[:, n * 512:n * 512 + w], 1.0, -3e38, ALU.add, ALU.max, top)\
                            .then_inc(frees("ab", (kind, u, n)), 1)
                        if n == len(per_bank) - 1:
                            b.drained("ab", (kind, u, n))
                            if n:
                                steps.do(dve.tensor_reduce(mx[:, u:u + 1], mx2[:, 2 * u:2 * u + 2], AX.X, ALU.max))
                            dve.tensor_scalar(nm[:, u:u + 1], mx[:, u:u + 1], -B2_SCALE, None, ALU.mult).then_inc(sem("b2_nm"), 1)
                    elif kind == "o":
                        at = h * 64 + (0 if which == "A" else 256)
                        weights_out("ab", (kind, u, n), b2_ocat[:, t, at:at + 64])

                def stick_unit(kind, u, n):
                    buf = b2_c[u]
                    zm, sp = buf[:, 0:384], buf[:, 384:768]
                    if kind == "s":
                        b.filled("c", (kind, u, n))
                        dve.scalar_tensor_tensor(out=zm, in0=bank("c", (kind, u, n))[:, 0:384], scalar=B2_SCALE, in1=b2_cmask[:, :],
                                                 op0=ALU.mult, op1=ALU.add).then_inc(frees("c", (kind, u, n)), 1)
                        b.drained("c", (kind, u, n))
                        dve.scalar_tensor_tensor(out=sp, in0=zm, scalar=-1.0, in1=zm, op0=ALU.mult, op1=ALU.min).then_inc(sem("c_abs"), 1)
                    elif kind == "p":
                        dve.wait_ge(sem("c_ln"), i * len(C_UNITS) + u + 1)
                        dve.scalar_tensor_tensor(out=sp, in0=zm, scalar=0.0, in1=sp, op0=ALU.max, op1=ALU.add)\
                            .then_inc(sem("c_softplus"), 1)
                    elif kind == "c":
                        b.filled("c", (kind, u, n))
                        dve.tensor_tensor(zm, zm, bank("c", (kind, u, n))[:, 0:384], ALU.subtract).then_inc(frees("c", (kind, u, n)), 1)

                dve.wait_ge(sem("b2_in"), 16)
                for which, kind, u, n in b2_schedule(ATT_LAGS, "spc"):
                    (softmax_unit if which == "ab" else stick_unit)(kind, u, n)
                def split_bank(name, j, high, low, sig):
                    dve.wait_ge(sig, i * 4 + j + 1)
                    at = slice(2 * j, 2 * j + 2)
                    low_part(low[:, at, :], bank(name, j)[:, :].rearrange("p (n q) -> p n q", n=2), high[:, at, :], frees(name, j))

                def branch(c, n):
                    for t in range(TT):
                        gate, key = (c, "gate", n, t), (c, "branch", n, t)
                        b.filled("merge", key)
                        b.drained("merge", gate)
                        part = b2_sig[:, n, t, :]
                        dve.tensor_tensor(part, bank("merge", key)[:, :], part, ALU.mult).then_inc(frees("merge", key), 1)
                        if n:
                            total = b2_merged[:, t, c * 512:(c + 1) * 512]
                            b.drained("merge", key)
                            if n == 1:
                                steps.do(dve.tensor_tensor(total, b2_sig[:, 0, t, :], part, ALU.add))
                            else:
                                dve.tensor_tensor(total, total, part, ALU.add).then_inc(sem("b2_merged"), 1)

                for pair in range(KD // 2):
                    split_tokens(pair)
                for what, name, k, m in split_order(MLP_CHUNKS):
                    if what == "piece":
                        split_weights(name, k, m)
                        if name == "merge" and k % 4 == 3 and m == 3:
                            branch(k // 4, 0)
                        elif m == 0 and (name, k) in (("merge", 4), ("wo", 0)):
                            branch(0 if name == "merge" else 1, 1)
                    elif what == "begin":
                        for j in range(4):
                            split_bank("ocat", j, o_hi, o_lo, sem("ocat_hi"))
                    elif what == "out" and name == "merge" and k % 4 == 3:
                        branch(k // 4, 2)
                    elif what == "late" and (name, k) == ("merge", 7):
                        for j in range(4):
                            split_bank("mergeT", j, a_hi, a_lo, sem("merge_hi"))
                    elif what == "out" and name == "wo":
                        at, w = sum(WO_PIECES[:k]), WO_PIECES[k]
                        for t in range(TT):
                            b.filled("wo", (k, t))
                            x = X[:, t, at:at + w]
                            dve.tensor_tensor(x, x, bank("wo", (k, t))[:, 0:w], ALU.add).then_inc(frees("wo", (k, t)), 1)
                    elif what == "late" and (name, k) == ("wo", 2):
                        scale_tokens(region(B2_XN2, TT, D), 2)
                        gain_out("nmlp", KD, 1)
                    elif what == "out" and name == "up":
                        for n in range(2):
                            b.drained("up", (k, n))
                            dve.tensor_tensor(b2_sq[:, n, :], b2_sq[:, n, :], b2_sq[:, n, :], ALU.mult).then_inc(sem("b2_squared"), 1)
                    elif what == "late" and name == "up":
                        for n in range(2):
                            dve.wait_ge(sem("hidden_hi"), i * (2 * N_FF) + 2 * k + n + 1)
                            at = slice(k % 2 * 4 + 2 * n, k % 2 * 4 + 2 * n + 2)
                            low_part(o_lo[:, at, :], b2_sq[:, n, :].rearrange("p (m q) -> p m q", m=2), o_hi[:, at, :], sem("b2_hidden"))
                    elif what == "out" and name == "down":
                        for t in range(TT):
                            for h in range(2):
                                b.filled("down", (k, t, h))
                                if k:
                                    b.drained("down", (k - 1, t, h))
                                x = X[:, t, h * 512:(h + 1) * 512]
                                dve.tensor_tensor(x, x, bank("down", (k, t, h))[:, :], ALU.add).then_inc(frees("down", (k, t, h)), 1)
            b.lap = LAP["b2"] * (B2_LAYERS - 1)
            b.drained("down", (N_FF - 1, 1, 1))
            last_norm(18, 32, xn4, sem("result"))


def _k_major(w):
    k, n = w.shape
    return w.reshape(k // P, P, n).transpose(1, 0, 2).reshape(P, -1)

def _lay_out(a):
    f = np.float32
    stream = np.zeros((N_CHUNKS, P, CHUNK), f)

    def put(at, *parts):
        off = 0
        for part in parts:
            stream[at, :, off:off + part.shape[1]] = part
            off += part.shape[1]

    def columns(name, w, width=NCOL, first=0):
        for n in range(w.shape[1] // width):
            put(CHUNK_AT[name, first + n], _k_major(w[:, n * width:(n + 1) * width]))

    heads = [h + 4 * s for h in range(4) for s in range(2)]
    in0 = a["ev_w_in"][0]
    kv_cols, q_cols, g_cols = in0[:, :256], in0[:, 256:768].reshape(D, 8, 64)[:, heads].reshape(D, 512), in0[:, 768:]
    in0 = np.concatenate([g_cols, kv_cols[:, 128:], kv_cols[:, :128], q_cols], 1)
    out0 = a["ev_w_out"][0]
    out0 = np.concatenate([out0[:512].reshape(8, 64, D)[heads].reshape(512, D), out0[512:]], 0)
    in1 = a["od_w_in"][0]
    for layer in range(2):
        columns(f"mod{layer}", a["mod_w"][layer])
        at = CHUNK_AT[f"moe{layer}", 0]
        for e in range(N_EXP):
            w1, w3, w2 = (a[n][layer, e] for n in ("exp_w1", "exp_w3", "exp_w2"))
            for c in range(2):
                put(at + 6 * e + 2 * c, _k_major(w1[:, c * 512:(c + 1) * 512]))
                put(at + 6 * e + 2 * c + 1, _k_major(w3[:, c * 512:(c + 1) * 512]))
                put(at + 6 * e + 4 + c, _k_major(w2[c * 512:(c + 1) * 512]))
    columns("evz", in0[:, :1536])
    put(CHUNK_AT["evz", 3], _k_major(in0[:, 1536:]))
    columns("mix0", out0)
    columns("odz", in1[:, :4 * NCOL])
    put(CHUNK_AT["odz", 4], _k_major(in1[:, 4 * NCOL:]), _k_major(a["od_w_uq"][0]))
    put(CHUNK_AT["ukv", 0], _k_major(a["od_w_ukv"][0]))
    columns("mix1", a["od_w_out"][0])
    per = CHUNK_LAP["b2"] * SLOTS
    for i in range(B2_LAYERS):
        w_in = a["w_in_2"][i]
        w_out = np.concatenate([a["w_out_a_2"][i], a["w_out_b_2"][i], a["w_out_c_2"][i]], 0)
        for c in range(9):
            put(CHUNK_AT["qkv", c] + i * per, _k_major(w_in[:, c * NCOL:(c + 1) * NCOL]))
        for c in range(2):
            cols = slice(c * NCOL, (c + 1) * NCOL)
            put(CHUNK_AT["merge", 4 * c + 3] + i * per, _k_major(w_out[:, cols]))
            for g in range(3):
                put(CHUNK_AT["merge", 4 * c + g] + i * per, _k_major(w_in[:, 3 * B2_W + g * D:3 * B2_W + (g + 1) * D][:, cols]))
        at = 0
        for c, w in enumerate(WO_PIECES):
            put(CHUNK_AT["wo", c] + i * per, _k_major(a["w_o_2"][i][:, at:at + w]))
            at += w
        for j in range(N_FF):
            put(CHUNK_AT["up", j] + i * per, _k_major(a["w_up_2"][i][:, j * 512:(j + 1) * 512]))
            put(CHUNK_AT["down", j] + i * per, _k_major(a["w_down_2"][i][j * 512:(j + 1) * 512]))

    const = shape_constants()
    cols = lambda v: v.reshape(-1, P).T
    rows = lambda v: np.broadcast_to(v.reshape(1, -1), (P, v.size))
    small = [cols(a[n][i]) for n in ("norm1_g", "norm2_g", "norm_mix_2", "norm_mlp_2") for i in range(2)]
    small += [cols(a["od_q_norm_g"][0]), cols(a["od_kv_norm_g"][0])]
    small += [_k_major(a["router_w"][i]) for i in range(2)] + [np.zeros((P, N_EXP), f)]
    return {
        "stream": stream,
        "base": const["base"],
        "small": np.concatenate(small, 1),
        "ccols": np.concatenate([np.stack([cols(a["c"][0]), cols(a["c_ctx"])], 2), np.zeros((P, KD, 30), f)], 2),
        "x_in": np.concatenate([a["x"][0], a["ctx"][0]], 0).reshape(2 * TT, P, D).transpose(1, 0, 2),
        "modb": np.repeat(a["mod_b"].reshape(2, 12, 4, P).transpose(0, 2, 1, 3).reshape(2, 4, 1, 12 * P), 2, 2),
        "ev_pack": np.concatenate([const["win"], a["ev_sgu_w"][0].transpose(2, 0, 1).reshape(P, -1), rows(a["ev_sgu_norm_g"][0]),
                                   a["ev_sgu_b"][0].T, rows(a["ev_sink"][0][heads]), const["ev_rope"]], 1),
        "od_rope": const["od_rope"],
        "od_pack": np.concatenate([const["shift"], rows(a["od_conv_w"][0])], 1),
        "b2_masks": const["b2_masks"],
        "b2_rope": const["b2_rope"],
        "gains": np.stack([rows(a["final_g"]), rows(a["norm_final_2"])], 0),
    }

def kernel(**inputs):
    import concourse.bacc as bacc
    from concourse.bass_utils import run_bass_kernel_spmd

    a = {k: np.asarray(v) for k, v in inputs.items()}
    arrays = {"in_" + k: np.ascontiguousarray(v) for k, v in _lay_out(a).items()}
    nc = bacc.Bacc("TRN2", target_bir_lowering=False, num_devices=1)
    args = [nc.dram_tensor(n, v.shape, F32, kind="ExternalInput").ap() for n, v in arrays.items()]
    args.append(nc.dram_tensor("out", (1, SEQ, D), F32, kind="ExternalOutput").ap())
    program(nc, *args)
    r = run_bass_kernel_spmd(nc, [arrays], core_ids=[0])
    return r.results[0]["out"]
```
